# Optimizing a Trainium2 kernel written in Bass

```python
import math
import jax, jax.numpy as jnp
from jax import lax
import numpy as np

D_MODEL = 1024
BATCH = 1
SEQ = 256
DEPTH = 1

GLA_HEADS = 4
GLA_DK = D_MODEL // 8
GLA_DV = D_MODEL // 4
GLA_LOWRANK = 16
GLA_GATE_NORM = 16.0
GLA_CHUNK = 64
MOBA_HEADS = 8
MOBA_HD = D_MODEL // 8
MOBA_BLOCK = 256
MOBA_TOPK = 3
MOBA_Q_CHUNK = 16
ROPE_THETA = 500000.0
ROPE_DIM = MOBA_HD // 4
PEER_HEADS = 8
PEER_NKEYS = 128
PEER_N_EXPERTS = PEER_NKEYS * PEER_NKEYS
PEER_DKEY = 256
PEER_TOPK = 16
PEER_TOKEN_CHUNK = 128
DEEPNORM_ALPHA = (2.0 * DEPTH) ** 0.25
DEEPNORM_BETA = (8.0 * DEPTH) ** -0.25
LN_EPS = 1e-5
RMS_EPS = 1e-6
NEG_INF = -1e30

GLA_QK_W = GLA_HEADS * GLA_DK
GLA_V_W = GLA_HEADS * GLA_DV
MOBA_W = MOBA_HEADS * MOBA_HD
IN_SPLITS = (GLA_QK_W, GLA_QK_W, GLA_V_W, GLA_V_W, GLA_LOWRANK, MOBA_W, MOBA_W, MOBA_W, D_MODEL, D_MODEL)
IN_IS_VALUE = (False, False, True, False, False, False, False, True, False, False)
IN_WIDTH = sum(IN_SPLITS)
IN_SPLIT_POINTS = tuple(int(v) for v in np.cumsum(IN_SPLITS)[:-1])

kernel_name = "hybrid_gla_moba_peer_deepnorm"

def layer_norm(x, g, b):
    xf = x.astype(jnp.float32)
    mu = xf.mean(-1, keepdims=True)
    var = jnp.square(xf - mu).mean(-1, keepdims=True)
    return ((xf - mu) * lax.rsqrt(var + LN_EPS) * g.astype(jnp.float32) + b.astype(jnp.float32)).astype(x.dtype)

def rms_norm(x, g):
    xf = x.astype(jnp.float32)
    return xf * lax.rsqrt(jnp.mean(xf * xf, -1, keepdims=True) + RMS_EPS) * g.astype(jnp.float32)

def partial_rope(x):
    T = x.shape[1]
    half = ROPE_DIM // 2
    inv_freq = jnp.power(ROPE_THETA, -jnp.arange(half, dtype=jnp.float32) * 2.0 / ROPE_DIM)
    ang = jnp.arange(T, dtype=jnp.float32)[:, None] * inv_freq[None, :]
    cos = jnp.cos(ang)[None, :, None, :]
    sin = jnp.sin(ang)[None, :, None, :]
    xf = x.astype(jnp.float32)
    x1, x2, rest = xf[..., :half], xf[..., half:ROPE_DIM], xf[..., ROPE_DIM:]
    out = jnp.concatenate([x1 * cos - x2 * sin, x1 * sin + x2 * cos, rest], axis=-1)
    return out.astype(x.dtype)

def gla_chunked(q, k, v, log_decay):
    B, H, T, dk = q.shape
    dv = v.shape[-1]
    C = GLA_CHUNK
    nc = T // C
    q = q.reshape(B, H, nc, C, dk)
    k = k.reshape(B, H, nc, C, dk)
    v = v.reshape(B, H, nc, C, dv)
    b = jnp.cumsum(log_decay.reshape(B, H, nc, C, dk), axis=3)
    ref = b[:, :, :, C // 2 - 1:C // 2, :]
    a = jnp.einsum('bhncd,bhnsd->bhncs', q * jnp.exp(b - ref), k * jnp.exp(ref - b))
    causal = jnp.tril(jnp.ones((C, C), dtype=bool))
    o_intra = jnp.einsum('bhncs,bhnsv->bhncv', jnp.where(causal, a, 0.0), v)
    b_last = b[:, :, :, -1, :]
    q_inter = q * jnp.exp(b)
    k_state = k * jnp.exp(b_last[:, :, :, None, :] - b)
    decay_last = jnp.exp(b_last)

    def step(S, inp):
        qn, kn, vn, dn = inp
        o = jnp.einsum('bhcd,bhdv->bhcv', qn, S)
        S = dn[..., None] * S + jnp.einsum('bhcd,bhcv->bhdv', kn, vn)
        return S, o

    xs = (jnp.moveaxis(q_inter, 2, 0), jnp.moveaxis(k_state, 2, 0),
          jnp.moveaxis(v, 2, 0), jnp.moveaxis(decay_last, 2, 0))
    S0 = jnp.zeros((B, H, dk, dv), jnp.float32)
    _, o_inter = lax.scan(step, S0, xs)
    o = o_intra + jnp.moveaxis(o_inter, 0, 2)
    return o.reshape(B, H, T, dv)

def moba_attention(q, k, v):
    B, H, T, hd = q.shape
    nb = -(-T // MOBA_BLOCK)
    T_pad = nb * MOBA_BLOCK
    n_sel = min(MOBA_TOPK, nb)
    scale = hd ** -0.5
    pad = ((0, 0), (0, 0), (0, T_pad - T), (0, 0))
    k_pad = jnp.pad(k, pad)
    v_pad = jnp.pad(v, pad)
    kb = k_pad.reshape(B, H, nb, MOBA_BLOCK, hd)
    vb = v_pad.reshape(B, H, nb, MOBA_BLOCK, hd)
    k_mean = kb.astype(jnp.float32).mean(axis=3)
    gate = jnp.einsum('bhtd,bhnd->bhtn', q.astype(jnp.float32), k_mean)
    q_blk = jnp.arange(T) // MOBA_BLOCK
    past = jnp.arange(nb)[None, :] < q_blk[:, None]
    gate = jnp.where(past, gate, NEG_INF)
    _, sel = lax.top_k(gate, n_sel)
    sel_valid = sel < q_blk[:, None]
    bi = jnp.arange(B)[:, None, None, None]
    hi = jnp.arange(H)[None, :, None, None]
    Q = MOBA_Q_CHUNK

    def chunk(c):
        t0 = c * Q
        qc = lax.dynamic_slice_in_dim(q, t0, Q, axis=2)
        sc = lax.dynamic_slice_in_dim(sel, t0, Q, axis=2)
        okc = lax.dynamic_slice_in_dim(sel_valid, t0, Q, axis=2)
        k_sel = kb[bi, hi, sc]
        v_sel = vb[bi, hi, sc]
        blk0 = (t0 // MOBA_BLOCK) * MOBA_BLOCK
        k_own = lax.dynamic_slice_in_dim(k_pad, blk0, MOBA_BLOCK, axis=2)
        v_own = lax.dynamic_slice_in_dim(v_pad, blk0, MOBA_BLOCK, axis=2)
        qpos = t0 + jnp.arange(Q)
        kpos = blk0 + jnp.arange(MOBA_BLOCK)
        s_sel = jnp.einsum('bhqd,bhqskd->bhqsk', qc, k_sel).astype(jnp.float32) * scale
        s_sel = jnp.where(okc[..., None], s_sel, NEG_INF).reshape(B, H, Q, n_sel * MOBA_BLOCK)
        s_own = jnp.einsum('bhqd,bhkd->bhqk', qc, k_own).astype(jnp.float32) * scale
        s_own = jnp.where(kpos[None, :] <= qpos[:, None], s_own, NEG_INF)
        p = jax.nn.softmax(jnp.concatenate([s_sel, s_own], axis=-1), axis=-1).astype(v.dtype)
        p_sel = p[..., :n_sel * MOBA_BLOCK].reshape(B, H, Q, n_sel, MOBA_BLOCK)
        p_own = p[..., n_sel * MOBA_BLOCK:]
        return (jnp.einsum('bhqsk,bhqskd->bhqd', p_sel, v_sel)
                + jnp.einsum('bhqk,bhkd->bhqd', p_own, v_own))

    out = lax.map(chunk, jnp.arange(T // Q))
    return jnp.moveaxis(out, 0, 2).reshape(B, H, T, hd)

def hybrid_token_mixer(x, w_in, gla_w_decay, gla_b_decay, gla_norm_g, w_out):
    B, T, _ = x.shape
    proj = x @ w_in
    (q_a, k_a, v_a, r_a, lr_a, q_b, k_b, v_b, gate_a, gate_b) = jnp.split(proj, IN_SPLIT_POINTS, axis=-1)

    def heads(t, h):
        return t.reshape(B, T, h, -1).transpose(0, 2, 1, 3).astype(jnp.float32)

    log_decay = jax.nn.log_sigmoid((lr_a @ gla_w_decay + gla_b_decay).astype(jnp.float32)) / GLA_GATE_NORM
    o_a = gla_chunked(heads(q_a, GLA_HEADS) * (GLA_DK ** -0.5), heads(k_a, GLA_HEADS),
                      heads(v_a, GLA_HEADS), heads(log_decay, GLA_HEADS))
    o_a = o_a.transpose(0, 2, 1, 3)
    o_a = rms_norm(o_a, gla_norm_g) * jax.nn.silu(r_a.reshape(B, T, GLA_HEADS, GLA_DV).astype(jnp.float32))
    y_a = o_a.reshape(B, T, GLA_V_W).astype(x.dtype)

    qb = partial_rope(q_b.reshape(B, T, MOBA_HEADS, MOBA_HD)).transpose(0, 2, 1, 3)
    kb = partial_rope(k_b.reshape(B, T, MOBA_HEADS, MOBA_HD)).transpose(0, 2, 1, 3)
    vb = v_b.reshape(B, T, MOBA_HEADS, MOBA_HD).transpose(0, 2, 1, 3)
    o_b = moba_attention(qb, kb, vb)
    y_b = o_b.transpose(0, 2, 1, 3).reshape(B, T, MOBA_W).astype(x.dtype)

    y = jax.nn.sigmoid(gate_a) * y_a + jax.nn.sigmoid(gate_b) * y_b
    return y @ w_out

def peer_ffn(x, w_q, sub_keys, u_tab, v_tab):
    B, T, D = x.shape
    N = B * T
    K = PEER_TOPK
    xt = x.reshape(N, D)
    qry = (xt @ w_q).reshape(N, PEER_HEADS, 2, PEER_DKEY // 2).astype(jnp.float32)
    s = jnp.einsum('nhpd,pkd->nhpk', qry, sub_keys.astype(jnp.float32))
    s_top, i_top = lax.top_k(s, K)
    cand = (s_top[:, :, 0, :, None] + s_top[:, :, 1, None, :]).reshape(N, PEER_HEADS, K * K)
    cand_id = (i_top[:, :, 0, :, None] * PEER_NKEYS + i_top[:, :, 1, None, :]).reshape(N, PEER_HEADS, K * K)
    best, pos = lax.top_k(cand, K)
    expert = jnp.take_along_axis(cand_id, pos, axis=-1)
    gate = jax.nn.softmax(best, axis=-1)
    nchunk = N // PEER_TOKEN_CHUNK

    def chunk(args):
        xc, ec, gc = args
        u = u_tab[ec]
        hid = jax.nn.gelu(jnp.einsum('cd,chkd->chk', xc, u).astype(jnp.float32), approximate=False)
        w = (gc * hid).astype(x.dtype)
        return jnp.einsum('chk,chkd->cd', w, v_tab[ec])

    out = lax.map(chunk, (xt.reshape(nchunk, PEER_TOKEN_CHUNK, D),
                          expert.reshape(nchunk, PEER_TOKEN_CHUNK, PEER_HEADS, K),
                          gate.reshape(nchunk, PEER_TOKEN_CHUNK, PEER_HEADS, K)))
    return out.reshape(B, T, D)

def setup_inputs(seed: int = 0) -> dict:
    key = jax.random.key(seed)
    ks = jax.random.split(key, 16)
    f32 = jnp.float32

    def nrm(k, shape, s):
        return jax.random.normal(k, shape, f32) * s

    col_scale = jnp.concatenate([jnp.full((w,), DEEPNORM_BETA if is_v else 1.0, f32)
                                 for w, is_v in zip(IN_SPLITS, IN_IS_VALUE)])
    return {
        "x": nrm(ks[0], (BATCH, SEQ, D_MODEL), 1.0),
        "w_in": nrm(ks[1], (DEPTH, D_MODEL, IN_WIDTH), D_MODEL ** -0.5) * col_scale,
        "gla_w_decay": nrm(ks[2], (DEPTH, GLA_LOWRANK, GLA_QK_W), GLA_LOWRANK ** -0.5),
        "gla_b_decay": nrm(ks[3], (DEPTH, GLA_QK_W), 0.1),
        "gla_norm_g": 1.0 + nrm(ks[4], (DEPTH, GLA_DV), 0.02),
        "w_out": nrm(ks[5], (DEPTH, D_MODEL, D_MODEL), D_MODEL ** -0.5 * DEEPNORM_BETA),
        "ln1_g": 1.0 + nrm(ks[6], (DEPTH, D_MODEL), 0.02),
        "ln1_b": nrm(ks[7], (DEPTH, D_MODEL), 0.02),
        "peer_w_q": nrm(ks[8], (DEPTH, D_MODEL, PEER_HEADS * PEER_DKEY), D_MODEL ** -0.5),
        "peer_sub_keys": nrm(ks[9], (DEPTH, 2, PEER_NKEYS, PEER_DKEY // 2), (PEER_DKEY // 2) ** -0.5),
        "peer_u": nrm(ks[10], (DEPTH, PEER_N_EXPERTS, D_MODEL), D_MODEL ** -0.5),
        "peer_v": nrm(ks[11], (DEPTH, PEER_N_EXPERTS, D_MODEL), DEEPNORM_BETA),
        "ln2_g": 1.0 + nrm(ks[12], (DEPTH, D_MODEL), 0.02),
        "ln2_b": nrm(ks[13], (DEPTH, D_MODEL), 0.02),
    }

def reference(x, w_in, gla_w_decay, gla_b_decay, gla_norm_g, w_out, ln1_g, ln1_b,
              peer_w_q, peer_sub_keys, peer_u, peer_v, ln2_g, ln2_b):
    for l in range(DEPTH):
        h = hybrid_token_mixer(x, w_in[l], gla_w_decay[l], gla_b_decay[l], gla_norm_g[l], w_out[l])
        x = layer_norm(DEEPNORM_ALPHA * x + h, ln1_g[l], ln1_b[l])
        h = peer_ffn(x, peer_w_q[l], peer_sub_keys[l], peer_u[l], peer_v[l])
        x = layer_norm(DEEPNORM_ALPHA * x + h, ln2_g[l], ln2_b[l])
    return x


_drawn_inputs = setup_inputs


def setup_inputs(seed=0):
    import zlib

    import numpy as np

    out = dict(_drawn_inputs(seed))
    spreads = {}
    factors = {'gla_norm_g': 3.701, 'ln2_g': 2.89, 'ln2_b': 2.747}
    for name, (base, spread) in spreads.items():
        noise = np.random.default_rng([zlib.crc32(name.encode()), seed]).standard_normal(out[name].shape)
        drawn = base * np.exp(spread * noise) if base else spread * noise
        out[name] = __import__('jax').numpy.asarray(drawn.astype(out[name].dtype))
    for name, factor in factors.items():
        out[name] = (out[name] * factor).astype(out[name].dtype)
    return out
```

```python
import numpy as np
import concourse.bass as bass
from concourse import mybir
from concourse.alu_op_type import AluOpType as ALU

F32 = mybir.dt.float32
F32R = mybir.dt.float32r
U32 = mybir.dt.uint32
ACT = mybir.ActivationFunctionType
AX = mybir.AxisListType

P = 128
SEQ, D = 256, 1024
NT = SEQ // P
KC = D // P
W = 1024
NS = 4
AHEAD = NS - 1

GH, GDK, GDV, GLR, GC = 4, D // 8, D // 4, 16, 64
NCH = SEQ // GC
GATE_NORM = 16.0
MH, HD = 8, D // 8
HALF = HD // 8
THETA = 500000.0
PH, NK, TOPK = 8, 128, 16
ALPHA = 2.0 ** 0.25
LN_EPS, RMS_EPS, NEG = 1e-5, 1e-6, -1e30
LOWEST = -3.0e38

CW = 512
ORDER = (("q_b", 1024), ("k_b", 1024), ("v_b", 1024), ("q_a", 512), ("k_a", 512),
         ("v_a", 1024), ("r_a", 1024), ("gate_b", 1024), ("gate_a", 1024))
WIDTH_IN = (("q_a", 512), ("k_a", 512), ("v_a", 1024), ("r_a", 1024), ("lr", 16), ("q_b", 1024),
            ("k_b", 1024), ("v_b", 1024), ("gate_a", 1024), ("gate_b", 1024))
AT = {}
_o = 0
for _n, _w in ORDER:
    AT[_n] = _o
    _o += _w
PW = _o
NCHUNK = PW // CW

TILES_IN = NCHUNK * 4
TILES_OUT = D // P
TILES_Q = PH * 2
TILES_U = NK
TILES_V = NK
T_OUT = TILES_IN
T_Q = T_OUT + TILES_OUT
T_U = T_Q + TILES_Q
T_V = T_U + TILES_U
T_END = T_V + TILES_V
LOOPED = 6


class Tile:

    def __init__(self, first, i=None, per=0):
        self.first, self.i, self.per = first, i, per
        self.slot = first % NS

    def plus(self, n):
        return Tile(self.first + n, self.i, self.per)

    def number(self, add=0):
        return self.first + add if self.i is None else self.i * self.per + (self.first + add)

    def round(self, times=1, add=0):
        r = self.first // NS * times + add
        return r if self.i is None else self.i * (self.per // NS * times) + r


class Chain:

    def __init__(self, eng, sem, spare):
        self.eng, self.sem, self.spare = eng, sem, spare
        self.n, self.i, self.per = 0, None, 0

    def enter(self, i, per):
        self.i, self.per, self.start = i, per, self.n

    def leave(self, times):
        assert self.n - self.start == self.per, (self.n - self.start, self.per)
        self.n = self.start + times * self.per
        self.i = None

    def step(self, ins):
        ins.then_inc(self.sem, 1)
        self.n += 1

    def wait(self):
        if self.i is None:
            self.eng.wait_ge(self.sem, self.n)
        else:
            hold(self.eng, self.sem, self.i * self.per + self.n, self.spare)

    def do(self, ins):
        self.step(ins)
        self.wait()


def hold(eng, sem, value, spare):
    eng.wait_ge(sem, value)
    eng.sem_inc(spare, 1)


def layer(nc, x, xT, w_lr, w_tiles_in, w_tiles_out, w_tiles_q, w_tiles_u, w_tiles_v, w_decay,
          b_decay, norm_g, keysT, ln1_g, ln1_b, ln2_g, ln2_b, cos, sin, out):
    start = (nc.sbuf_base + 63) // 64 * 64
    at = [start]

    def place(name, shape, dt=F32, alias=None):
        size = int(np.prod(shape[1:])) * 4
        offset = at[0] if alias is None else alias
        t = nc.alloc_sbuf_tensor_at(name, shape, dt, offset=offset)
        if alias is None:
            at[0] += (size + 31) // 32 * 32
        return t

    ring_at = at[0]
    raw = place("raw", [P, NS, W])
    wlo = place("wlo", [P, NS, W], F32R, alias=ring_at)
    whi = place("whi", [P, NS, W], F32R)
    act_at = at[0]
    ahi = place("ahi", [P, KC, SEQ], F32R)
    alo = place("alo", [P, KC, SEQ], F32R)
    hot_i = place("hot_i", [P, 2, 8, P], alias=act_at)
    hot_j = place("hot_j", [P, 2, 8, P], alias=act_at + 8192)
    xt = place("xt", [P, NT, D])
    ident = place("ident", [P, P])
    keys = place("keys", [P, 2, NK])
    iota = place("iota", [P, P])
    stats = place("stats", [P, NT, 2, 6])
    mv = place("mv", [P, NT, 2])
    rstd = place("rstd", [P, NT])
    work_at = at[0]

    proj = place("proj", [P, NT, PW])
    xraw_at = at[0]
    xraw = place("xraw", [P, KC, SEQ])
    rope_t = place("rope_t", [P, 4, 2 * MH, HALF])
    state = place("state", [P, NCH - 1, GH, GDV], alias=xraw_at)
    g1b = place("g1b", [P, D])
    b1b = place("b1b", [P, D])
    qk = place("qk", [P, 2, 4 * P])
    masked = place("masked", [P, 2, 3 * P])
    probs = place("probs", [P, 2, 3 * P])
    probsT = place("probsT", [P, 2, 3 * P])
    causal = place("causal", [P, 3 * P])
    gla = [place(f"gla{n}", [P, GH, NCH, GC]) for n in range(5)]
    ksT = place("ksT", [P, NT, GH, P])
    attT = place("attT", [P, NT, GH, P])
    chunk_mask = place("chunk_mask", [P, P])
    scan_mask = place("scan_mask", [P, SEQ])
    rope_c = place("rope_c", [P, NT, HALF])
    rope_s = place("rope_s", [P, NT, HALF])
    gnorm = place("gnorm", [P, GDV])
    wlr = place("wlr", [P, KC, GLR])
    lrT = place("lrT", [GLR, SEQ])
    wdec = place("wdec", [GLR, GH * GDK])
    bdec = place("bdec", [P, GH])
    elast = place("elast", [P, GH, NCH])
    nmax = place("nmax", [P, 2, 2])
    rowsum = place("rowsum", [P, 2, 2])
    rrow = place("rrow", [P, 2, 2])
    ssq = place("ssq", [P, NT * GH])
    rrms = place("rrms", [P, NT * GH])
    square = place("square", [P, GDV])
    assert at[0] <= nc.sbuf_usable_end, at[0]

    at[0] = work_at
    H = place("H", [P, NK, SEQ])
    SC = NK - 2 * PH
    tail_at = at[0]
    sel = place("sel", [P, 3, NT * P])
    selT = place("selT", [P, 3, SEQ])
    qs = place("qs", [P, 2, SEQ])
    s_cur = place("s_cur", [P, 2, NK])
    s_cut = place("s_cut", [P, 2, NK])
    top = place("top", [P, 2, TOPK])
    topi = place("topi", [P, 2, TOPK], U32)
    topf = place("topf", [P, 2, TOPK])
    cand = place("cand", [P, TOPK, TOPK])
    cand_cut = place("cand_cut", [P, TOPK, TOPK])
    best = place("best", [P, TOPK])
    pos = place("pos", [P, TOPK], U32)
    posab = place("posab", [P, 2, TOPK], U32)
    posf = place("posf", [P, 2, TOPK])
    hot16 = place("hot16", [P, 2, TOPK, TOPK])
    nbest = place("nbest", [P, 1])
    gexp = place("gexp", [P, TOPK])
    gsum = place("gsum", [P, 1])
    grec = place("grec", [P, 1])
    gate8 = place("gate8", [P, 2, 8])
    assert at[0] <= nc.sbuf_usable_end, at[0]
    at[0] = tail_at
    hhi = place("hhi", [P, NS, SEQ], F32R)
    hlo = place("hlo", [P, NS, SEQ], F32R)
    g2b = place("g2b", [P, D])
    b2b = place("b2b", [P, D])
    assert at[0] <= nc.sbuf_usable_end, at[0]

    ps = nc.alloc_psum_tensor("ps", [P, 8, CW], F32)
    HID = (2, 3, 4, 5)
    OUTB = (6, 7, 0, 1)

    names = ("raw_full0 raw_full1 raw_full2 raw_full3 in_xT in_lr in_x in_small in_ln1 in_ln2 hi_ready "
             "lo_ready_dve lo_ready_pool tiles_used evac_act evac_dve consts act_split_hi "
             "act_split_lo lr_done lr_copied z_done z_read roped mo_tp mo_qk mo_s mo_max mo_exp "
             "mo_pt mo_ptc mo_o mo_out gl_l gl_sum gl_exp gl_tp gl_qk gl_mm gl_ks gl_att gl_ds "
             "gl_state gl_o gl_ssq gl_var gl_sqrt gates_f gates_p y_ready y_tp out_done ln_var "
             "ln_sqrt ln_half ln_pool ln_done x1_tp q_copied sc_done sc_copied hid_used r_neg r_exp "
             "sel_done sel_tp selT_done hot_ready hot_scaled g_done g_used w_hi w_lo v_done out_ready "
             "stored dve_own pool_own act_own spare ").split()
    S = {n: nc.alloc_semaphore(n) for n in names}

    class s:
        pass
    raw_full = [S[f"raw_full{n}"] for n in range(NS)]

    block = nc.Block()
    block.__enter__()

    def spare_hold(e, sem, value):
        hold(e, sem, value, S["spare"])

    @block.sync
    def _(sp):
        def load(tile, src, wait=True):
            if wait:
                sp.wait_ge(S["tiles_used"], tile.number(1 - NS))
            sp.dma_start(raw[:, tile.slot, :], src).then_inc(raw_full[tile.slot], 16)

        sp.dma_start(xraw[:, :, :], xT).then_inc(S["in_xT"], 16)
        for k in range(NS):
            load(Tile(k), w_tiles_in[k, :, :], wait=False)
        for first, n, src, skip in ((0, TILES_IN, w_tiles_in, 1), (T_OUT, TILES_OUT, w_tiles_out, 0),
                                    (T_Q, TILES_Q, w_tiles_q, 0), (T_U, TILES_U, w_tiles_u, 0),
                                    (T_V, TILES_V, w_tiles_v, 0)):
            with sp.Fori(skip, n // NS) as i:
                for k in range(NS):
                    load(Tile(first + k, i, NS), src[bass.ds(i * NS + k, 1), :, :].rearrange("a p n -> p (a n)"))
        for t in range(NT):
            sp.wait_ge(S["out_ready"], t + 1)
            sp.dma_start(out[t * P:(t + 1) * P, :], xt[:, t, :]).then_inc(S["stored"], 16)
        sp.wait_ge(S["stored"], 16 * NT)

    @block.gpsimd
    def _(pool):
        own = Chain(pool, S["pool_own"], S["spare"])

        def split_lo(tile):
            if tile.slot == NS - 1:
                pool.wait_ge(S["hi_ready"], tile.number(1))
                pool.tensor_tensor(wlo[:, tile.slot, :], raw[:, tile.slot, :],
                                   whi[:, tile.slot, :].bitcast(F32), ALU.subtract)\
                    .then_inc(S["lo_ready_pool"], 1)

        pool.dma_start(wlr[:, :, :], w_lr).then_inc(S["in_lr"], 16)
        pool.dma_start(wdec[:, :], w_decay).then_inc(S["in_small"], 16)
        pool.dma_start(bdec[:, :], b_decay).then_inc(S["in_small"], 16)
        pool.dma_start(rope_c[:, :, :], cos).then_inc(S["in_small"], 16)
        pool.dma_start(rope_s[:, :, :], sin).then_inc(S["in_small"], 16)
        pool.dma_start(keys[:, :, :], keysT).then_inc(S["in_small"], 16)
        pool.dma_start(gnorm[:, :], norm_g.to_broadcast([P, GDV])).then_inc(S["in_small"], 16)
        pool.dma_start(xt[:, :, :], x.rearrange("(t p) d -> p t d", p=P)).then_inc(S["in_x"], 16)
        pool.dma_start(g1b[:, :], ln1_g.to_broadcast([P, D])).then_inc(S["in_ln1"], 16)
        pool.dma_start(b1b[:, :], ln1_b.to_broadcast([P, D])).then_inc(S["in_ln1"], 16)

        own.step(pool.memset(scan_mask[:, :], 1.0))
        own.step(pool.memset(ident[:, :], 0.0))
        own.step(pool.memset(causal[:, :], 0.0))
        own.step(pool.memset(chunk_mask[:, :], 1.0))
        own.step(pool.memset(attT[:, :, :, :], 0.0))
        own.do(pool.iota(iota[:, :], [[1, P]], base=0, channel_multiplier=0,
                         allow_small_or_imprecise_dtypes=True))
        own.step(pool.memset(scan_mask[:, :].rearrange("p (c t) -> p c t", t=GC)[:, :, 0:1], 0.0))
        own.step(pool.affine_select(out=ident[:, :], in_=ident[:, :], compare_op=ALU.not_equal, fill=1.0,
                                    base=0, pattern=[[-1, P]], channel_multiplier=1))
        for c in (0, 2):
            part = causal[:, c * P:(c + 1) * P]
            own.step(pool.affine_select(out=part, in_=part, compare_op=ALU.is_ge, fill=NEG, base=0,
                                        pattern=[[-1, P]], channel_multiplier=1))
        own.do(pool.affine_select(out=chunk_mask[:, :], in_=chunk_mask[:, :], compare_op=ALU.is_ge,
                                  fill=0.0, base=0, pattern=[[1, P]], channel_multiplier=-1))
        own.do(pool.memset(chunk_mask[0:GC, GC:P], 0.0))
        pool.sem_inc(S["consts"], 1)

        with pool.Fori(0, LOOPED) as i:
            split_lo(Tile(3, i, NS))

        pool.wait_ge(S["in_small"], 96)
        pool.wait_ge(S["evac_act"], 4)
        pool.wait_ge(S["evac_dve"], 4)
        for t in range(NT):
            heads = proj[:, t, 0:2 * D].rearrange("p (h d) -> p h d", d=HD)
            x1, x2 = heads[:, :, 0:HALF], heads[:, :, HALF:2 * HALF]
            c = rope_c[:, t, None, :].to_broadcast([P, 2 * MH, HALF])
            sn = rope_s[:, t, None, :].to_broadcast([P, 2 * MH, HALF])
            for n, (a, b) in enumerate(((x1, c), (x2, sn), (x1, sn), (x2, c))):
                own.step(pool.tensor_tensor(rope_t[:, n, :, :], a, b, ALU.mult))
            own.wait()
            own.step(pool.tensor_tensor(x1, rope_t[:, 0, :, :], rope_t[:, 1, :, :], ALU.subtract))
            own.do(pool.tensor_tensor(x2, rope_t[:, 2, :, :], rope_t[:, 3, :, :], ALU.add))
        pool.sem_inc(S["roped"], 1)

        for c in range(LOOPED, NCHUNK):
            split_lo(Tile(4 * c + 3))
        pool.wait_ge(S["gates_f"], 1)
        pool.wait_ge(S["mo_out"], MH)
        for t in range(NT):
            r = proj[:, t, AT["r_a"]:AT["r_a"] + D].rearrange("p (h v) -> p h v", v=GDV)
            own.step(pool.tensor_tensor(r, r, gnorm[:, None, :].to_broadcast([P, GH, GDV]), ALU.mult))
            yb = proj[:, t, 0:D]
            own.step(pool.tensor_tensor(yb, yb, proj[:, t, AT["gate_b"]:AT["gate_b"] + D], ALU.mult))
        own.wait()
        pool.wait_ge(S["gates_f"], 2)
        for t in range(NT):
            r = proj[:, t, AT["r_a"]:AT["r_a"] + D]
            pool.tensor_tensor(r, r, proj[:, t, AT["gate_a"]:AT["gate_a"] + D], ALU.mult)\
                .then_inc(S["gates_p"], 1)
        for k in range(2):
            split_lo(Tile(T_OUT + 4 * k + 3))
        pool.wait_ge(S["in_ln1"], 32)
        pool.wait_ge(S["ln_half"], 1)
        own.do(pool.tensor_tensor(xt[:, 1, :], xt[:, 1, :], g1b[:, :], ALU.mult))
        pool.tensor_tensor(xt[:, 1, :], xt[:, 1, :], b1b[:, :], ALU.add).then_inc(S["ln_pool"], 1)

        with pool.Fori(0, (T_V - T_Q) // NS) as i:
            split_lo(Tile(T_Q + 3, i, NS))
        pool.wait_ge(S["g_used"], SEQ // 8)
        pool.dma_start(g2b[:, :], ln2_g.to_broadcast([P, D])).then_inc(S["in_ln2"], 16)
        pool.dma_start(b2b[:, :], ln2_b.to_broadcast([P, D])).then_inc(S["in_ln2"], 16)
        with pool.Fori(0, TILES_V // NS) as i:
            split_lo(Tile(T_V + 3, i, NS))

    @block.scalar
    def _(act):
        own = Chain(act, S["act_own"], S["spare"])

        def split_hi(tile):
            act.wait_ge(raw_full[tile.slot], tile.round(16, 16))
            act.activation(whi[:, tile.slot, :], raw[:, tile.slot, :], ACT.Copy)\
                .then_inc(S["hi_ready"], 1)

        act.wait_ge(S["in_xT"], 16)
        act.activation(ahi[:, :, :], xraw[:, :, :], ACT.Copy).then_inc(S["act_split_hi"], 1)
        act.wait_ge(S["lr_done"], 1)
        act.activation(lrT[:, :], ps[0:GLR, 4, 0:SEQ], ACT.Copy).then_inc(S["lr_copied"], 1)
        for m in range(AHEAD):
            split_hi(Tile(m))
        act.wait_ge(S["z_read"], 1)
        z, l = gla[0][:, :, :, :], gla[1][:, :, :, :]
        own.do(act.activation(l, z, ACT.Abs))
        own.do(act.activation(l, l, ACT.Exp, scale=-1.0))
        act.activation(l, l, ACT.Ln, bias=1.0).then_inc(S["gl_l"], 1)

        def evac(c, bank, dst, reg):
            if reg:
                spare_hold(act, S["tiles_used"], c)
            else:
                act.wait_ge(S["tiles_used"], c)
            act.activation(dst, ps[:, bank, :], ACT.Copy).then_inc(S["evac_act"], 1)

        with act.Fori(0, LOOPED // 2) as i:
            for k in range(8):
                tile = Tile(k, i, 8)
                split_hi(tile.plus(AHEAD))
                if k % 4 == 3:
                    evac(tile.number(1), 2 * (k // 4), proj[:, 0, bass.ds((i * 2 + k // 4) * CW, CW)], True)

        scale = HD ** -0.5
        for c in range(LOOPED, NCHUNK):
            h = c - LOOPED
            for q in range(4):
                m = 4 * c + q
                if h < MH and q == 2:
                    act.wait_ge(S["mo_max"], h + 1)
                    for t, (a, b) in enumerate(((0, P), (P, 3 * P))):
                        act.activation(probs[:, h % 2, a:b], masked[:, h % 2, a:b], ACT.Exp,
                                       bias=nmax[:, h % 2, t:t + 1], scale=scale,
                                       accum_out=rowsum[:, h % 2, t:t + 1]).then_inc(S["mo_exp"], 1)
                split_hi(Tile(m + AHEAD))
                if h < MH and q == 0:
                    act.wait_ge(S["mo_tp"], h + 1)
                    act.activation(qk[:, h % 2, :], ps[:, 4, :], ACT.Copy).then_inc(S["mo_qk"], 1)
                if q == 3:
                    evac(m + 1, 2 * (c % 2), proj[:, 0, c * CW:(c + 1) * CW], False)
                    if c == LOOPED:
                        act.wait_ge(S["gl_sum"], 1)
                        own.do(act.activation(gla[1][:, :, :, :], gla[0][:, :, :, :], ACT.Exp,
                                              scale=-1.0 / GATE_NORM))
                        own.step(act.activation(gla[0][:, :, :, :], gla[0][:, :, :, :], ACT.Exp,
                                                scale=1.0 / GATE_NORM))
                    if c == LOOPED + 1:
                        act.activation(gla[3][:, :, :, :], gla[2][:, :, :, :], ACT.Exp,
                                       scale=1.0 / GATE_NORM)
                        act.activation(gla[4][:, :, :, :], gla[4][:, :, :, :], ACT.Exp,
                                       scale=1.0 / GATE_NORM)
                        act.activation(elast[:, :, :, None], gla[2][:, :, :, GC - 1:GC], ACT.Exp,
                                       scale=1.0 / GATE_NORM).then_inc(S["gl_exp"], 1)
                    if c == NCHUNK - 2:
                        act.wait_ge(S["evac_dve"], NCHUNK - 2)
                        act.wait_ge(S["evac_act"], NCHUNK - 2)
                        for name, f in (("r_a", ACT.Silu), ("gate_b", ACT.Sigmoid)):
                            v = proj[:, :, AT[name]:AT[name] + D]
                            own.step(act.activation(v, v, f))
                        own.wait()
                        act.sem_inc(S["gates_f"], 1)
        act.wait_ge(S["evac_dve"], NCHUNK)
        act.wait_ge(S["evac_act"], NCHUNK)
        v = proj[:, :, AT["gate_a"]:AT["gate_a"] + D]
        own.do(act.activation(v, v, ACT.Sigmoid))
        act.sem_inc(S["gates_f"], 1)
        act.wait_ge(S["gl_mm"], 1)
        for t in range(NT):
            act.activation(ksT[:, t, :, :].rearrange("p h d -> p (h d)"), ps[:, 4 + t, :], ACT.Copy)\
                .then_inc(S["gl_ks"], 1)
        for t in range(NT):
            act.wait_ge(S["gl_o"], t + 1)
            for h in range(GH):
                bank = ((6, 7), (0, 1))[t][h // 2]
                own.do(act.activation(square[:, :], ps[:, bank, (h % 2) * GDV:(h % 2 + 1) * GDV], ACT.Square,
                                      accum_out=ssq[:, t * GH + h:t * GH + h + 1]))
        act.sem_inc(S["gl_ssq"], 1)
        act.wait_ge(S["gl_var"], 1)
        act.activation(rrms[:, :], ssq[:, :], ACT.Sqrt).then_inc(S["gl_sqrt"], 1)

        def split_act(sem):
            for b in range(4):
                act.wait_ge(S[sem], b + 1)
                act.activation(ahi[:, 2 * b:2 * b + 2, :].rearrange("p k n -> p (k n)"), ps[:, 2 + b, :],
                               ACT.Copy).then_inc(S["act_split_hi"], 1)

        split_act("y_tp")
        for k in range(TILES_OUT):
            split_hi(Tile(T_OUT + k + AHEAD))

        def ln_sqrt(n):
            act.wait_ge(S["ln_var"], n)
            act.activation(rstd[:, :], rstd[:, :], ACT.Sqrt).then_inc(S["ln_sqrt"], 1)

        ln_sqrt(1)
        split_act("x1_tp")

        with act.Fori(0, TILES_Q // 4) as i:
            for k in range(4):
                tile = Tile(T_Q + k, i, 4)
                split_hi(tile.plus(AHEAD))
                act.wait_ge(S["tiles_used"], tile.number(1))
                act.activation(qs[:, k % 2, :], ps[:, HID[k], 0:SEQ], ACT.Copy).then_inc(S["q_copied"], 1)

        with act.Fori(0, NT * PH) as i:
            for k in range(8):
                tile = Tile(T_U + k, i, 8)
                split_hi(tile.plus(AHEAD))
                if k == 7:
                    spare_hold(act, S["r_neg"], i + 1)
                    act.activation(gexp[:, :], best[:, :], ACT.Exp, bias=nbest[:, :],
                                   accum_out=gsum[:, :]).then_inc(S["r_exp"], 1)
                spare_hold(act, S["tiles_used"], tile.number(1))
                act.activation(H[:, bass.ds(i * 8 + k, 1), :].rearrange("p a n -> p (a n)"),
                               ps[:, HID[k % 4], 0:SEQ], ACT.Gelu).then_inc(S["hid_used"], 1)

        with act.Fori(0, SEQ // 16) as i:
            for b in range(2):
                spare_hold(act, S["selT_done"], 1)
                spare_hold(act, S["hot_ready"], i * 2 + (b + 1))
                act.activation(gate8[:, b, :], selT[:, 2, bass.ds(i * 16 + 8 * b, 8)], ACT.Copy)\
                    .then_inc(S["act_own"], 1)
                act.wait_ge(S["act_own"], i * 2 + (own.n + b + 1))
                for k in range(8):
                    last = act.activation(hot_i[:, b, k, :], hot_i[:, b, k, :], ACT.Copy,
                                          scale=gate8[:, b, k:k + 1])
                last.then_inc(S["hot_scaled"], 1)

        def split_h(tile):
            n = tile.number(-T_V)
            if tile.i is None:
                if tile.first - T_V >= NS:
                    act.wait_ge(S["tiles_used"], tile.number(1 - NS))
            else:
                spare_hold(act, S["tiles_used"], tile.number(1 - NS))
            src = H[:, n, :] if tile.i is None else H[:, bass.ds(n, 1), :].rearrange("p a n -> p (a n)")
            act.activation(hhi[:, tile.slot, :], src, ACT.Copy).then_inc(S["w_hi"], 1)

        act.wait_ge(S["g_used"], SEQ // 8)
        for k in range(AHEAD):
            split_h(Tile(T_V + k))
        for k in range(4):
            split_h(Tile(T_V + k + AHEAD))
            split_hi(Tile(T_V + k + AHEAD))
        with act.Fori(1, TILES_V // 4 - 1) as i:
            for k in range(4):
                tile = Tile(T_V + k, i, 4).plus(AHEAD)
                split_h(tile)
                split_hi(tile)
        for m in range(T_END - 4 + AHEAD, T_END):
            split_h(Tile(m))
            split_hi(Tile(m))
        ln_sqrt(2)

    @block.vector
    def _(dve):
        own = Chain(dve, S["dve_own"], S["spare"])

        def split_lo(tile):
            if tile.slot < NS - 1:
                dve.wait_ge(S["hi_ready"], tile.number(1))
                dve.tensor_tensor(wlo[:, tile.slot, :], raw[:, tile.slot, :],
                                  whi[:, tile.slot, :].bitcast(F32), ALU.subtract)\
                    .then_inc(S["lo_ready_dve"], 1)

        dve.wait_ge(S["act_split_hi"], 1)
        dve.tensor_tensor(alo[:, :, :], xraw[:, :, :], ahi[:, :, :].bitcast(F32), ALU.subtract)\
            .then_inc(S["act_split_lo"], 1)
        dve.wait_ge(S["in_small"], 96)
        dve.wait_ge(S["z_done"], 1)
        for h in range(GH):
            own.step(dve.tensor_scalar(gla[0][:, h, :, :].rearrange("p c t -> p (c t)"),
                                       ps[:, 4 + h // 2, (h % 2) * SEQ:(h % 2 + 1) * SEQ],
                                       bdec[:, h:h + 1], None, ALU.add))
        own.wait()
        dve.sem_inc(S["z_read"], 1)
        for m in range(AHEAD):
            split_lo(Tile(m))
        dve.wait_ge(S["gl_l"], 1)
        own.do(dve.scalar_tensor_tensor(out=gla[1][:, :, :, :].rearrange("p h c t -> p (h c t)"),
                                        in0=gla[0][:, :, :, :].rearrange("p h c t -> p (h c t)"), scalar=0.0,
                                        in1=gla[1][:, :, :, :].rearrange("p h c t -> p (h c t)"),
                                        op0=ALU.min, op1=ALU.subtract))
        dve.wait_ge(S["consts"], 1)
        for h in range(GH):
            own.step(dve.tensor_tensor_scan(gla[2][:, h, :, :].rearrange("p c t -> p (c t)"), scan_mask[:, :],
                                            gla[1][:, h, :, :].rearrange("p c t -> p (c t)"), 0.0,
                                            ALU.mult, ALU.add))
        own.wait()

        def rows(a):
            return a.rearrange("p h c t -> p (h c) t")

        b_all = rows(gla[2][:, :, :, :])
        own.step(dve.tensor_tensor(rows(gla[0][:, :, :, :]), b_all,
                                   b_all[:, :, GC // 2 - 1:GC // 2].to_broadcast([P, GH * NCH, GC]),
                                   ALU.subtract))
        own.do(dve.tensor_tensor(rows(gla[4][:, :, :, :]),
                                 b_all[:, :, GC - 1:GC].to_broadcast([P, GH * NCH, GC]), b_all,
                                 ALU.subtract))
        dve.sem_inc(S["gl_sum"], 1)

        with dve.Fori(0, LOOPED // 2) as i:
            for k in range(8):
                tile = Tile(k, i, 8)
                split_lo(tile.plus(AHEAD))
                if k % 4 == 3:
                    spare_hold(dve, S["tiles_used"], tile.number(1))
                    dve.tensor_copy(proj[:, 1, bass.ds((i * 2 + k // 4) * CW, CW)],
                                    ps[:, 2 * (k // 4) + 1, :]).then_inc(S["evac_dve"], 1)

        scale = HD ** -0.5

        def normalize(h):
            dve.wait_ge(S["mo_exp"], 2 * h + 2)
            own.step(dve.reciprocal(rrow[:, h % 2, :], rowsum[:, h % 2, :]))
            dve.wait_ge(S["mo_o"], h + 1)
            own.wait()
            for t in range(NT):
                last = dve.tensor_scalar(proj[:, t, h * HD:(h + 1) * HD], ps[:, 7, t * P:(t + 1) * P],
                                         rrow[:, h % 2, t:t + 1], None, ALU.mult)
            last.then_inc(S["mo_out"], 1)

        for c in range(LOOPED, NCHUNK):
            h = c - LOOPED
            for q in range(4):
                m = 4 * c + q
                if q == 0 and 1 <= h <= MH:
                    normalize(h - 1)
                if q == 2 and h < MH:
                    dve.wait_ge(S["mo_s"], h + 1)
                    own.do(dve.tensor_tensor(masked[:, h % 2, :], ps[:, 5, 0:3 * P], causal[:, :], ALU.add))
                    own.step(dve.tensor_reduce(nmax[:, h % 2, 0:1], masked[:, h % 2, 0:P], AX.X, ALU.max))
                    own.do(dve.tensor_reduce(nmax[:, h % 2, 1:2], masked[:, h % 2, P:3 * P], AX.X, ALU.max))
                    dve.tensor_scalar(nmax[:, h % 2, :], nmax[:, h % 2, :], -scale, None, ALU.mult)\
                        .then_inc(S["mo_max"], 1)
                if q == 3 and h < MH:
                    dve.wait_ge(S["mo_pt"], h + 1)
                    dve.tensor_copy(probsT[:, h % 2, :], ps[:, 6, 0:3 * P]).then_inc(S["mo_ptc"], 1)
                split_lo(Tile(m + AHEAD))
                if q == 3:
                    dve.wait_ge(S["tiles_used"], m + 1)
                    dve.tensor_copy(proj[:, 1, c * CW:(c + 1) * CW], ps[:, 2 * (c % 2) + 1, :])\
                        .then_inc(S["evac_dve"], 1)
                if c == NCHUNK - 2 and q == 1:
                    dve.wait_ge(S["gl_exp"], 1)
                    dve.wait_ge(S["gl_tp"], 1)
                    for b in range(2):
                        def part(n):
                            return gla[n][:, 2 * b:2 * b + 2, :, :].rearrange("p h c t -> p (h c t)")
                        for n in (0, 3):
                            dve.scalar_tensor_tensor(out=part(n), in0=ps[:, 4 + b, :], scalar=GDK ** -0.5,
                                                     in1=part(n), op0=ALU.mult, op1=ALU.mult)
                        for n in (1, 4):
                            last = dve.tensor_tensor(part(n), ps[:, 6 + b, :], part(n), ALU.mult)
                    last.then_inc(S["gl_qk"], 1)
        dve.wait_ge(S["gl_mm"], 1)
        for t in range(NT):
            last = dve.copy_predicated(attT[:, t, :, :],
                                       chunk_mask[:, None, :].to_broadcast([P, GH, P]).bitcast(U32),
                                       ps[:, 6 + t, :].rearrange("p (h c) -> p h c", c=P))
        last.then_inc(S["gl_att"], 1)
        dve.wait_ge(S["gl_ds"], 1)
        own.do(dve.tensor_copy(state[:, 0, :, :].rearrange("p (b h) v -> p b (h v)", b=2), ps[:, 0:2, :]))
        dve.sem_inc(S["gl_state"], 1)
        for c in range(1, NCH - 1):
            dve.wait_ge(S["gl_ds"], c + 1)
            for h in range(GH):
                own.step(dve.scalar_tensor_tensor(out=state[:, c, h, :], in0=state[:, c - 1, h, :],
                                                  scalar=elast[:, h, c:c + 1],
                                                  in1=ps[:, 2 * c + h // 2, (h % 2) * GDV:(h % 2 + 1) * GDV],
                                                  op0=ALU.mult, op1=ALU.add))
            own.wait()
            dve.sem_inc(S["gl_state"], 1)
        dve.wait_ge(S["gl_ssq"], 1)
        dve.tensor_scalar(ssq[:, :], ssq[:, :], 1.0 / GDV, RMS_EPS, ALU.mult, ALU.add)\
            .then_inc(S["gl_var"], 1)
        dve.wait_ge(S["gl_sqrt"], 1)
        own.do(dve.reciprocal(rrms[:, :], rrms[:, :]))
        for t in range(NT):
            dve.wait_ge(S["gates_p"], t + 1)
            for h in range(GH):
                f = proj[:, t, AT["r_a"] + h * GDV:AT["r_a"] + (h + 1) * GDV]
                bank = ((6, 7), (0, 1))[t][h // 2]
                own.step(dve.scalar_tensor_tensor(out=f, in0=ps[:, bank, (h % 2) * GDV:(h % 2 + 1) * GDV],
                                                  scalar=rrms[:, t * GH + h:t * GH + h + 1], in1=f,
                                                  op0=ALU.mult, op1=ALU.mult))
            own.wait()
            dve.tensor_tensor(proj[:, t, 0:D], proj[:, t, 0:D], proj[:, t, AT["r_a"]:AT["r_a"] + D],
                              ALU.add).then_inc(S["y_ready"], 1)

        def split_act(count):
            for b in range(4):
                dve.wait_ge(S["act_split_hi"], count + b + 1)
                dve.tensor_tensor(alo[:, 2 * b:2 * b + 2, :].rearrange("p k n -> p (k n)"), ps[:, 2 + b, :],
                                  ahi[:, 2 * b:2 * b + 2, :].rearrange("p k n -> p (k n)").bitcast(F32),
                                  ALU.subtract).then_inc(S["act_split_lo"], 1)

        split_act(1)
        for k in range(TILES_OUT):
            split_lo(Tile(T_OUT + k + AHEAD))

        def layer_norm(banks, n, g, b, pool_helps):
            for t in range(NT):
                for half in range(2):
                    xs = xt[:, t, half * CW:(half + 1) * CW]
                    own.step(dve.scalar_tensor_tensor(out=xs, in0=xs, scalar=ALPHA, in1=ps[:, banks[2 * t + half], :],
                                                      op0=ALU.mult, op1=ALU.add))
            own.wait()
            for t in range(NT):
                for half in range(2):
                    own.step(dve.bn_stats(stats[:, t, half, :], xt[:, t, half * CW:(half + 1) * CW]))
            own.wait()
            for t in range(NT):
                own.step(dve.bn_aggr(mv[:, t, :], stats[:, t, :, :].rearrange("p a b -> p (a b)")))
            own.wait()
            dve.tensor_scalar(rstd[:, :], mv[:, :, 1], LN_EPS, None, ALU.add).then_inc(S["ln_var"], 1)
            dve.wait_ge(S["ln_sqrt"], n)
            own.do(dve.reciprocal(rstd[:, :], rstd[:, :]))
            for t in (1, 0) if pool_helps else (0, 1):
                own.do(dve.tensor_scalar(xt[:, t, :], xt[:, t, :], mv[:, t, 0:1], rstd[:, t:t + 1],
                                         ALU.subtract, ALU.mult))
                if pool_helps and t == 1:
                    dve.sem_inc(S["ln_half"], 1)
                    continue
                own.do(dve.tensor_tensor(xt[:, t, :], xt[:, t, :], g, ALU.mult))
                dve.tensor_tensor(xt[:, t, :], xt[:, t, :], b, ALU.add)\
                    .then_inc(S["ln_done"] if pool_helps else S["out_ready"], 1)

        dve.wait_ge(S["in_x"], 16)
        dve.wait_ge(S["in_ln1"], 32)
        dve.wait_ge(S["tiles_used"], T_Q)
        layer_norm(OUTB, 1, g1b[:, :], b1b[:, :], True)
        split_act(5)

        with dve.Fori(0, TILES_Q // 4) as i:
            for k in range(4):
                tile = Tile(T_Q + k, i, 4)
                split_lo(tile.plus(AHEAD))
                spare_hold(dve, S["sc_done"], i * 4 + (k + 1))
                dst = H[:, SC:NK, :].rearrange("p (t h) n -> p t (h n)", t=NT)
                dve.tensor_copy(dst[:, :, bass.ds(i * (4 * NK) + k * NK, NK)],
                                ps[:, k % 2, 0:2 * NK].rearrange("p (t k) -> p t k", t=NT))\
                    .then_inc(S["sc_copied"], 1)

        def routing(i):
            dve_max, dve_idx = dve.max, dve.max_index
            own.do(dve.tensor_copy(s_cur[:, :, :].rearrange("p a k -> p (a k)"),
                                   H[:, bass.ds(i + SC, 1), :].rearrange("p a n -> p (a n)")))
            for a in range(2):
                own.do(dve_max(top[:, a, 0:8], s_cur[:, a, :]))
                own.step(dve_idx(topi[:, a, 0:8], top[:, a, 0:8], s_cur[:, a, :]))
                own.do(dve.match_replace(s_cut[:, a, :], top[:, a, 0:8], s_cur[:, a, :], LOWEST))
                yield
                own.do(dve_max(top[:, a, 8:16], s_cut[:, a, :]))
                own.do(dve_idx(topi[:, a, 8:16], top[:, a, 8:16], s_cut[:, a, :]))
            yield
            own.step(dve.tensor_copy(topf[:, :, :], topi[:, :, :]))
            own.do(dve.tensor_tensor(cand[:, :, :], top[:, 0, :, None].to_broadcast([P, TOPK, TOPK]),
                                     top[:, 1, None, :].to_broadcast([P, TOPK, TOPK]), ALU.add))
            c1, c2 = (x[:, :, :].rearrange("p a b -> p (a b)") for x in (cand, cand_cut))
            own.do(dve_max(best[:, 0:8], c1))
            own.step(dve_idx(pos[:, 0:8], best[:, 0:8], c1))
            own.do(dve.match_replace(c2, best[:, 0:8], c1, LOWEST))
            yield
            own.do(dve_max(best[:, 8:16], c2))
            own.do(dve_idx(pos[:, 8:16], best[:, 8:16], c2))
            own.step(dve.tensor_scalar(posab[:, 0, :], pos[:, :], 4, None, ALU.logical_shift_right))
            own.step(dve.tensor_scalar(posab[:, 1, :], pos[:, :], TOPK - 1, None, ALU.bitwise_and))
            own.do(dve.tensor_scalar(nbest[:, :], best[:, 0:1], -1.0, None, ALU.mult))
            dve.sem_inc(S["r_neg"], 1)
            own.do(dve.tensor_copy(posf[:, :, :], posab[:, :, :]))
            yield
            for a in range(2):
                own.step(dve.tensor_tensor(hot16[:, a, :, :], posf[:, a, :, None].to_broadcast([P, TOPK, TOPK]),
                                           iota[:, None, 0:TOPK].to_broadcast([P, TOPK, TOPK]), ALU.is_equal))
            own.wait()
            for a in range(2):
                own.step(dve.tensor_tensor(hot16[:, a, :, :], hot16[:, a, :, :],
                                           topf[:, a, None, :].to_broadcast([P, TOPK, TOPK]), ALU.mult))
            own.wait()
            yield
            for a in range(2):
                own.step(dve.tensor_reduce(sel[:, a, bass.ds(i * TOPK, TOPK)], hot16[:, a, :, :], AX.X, ALU.add))
            yield
            spare_hold(dve, S["r_exp"], i + 1)
            own.do(dve.reciprocal(grec[:, :], gsum[:, :]))
            own.do(dve.tensor_scalar(sel[:, 2, bass.ds(i * TOPK, TOPK)], gexp[:, :], grec[:, :], None, ALU.mult))
            yield

        spare_hold(dve, S["sc_copied"], TILES_Q)
        with dve.Fori(0, NT * PH) as i:
            own.enter(i, 30)
            steps = routing(i)
            for k in range(8):
                split_lo(Tile(T_U + k, i, 8).plus(AHEAD))
                if k > 0:
                    next(steps, None)
                if k == 7:
                    for _ in steps:
                        pass
            own.leave(NT * PH)
        dve.sem_inc(S["sel_done"], 1)

        dve.wait_ge(S["sel_tp"], 1)
        own.step(dve.tensor_copy(selT[:, 0:2, :].rearrange("p a n -> p (a n)"), ps[:, 6, :]))
        own.do(dve.tensor_copy(selT[:, 2, :], ps[:, 7, 0:SEQ]))
        dve.sem_inc(S["selT_done"], 1)

        def hots(b, i):
            for hot, a in ((hot_i, 0), (hot_j, 1)):
                last = dve.tensor_tensor(hot[:, b, :, :], iota[:, None, :].to_broadcast([P, 8, P]),
                                         selT[:, a, bass.ds(i * 16 + 8 * b, 8)][:, :, None].to_broadcast([P, 8, P]),
                                         ALU.is_equal)
            last.then_inc(S["hot_ready"], 1)

        def into_h(b, i):
            spare_hold(dve, S["g_done"], i * 2 + (b + 1))
            hv = H[:, :, bass.ds(i * 16 + 8 * b, 8)].rearrange("p i n -> p n i")
            g = ps[:, 4 + 2 * b:6 + 2 * b, :].rearrange("p b (n i) -> p (b n) i", i=NK)
            dve.tensor_tensor(hv, hv, g, ALU.mult).then_inc(S["g_used"], 1)

        dve.wait_ge(S["hid_used"], TILES_U)
        with dve.Fori(0, SEQ // 16) as i:
            hots(0, i)
            hots(1, i)
            into_h(0, i)
            into_h(1, i)

        def split_h(tile):
            n = tile.number(-T_V)
            if tile.i is None:
                dve.wait_ge(S["w_hi"], n + 1)
                src = H[:, n, :]
            else:
                dve.wait_ge(S["w_hi"], tile.number(1 - T_V))
                src = H[:, bass.ds(n, 1), :].rearrange("p a n -> p (a n)")
            dve.tensor_tensor(hlo[:, tile.slot, :], src, hhi[:, tile.slot, :].bitcast(F32), ALU.subtract)\
                .then_inc(S["w_lo"], 1)

        for k in range(AHEAD):
            split_h(Tile(T_V + k))
        for k in range(4):
            split_h(Tile(T_V + k + AHEAD))
            split_lo(Tile(T_V + k + AHEAD))
        with dve.Fori(1, TILES_V // 4 - 1) as i:
            for k in range(4):
                tile = Tile(T_V + k, i, 4).plus(AHEAD)
                split_h(tile)
                split_lo(tile)
        for m in range(T_END - 4 + AHEAD, T_END):
            split_h(Tile(m))
            split_lo(Tile(m))
        dve.wait_ge(S["in_ln2"], 32)
        dve.wait_ge(S["tiles_used"], T_END)
        layer_norm((0, 1, 2, 3), 2, g2b[:, :], b2b[:, :], False)

    @block.tensor
    def _(pe):
        def tile_ready(tile):
            if tile.slot < NS - 1:
                pe.wait_ge(S["lo_ready_dve"], tile.round(NS - 1, tile.slot + 1))
            else:
                pe.wait_ge(S["lo_ready_pool"], tile.round(1, 1))

        def three(out, ah, al, bh, bl, start, stop, moving_first=False):
            pe.matmul(out, ah, bh, start=start, stop=False)
            pe.matmul(out, ah, bl, start=False, stop=False)
            return pe.matmul(out, al, bh, start=False, stop=stop)

        pe.wait_ge(S["in_xT"], 16)
        pe.wait_ge(S["in_lr"], 16)
        for c in range(KC):
            last = pe.matmul(ps[0:GLR, 4, 0:SEQ], wlr[:, c, :], xraw[:, c, :], start=c == 0, stop=c == KC - 1)
        last.then_inc(S["lr_done"], 1)
        pe.wait_ge(S["in_small"], 96)
        pe.wait_ge(S["lr_copied"], 1)
        for h in range(GH):
            last = pe.matmul(ps[:, 4 + h // 2, (h % 2) * SEQ:(h % 2 + 1) * SEQ],
                             wdec[:, h * GDK:(h + 1) * GDK], lrT[:, :], start=True, stop=True)
        last.then_inc(S["z_done"], 1)

        def project(tile, c2, q):
            tile_ready(tile)
            for t in range(NT):
                for kk in range(2):
                    k = 2 * q + kk
                    cols = slice(kk * CW, (kk + 1) * CW)
                    last = three(ps[:, 2 * c2 + t, :], ahi[:, k, t * P:(t + 1) * P], alo[:, k, t * P:(t + 1) * P],
                                 whi[:, tile.slot, cols], wlo[:, tile.slot, cols], k == 0, k == KC - 1)
            last.then_inc(S["tiles_used"], 1)

        pe.wait_ge(S["act_split_lo"], 1)
        for c in range(2):
            for q in range(4):
                project(Tile(4 * c + q), c, q)
        with pe.Fori(1, LOOPED // 2) as i:
            for c in range(2):
                pe.wait_ge(S["evac_act"], i * 2 + (c - 1))
                pe.wait_ge(S["evac_dve"], i * 2 + (c - 1))
                for q in range(4):
                    project(Tile(4 * c + q, i, 8), c, q)

        def turn(dst, src):
            return pe.transpose(dst, src, ident[:, :])

        def head_transposes(h):
            pe.wait_ge(S["roped"], 1)
            if h > 0:
                pe.wait_ge(S["mo_qk"], h)
            for n, part in enumerate((0, D)):
                for t in range(NT):
                    last = turn(ps[:, 4, (2 * n + t) * P:(2 * n + t + 1) * P],
                                proj[:, t, part + h * HD:part + (h + 1) * HD])
            last.then_inc(S["mo_tp"], 1)

        def head_scores(h):
            pe.wait_ge(S["mo_qk"], h + 1)
            if h > 0:
                pe.wait_ge(S["mo_max"], h)
            a = qk[:, h % 2, :]
            pe.matmul(ps[:, 5, 0:P], a[:, 0:P], a[:, 2 * P:3 * P], start=True, stop=True)
            pe.matmul(ps[:, 5, P:3 * P], a[:, P:2 * P], a[:, 2 * P:4 * P], start=True, stop=True)\
                .then_inc(S["mo_s"], 1)

        def head_probs(h):
            pe.wait_ge(S["mo_exp"], 2 * h + 2)
            if h > 0:
                pe.wait_ge(S["mo_ptc"], h)
            for n in range(3):
                last = turn(ps[:, 6, n * P:(n + 1) * P], probs[:, h % 2, n * P:(n + 1) * P])
            last.then_inc(S["mo_pt"], 1)

        def head_output(h):
            pe.wait_ge(S["mo_ptc"], h + 1)
            if h > 0:
                pe.wait_ge(S["mo_out"], h)
            v = AT["v_b"] + h * HD
            pt = probsT[:, h % 2, :]
            pe.matmul(ps[:, 7, 0:P], pt[:, 0:P], proj[:, 0, v:v + HD], start=True, stop=True)
            pe.matmul(ps[:, 7, P:2 * P], pt[:, P:2 * P], proj[:, 0, v:v + HD], start=True, stop=False)
            pe.matmul(ps[:, 7, P:2 * P], pt[:, 2 * P:3 * P], proj[:, 1, v:v + HD], start=False, stop=True)\
                .then_inc(S["mo_o"], 1)

        def gla_transposes():
            pe.wait_ge(S["mo_out"], MH)
            for n, name in enumerate(("q_a", "k_a")):
                for h in range(GH):
                    for t in range(NT):
                        col = ((h % 2) * NT + t) * P
                        last = turn(ps[:, 4 + 2 * n + h // 2, col:col + P],
                                    proj[:, t, AT[name] + h * GDK:AT[name] + (h + 1) * GDK])
            last.then_inc(S["gl_tp"], 1)

        def flat(n, h):
            return gla[n][:, h, :, :].rearrange("p c t -> p (c t)")

        def gla_within():
            pe.wait_ge(S["gl_qk"], 1)
            for t in range(NT):
                for h in range(GH):
                    turn(ps[:, 4 + t, h * P:(h + 1) * P], flat(4, h)[:, t * P:(t + 1) * P])
            for t in range(NT):
                for h in range(GH):
                    last = pe.matmul(ps[:, 6 + t, h * P:(h + 1) * P], flat(1, h)[:, t * P:(t + 1) * P],
                                     flat(0, h)[:, t * P:(t + 1) * P], start=True, stop=True)
            last.then_inc(S["gl_mm"], 1)

        for c in range(LOOPED, NCHUNK):
            h = c - LOOPED
            pe.wait_ge(S["evac_act"], c - 1)
            pe.wait_ge(S["evac_dve"], c - 1)
            beside = (head_transposes, head_scores, head_probs, head_output)
            for q in range(4):
                project(Tile(4 * c + q), c % 2, q)
                if h < MH:
                    beside[q](h)
                if c == NCHUNK - 2 and q == 0:
                    gla_transposes()
                if c == NCHUNK - 1 and q == 0:
                    gla_within()

        pe.wait_ge(S["evac_act"], NCHUNK)
        pe.wait_ge(S["evac_dve"], NCHUNK)
        pe.wait_ge(S["gl_ks"], 2)
        for c in range(NCH - 1):
            lo, t = (c % 2) * GC, c // 2
            for h in range(GH):
                v = AT["v_a"] + h * GDV
                last = pe.matmul(ps[:, 2 * c + h // 2, (h % 2) * GDV:(h % 2 + 1) * GDV],
                                 ksT[lo:lo + GC, t, h, :], proj[lo:lo + GC, t, v:v + GDV], start=True, stop=True)
            last.then_inc(S["gl_ds"], 1)
        pe.wait_ge(S["gl_att"], 1)
        for t in range(NT):
            pe.wait_ge(S["gl_state"], 2 * t + 1)
            for h in range(GH):
                v = AT["v_a"] + h * GDV
                bank = ((6, 7), (0, 1))[t][h // 2]
                cols = slice((h % 2) * GDV, (h % 2 + 1) * GDV)
                last = pe.matmul(ps[:, bank, cols], attT[:, t, h, :], proj[:, t, v:v + GDV], start=True,
                                 stop=False, skip_group_check=True)
                for c in (2 * t, 2 * t + 1):
                    if c > 0:
                        rows = slice((c % 2) * GC, (c % 2 + 1) * GC)
                        last = pe.matmul(ps[rows, bank, cols], flat(3, h)[:, c * GC:(c + 1) * GC],
                                         state[:, c - 1, h, :], start=False, stop=True, skip_group_check=True)
            last.then_inc(S["gl_o"], 1)

        def turn_act(src, sem, ready):
            for b in range(4):
                for kk in range(2):
                    for t in range(NT):
                        for sm, n in (ready[t] if b == 0 and kk == 0 else ()):
                            pe.wait_ge(sm, n)
                        k = 2 * b + kk
                        last = turn(ps[:, 2 + b, (kk * NT + t) * P:(kk * NT + t + 1) * P], src(t, k))
                last.then_inc(sem, 1)

        turn_act(lambda t, k: proj[:, t, k * P:(k + 1) * P], S["y_tp"],
                 (((S["y_ready"], 1),), ((S["y_ready"], 2),)))
        pe.wait_ge(S["act_split_lo"], 5)
        for k in range(TILES_OUT):
            tile = Tile(T_OUT + k)
            tile_ready(tile)
            for t in range(NT):
                for half in range(2):
                    cols = slice(half * CW, (half + 1) * CW)
                    last = three(ps[:, OUTB[2 * t + half], :], ahi[:, k, t * P:(t + 1) * P], alo[:, k, t * P:(t + 1) * P],
                                 whi[:, tile.slot, cols], wlo[:, tile.slot, cols], k == 0, k == KC - 1)
            last.then_inc(S["tiles_used"], 1)

        turn_act(lambda t, k: xt[:, t, k * P:(k + 1) * P], S["x1_tp"],
                 (((S["ln_done"], 1),), ((S["ln_pool"], 1),)))
        pe.wait_ge(S["act_split_lo"], 9)

        def by_tokens(tile, bank):
            tile_ready(tile)
            for k in range(KC):
                cols = slice(k * P, (k + 1) * P)
                o = ps[:, bank, 0:SEQ]
                wh, wl = whi[:, tile.slot, cols], wlo[:, tile.slot, cols]
                last = three(o, wh, wl, ahi[:, k, :], alo[:, k, :], k == 0, k == KC - 1)
            last.then_inc(S["tiles_used"], 1)

        def scores(i, k):
            pe.wait_ge(S["q_copied"], i * 4 + (k + 1))
            if k >= 2:
                pe.wait_ge(S["sc_copied"], i * 4 + (k - 1))
            for t in range(NT):
                last = pe.matmul(ps[:, k % 2, t * P:(t + 1) * P], qs[:, k % 2, t * P:(t + 1) * P], keys[:, k % 2, :],
                                 start=True, stop=True)
            last.then_inc(S["sc_done"], 1)

        with pe.Fori(0, TILES_Q // 4) as i:
            for k in range(4):
                by_tokens(Tile(T_Q + k, i, 4), HID[k])
                if k > 0:
                    scores(i, k - 1)
            scores(i, 3)
            pe.wait_ge(S["sc_copied"], i * 4 + 4)

        for k in range(4):
            by_tokens(Tile(T_U + k), HID[k])
        with pe.Fori(1, TILES_U // 4) as i:
            for k in range(4):
                pe.wait_ge(S["hid_used"], i * 4 + (k - 3))
                by_tokens(Tile(T_U + k, i, 4), HID[k])

        pe.wait_ge(S["sel_done"], 1)
        for a in range(3):
            for t in range(NT):
                last = turn(ps[:, 6 + a // 2, ((a % 2) * NT + t) * P:((a % 2) * NT + t + 1) * P],
                            sel[:, a, t * P:(t + 1) * P])
        last.then_inc(S["sel_tp"], 1)

        def gate_tables(b, i, wait):
            if wait:
                pe.wait_ge(S["g_used"], i * 2 + (b - 1))
            pe.wait_ge(S["hot_scaled"], b + 1 if i is None else i * 2 + (b + 1))
            for k in range(8):
                last = pe.matmul(ps[:, 4 + 2 * b + k // 4, (k % 4) * P:(k % 4 + 1) * P], hot_j[:, b, k, :],
                                 hot_i[:, b, k, :], start=True, stop=True)
            last.then_inc(S["g_done"], 1)

        pe.wait_ge(S["selT_done"], 1)
        for b in range(2):
            gate_tables(b, None, False)
        with pe.Fori(1, SEQ // 16) as i:
            for b in range(2):
                gate_tables(b, i, True)

        def values(tile, start, stop):
            pe.wait_ge(S["w_lo"], tile.number(1 - T_V))
            tile_ready(tile)
            for t in range(NT):
                tok = slice(t * P, (t + 1) * P)
                for half in range(2):
                    cols = slice(half * CW, (half + 1) * CW)
                    o = ps[:, 2 * t + half, :]
                    hh, hl = hhi[:, tile.slot, tok], hlo[:, tile.slot, tok]
                    wh, wl = whi[:, tile.slot, cols], wlo[:, tile.slot, cols]
                    pe.matmul(o, hh, wh, start=start, stop=False)
                    pe.matmul(o, hh, wl, start=False, stop=False)
                    last = pe.matmul(o, hl, wh, start=False, stop=stop)
            last.then_inc(S["tiles_used"], 1)

        for k in range(4):
            values(Tile(T_V + k), k == 0, False)
        with pe.Fori(1, TILES_V // 4 - 1) as i:
            for k in range(4):
                values(Tile(T_V + k, i, 4), False, False)
        for m in range(T_END - 4, T_END):
            values(Tile(m), False, m == T_END - 1)

    block.__exit__(None, None, None)


def _columns(w_in):
    parts, o = {}, 0
    for name, width in WIDTH_IN:
        parts[name] = w_in[:, o:o + width]
        o += width
    return parts


def kernel(x, w_in, gla_w_decay, gla_b_decay, gla_norm_g, w_out, ln1_g, ln1_b,
           peer_w_q, peer_sub_keys, peer_u, peer_v, ln2_g, ln2_b):
    import concourse.bacc as _bacc
    from concourse.bass_utils import run_bass_kernel_spmd as _run

    c = np.ascontiguousarray
    a = {k: np.asarray(v) for k, v in dict(
        x=x, w_in=w_in, gla_w_decay=gla_w_decay, gla_b_decay=gla_b_decay, gla_norm_g=gla_norm_g, w_out=w_out,
        ln1_g=ln1_g, ln1_b=ln1_b, peer_w_q=peer_w_q, peer_sub_keys=peer_sub_keys, peer_u=peer_u,
        peer_v=peer_v, ln2_g=ln2_g, ln2_b=ln2_b).items()}
    parts = _columns(a["w_in"][0])
    w = np.concatenate([parts[n] for n, _ in ORDER], axis=1)
    inv_freq = np.power(np.float32(THETA), -np.arange(HALF, dtype=np.float32) * np.float32(2.0) / np.float32(2 * HALF))
    ang = np.arange(SEQ, dtype=np.float32)[:, None] * inv_freq[None, :]
    rot = [c(f(ang).astype(np.float32).reshape(NT, P, HALF).transpose(1, 0, 2)) for f in (np.cos, np.sin)]
    x2 = a["x"].reshape(SEQ, D)
    arrays = {
        "x": c(x2),
        "xT": c(x2.T.reshape(KC, P, SEQ).transpose(1, 0, 2)),
        "w_lr": c(parts["lr"].reshape(KC, P, GLR).transpose(1, 0, 2)),
        "w_tiles_in": c(w.reshape(4, 2, P, NCHUNK, CW).transpose(3, 0, 2, 1, 4).reshape(TILES_IN, P, W)),
        "w_tiles_out": c(a["w_out"][0].reshape(TILES_OUT, P, W)),
        "w_tiles_q": c(a["peer_w_q"][0].reshape(KC, P, TILES_Q, P).transpose(2, 1, 0, 3).reshape(TILES_Q, P, W)),
        "w_tiles_u": c(a["peer_u"][0].reshape(NK, NK, KC, P).transpose(0, 3, 2, 1).reshape(TILES_U, P, W)),
        "w_tiles_v": c(a["peer_v"][0].reshape(TILES_V, P, W)),
        "w_decay": c(a["gla_w_decay"][0]),
        "b_decay": c(a["gla_b_decay"][0].reshape(GH, GDK).T),
        "norm_g": c(a["gla_norm_g"]),
        "keysT": c(a["peer_sub_keys"][0].transpose(2, 0, 1)),
        "ln1_g": c(a["ln1_g"]), "ln1_b": c(a["ln1_b"]), "ln2_g": c(a["ln2_g"]), "ln2_b": c(a["ln2_b"]),
        "cos": rot[0], "sin": rot[1],
    }
    nc = _bacc.Bacc("TRN2", target_bir_lowering=False, num_devices=1)
    args = [nc.dram_tensor(n, v.shape, mybir.dt.from_np(v.dtype), kind="ExternalInput").ap()
            for n, v in arrays.items()]
    args.append(nc.dram_tensor("out", (SEQ, D), F32, kind="ExternalOutput").ap())
    layer(nc, *args)
    r = _run(nc, [arrays], core_ids=[0])
    return r.results[0]["out"].reshape(1, SEQ, D)
```

```python
import numpy as np
import concourse.bass as bass
from concourse import mybir
from concourse.alu_op_type import AluOpType as ALU

F32 = mybir.dt.float32
F32R = mybir.dt.float32r
BF16 = mybir.dt.bfloat16
U32 = mybir.dt.uint32
ACT = mybir.ActivationFunctionType
AX = mybir.AxisListType

P = 128
SEQ, D = 256, 1024
NT = SEQ // P
KC = D // P
W = 1024
NS = 4
AHEAD = NS - 1

GH, GDK, GDV, GLR, GC = 4, D // 8, D // 4, 16, 64
NCH = SEQ // GC
GATE_NORM = 16.0
MH, HD = 8, D // 8
HALF = HD // 8
THETA = 500000.0
PH, NK, TOPK = 8, 128, 16
ALPHA = 2.0 ** 0.25
LN_EPS, RMS_EPS, NEG = 1e-5, 1e-6, -1e30
LOWEST = -3.0e38

CW = 512
ORDER = (("q_b", 1024), ("k_b", 1024), ("v_b", 1024), ("q_a", 512), ("k_a", 512),
         ("v_a", 1024), ("r_a", 1024), ("gate_b", 1024), ("gate_a", 1024))
WIDTH_IN = (("q_a", 512), ("k_a", 512), ("v_a", 1024), ("r_a", 1024), ("lr", 16), ("q_b", 1024),
            ("k_b", 1024), ("v_b", 1024), ("gate_a", 1024), ("gate_b", 1024))
AT = {}
_o = 0
for _n, _w in ORDER:
    AT[_n] = _o
    _o += _w
PW = _o
NCHUNK = PW // CW

TILES_IN = NCHUNK * 4
TILES_OUT = D // P
TILES_Q = PH * 2
TILES_U = NK
TILES_V = NK
T_OUT = TILES_IN
T_Q = T_OUT + TILES_OUT
T_U = T_Q + TILES_Q
T_V = T_U + TILES_U
T_END = T_V + TILES_V
DVE_COLS = 3 * W // 4
LOOPED = 6
BLK = 8
HOTS = 2
GB = 4
POOL_TOKS = 6
LAG = 3


class Tile:

    def __init__(self, first, i=None, per=0):
        self.first, self.i, self.per = first, i, per
        self.slot = first % NS

    def plus(self, n):
        return Tile(self.first + n, self.i, self.per)

    def number(self, add=0):
        return self.first + add if self.i is None else self.i * self.per + (self.first + add)

    def round(self, times=1, add=0):
        r = self.first // NS * times + add
        return r if self.i is None else self.i * (self.per // NS * times) + r


class Chain:

    def __init__(self, eng, sem, spare):
        self.eng, self.sem, self.spare = eng, sem, spare
        self.n, self.i, self.per = 0, None, 0

    def enter(self, i, per):
        self.i, self.per, self.start = i, per, self.n

    def leave(self, times):
        assert self.n - self.start == self.per, (self.n - self.start, self.per)
        self.n = self.start + times * self.per
        self.i = None

    def step(self, ins):
        ins.then_inc(self.sem, 1)
        self.n += 1

    def wait(self):
        if self.i is None:
            self.eng.wait_ge(self.sem, self.n)
        else:
            hold(self.eng, self.sem, self.i * self.per + self.n, self.spare)

    def do(self, ins):
        self.step(ins)
        self.wait()


def hold(eng, sem, value, spare):
    eng.wait_ge(sem, value)
    eng.sem_inc(spare, 1)


def layer(nc, x, xT, w_lr, w_tiles_in, w_tiles_out, w_tiles_q, w_tiles_u, w_tiles_v, w_decay,
          b_decay, norm_g, keysT, ln1_g, ln1_b, ln2_g, ln2_b, cos, sin, out):
    start = (nc.sbuf_base + 63) // 64 * 64
    at = [start]

    def place(name, shape, dt=F32, alias=None):
        size = int(np.prod(shape[1:])) * (2 if dt is BF16 else 4)
        offset = at[0] if alias is None else alias
        t = nc.alloc_sbuf_tensor_at(name, shape, dt, offset=offset)
        if alias is None:
            at[0] += (size + 31) // 32 * 32
        return t

    ring_at = at[0]
    raw = place("raw", [P, NS, W])
    wlo = place("wlo", [P, NS, W], F32R, alias=ring_at)
    whi = place("whi", [P, NS, W], F32R)
    act_at = at[0]
    ahi = place("ahi", [P, KC, SEQ], F32R)
    alo = place("alo", [P, KC, SEQ], F32R)
    hot_size = BLK * P * 4
    hot_i = [place(f"hot_i{b}", [P, BLK, P], alias=act_at + b * hot_size) for b in range(2)]
    hot_j = [place(f"hot_j{b}", [P, BLK, P], alias=act_at + (2 + b) * hot_size) for b in range(2)]
    xt = place("xt", [P, NT, D])
    ident = place("ident", [P, P])
    keys = place("keys", [P, 2, NK])
    iota = place("iota", [P, P])
    stats = place("stats", [P, NT, 2, 6])
    mv = place("mv", [P, NT, 2])
    rstd = place("rstd", [P, NT])
    gate_warm = place("gate_warm", [P, 1])
    work_at = at[0]

    proj = place("proj", [P, NT, PW])
    xraw_at = at[0]
    xraw = place("xraw", [P, KC, SEQ])
    rope_t = place("rope_t", [P, 4, 2 * MH, HALF])
    state = place("state", [P, NCH - 1, GH, GDV], alias=xraw_at)
    g1b = place("g1b", [P, D])
    b1b = place("b1b", [P, D])
    qk = place("qk", [P, 2, 4 * P])
    masked = place("masked", [P, 2, 3 * P])
    probs = place("probs", [P, 2, 3 * P])
    probsT = place("probsT", [P, 2, 3 * P])
    causal = place("causal", [P, 3 * P])
    gla = [place(f"gla{n}", [P, GH, NCH, GC]) for n in range(5)]
    ksT = place("ksT", [P, NT, GH, P])
    attT = place("attT", [P, NT, GH, P])
    chunk_mask = place("chunk_mask", [P, P])
    scan_mask = place("scan_mask", [P, SEQ])
    rope_c = place("rope_c", [P, NT, HALF])
    rope_s = place("rope_s", [P, NT, HALF])
    gnorm = place("gnorm", [P, GDV])
    wlr = place("wlr", [P, KC, GLR])
    lrT = place("lrT", [GLR, SEQ])
    wdec = place("wdec", [GLR, GH * GDK])
    bdec = place("bdec", [P, GH])
    elast = place("elast", [P, GH, NCH])
    nmax = place("nmax", [P, 2, 2])
    rowsum = place("rowsum", [P, 2, 2])
    rrow = place("rrow", [P, 2, 2])
    ssq = place("ssq", [P, NT * GH])
    rrms = place("rrms", [P, NT * GH])
    square = place("square", [P, GDV])
    assert at[0] <= nc.sbuf_usable_end, at[0]

    at[0] = work_at
    H = place("H", [P, NK, SEQ])
    SC = NK - 2 * PH
    tail_at = at[0]
    sel = place("sel", [P, 3, NT * P])
    selT = place("selT", [P, 2, SEQ], BF16)
    gateT = place("gateT", [P, SEQ])
    iota8 = place("iota8", [P, P, BLK], BF16)
    gate8 = place("gate8", [P, HOTS, BLK])
    gdiff = place("gdiff", [P, NT * P])
    gsum = place("gsum", [P, NT * PH])
    hot_at = at[0]
    qs = place("qs", [P, 2, SEQ])
    s_cur = place("s_cur", [P, 2, NK])
    s_cut = place("s_cut", [P, 2, NK])
    top = place("top", [P, 2, TOPK])
    topi = place("topi", [P, 2, TOPK], U32)
    topf = place("topf", [P, 2, TOPK])
    cand = place("cand", [P, TOPK, TOPK])
    cand_cut = place("cand_cut", [P, TOPK, TOPK])
    best = place("best", [P, TOPK])
    pos = place("pos", [P, TOPK], U32)
    posab = place("posab", [P, 2, TOPK], U32)
    posf = place("posf", [P, 2, TOPK])
    hot16 = place("hot16", [P, 2, TOPK, TOPK])
    raw_i = [place(f"raw_i{b}", [P, P, BLK], BF16, alias=hot_at + b * hot_size // 2) for b in range(HOTS)]
    raw_j = [place(f"raw_j{b}", [P, P, BLK], BF16, alias=hot_at + (HOTS + b) * hot_size // 2) for b in range(HOTS)]
    at[0] = max(at[0], hot_at + 2 * hot_size)
    assert at[0] <= nc.sbuf_usable_end, at[0]
    at[0] = tail_at
    hhi = place("hhi", [P, NS, SEQ], F32R)
    hlo = place("hlo", [P, NS, SEQ], F32R)
    g2b = place("g2b", [P, D])
    b2b = place("b2b", [P, D])
    assert at[0] <= nc.sbuf_usable_end, at[0]

    ps = nc.alloc_psum_tensor("ps", [P, 8, CW], F32)
    HID = (2, 3, 4, 5)
    OUTB = (6, 7, 0, 1)

    names = ("raw_full0 raw_full1 raw_full2 raw_full3 in_xT0 in_xT1 in_xT2 in_xT3 in_lr in_x in_small in_ln1 in_ln2 hi_ready "
             "lo_ready_dve lo_ready_pool tiles_used evac_act evac_dve consts act_split_hi "
             "act_split_lo lr_done lr_copied z_done z_read roped mo_tp mo_qk mo_s mo_max mo_exp "
             "mo_pt mo_ptc mo_o mo_out gl_l gl_sum gl_exp gl_tp gl_qk gl_mm gl_ks gl_att gl_ds "
             "gl_state gl_o gl_ssq gl_var gl_sqrt gates_f gates_p y_ready y_tp out_done ln_var "
             "ln_sqrt ln_half ln_pool ln_done x1_tp q_copied sc_done sc_copied hid_used r_neg r_exp "
             "half_done sel_done sel_tp selT_done iota8_ready hot_ready j_scaled hots_wide g_done g_used w_hi w_lo v_done out_ready "
             "stored dve_own pool_own act_own spare ").split()
    S = {n: nc.alloc_semaphore(n) for n in names}

    class s:
        pass
    raw_full = [S[f"raw_full{n}"] for n in range(NS)]
    in_xT = [S[f"in_xT{n}"] for n in range(NS)]

    block = nc.Block()
    block.__enter__()

    def spare_hold(e, sem, value):
        hold(e, sem, value, S["spare"])

    @block.sync
    def _(sp):
        def load(tile, src, wait=True):
            if wait:
                sp.wait_ge(S["tiles_used"], tile.number(1 - NS))
            sp.dma_start(raw[:, tile.slot, :], src).then_inc(raw_full[tile.slot], 16)

        for k in range(NS):
            sp.dma_start(xraw[:, 2 * k:2 * k + 2, :], xT[:, 2 * k:2 * k + 2, :]).then_inc(in_xT[k], 16)
            load(Tile(k), w_tiles_in[k, :, :], wait=False)
        for first, n, src, skip in ((0, TILES_IN, w_tiles_in, 1), (T_OUT, TILES_OUT, w_tiles_out, 0),
                                    (T_Q, TILES_Q, w_tiles_q, 0), (T_U, TILES_U, w_tiles_u, 0),
                                    (T_V, TILES_V, w_tiles_v, 0)):
            with sp.Fori(skip, n // NS) as i:
                for k in range(NS):
                    load(Tile(first + k, i, NS), src[bass.ds(i * NS + k, 1), :, :].rearrange("a p n -> p (a n)"))
        for t in range(NT):
            sp.wait_ge(S["out_ready"], t + 1)
            sp.dma_start(out[t * P:(t + 1) * P, :], xt[:, t, :]).then_inc(S["stored"], 16)
        sp.wait_ge(S["stored"], 16 * NT)

    @block.gpsimd
    def _(pool):
        own = Chain(pool, S["pool_own"], S["spare"])

        def split_lo(tile):
            pool.wait_ge(S["hi_ready"], tile.number(1))
            pool.tensor_tensor(wlo[:, tile.slot, DVE_COLS:], raw[:, tile.slot, DVE_COLS:],
                               whi[:, tile.slot, DVE_COLS:].bitcast(F32), ALU.subtract)\
                .then_inc(S["lo_ready_pool"], 1)

        pool.dma_start(wlr[:, :, :], w_lr).then_inc(S["in_lr"], 16)
        pool.dma_start(wdec[:, :], w_decay).then_inc(S["in_small"], 16)
        pool.dma_start(bdec[:, :], b_decay).then_inc(S["in_small"], 16)
        pool.dma_start(rope_c[:, :, :], cos).then_inc(S["in_small"], 16)
        pool.dma_start(rope_s[:, :, :], sin).then_inc(S["in_small"], 16)
        pool.dma_start(keys[:, :, :], keysT).then_inc(S["in_small"], 16)
        pool.dma_start(gnorm[:, :], norm_g.to_broadcast([P, GDV])).then_inc(S["in_small"], 16)
        pool.dma_start(xt[:, :, :], x.rearrange("(t p) d -> p t d", p=P)).then_inc(S["in_x"], 16)
        pool.dma_start(g1b[:, :], ln1_g.to_broadcast([P, D])).then_inc(S["in_ln1"], 16)
        pool.dma_start(b1b[:, :], ln1_b.to_broadcast([P, D])).then_inc(S["in_ln1"], 16)

        own.step(pool.memset(scan_mask[:, :], 1.0))
        own.step(pool.memset(ident[:, :], 0.0))
        own.step(pool.memset(causal[:, :], 0.0))
        own.step(pool.memset(chunk_mask[:, :], 1.0))
        own.step(pool.memset(attT[:, :, :, :], 0.0))
        own.do(pool.iota(iota[:, :], [[1, P]], base=0, channel_multiplier=0,
                         allow_small_or_imprecise_dtypes=True))
        own.step(pool.memset(scan_mask[:, :].rearrange("p (c t) -> p c t", t=GC)[:, :, 0:1], 0.0))
        own.step(pool.affine_select(out=ident[:, :], in_=ident[:, :], compare_op=ALU.not_equal, fill=1.0,
                                    base=0, pattern=[[-1, P]], channel_multiplier=1))
        for c in (0, 2):
            part = causal[:, c * P:(c + 1) * P]
            own.step(pool.affine_select(out=part, in_=part, compare_op=ALU.is_ge, fill=NEG, base=0,
                                        pattern=[[-1, P]], channel_multiplier=1))
        own.do(pool.affine_select(out=chunk_mask[:, :], in_=chunk_mask[:, :], compare_op=ALU.is_ge,
                                  fill=0.0, base=0, pattern=[[1, P]], channel_multiplier=-1))
        own.do(pool.memset(chunk_mask[0:GC, GC:P], 0.0))
        pool.sem_inc(S["consts"], 1)

        for m in range(AHEAD):
            split_lo(Tile(m))
        with pool.Fori(0, LOOPED - 2) as i:
            for k in range(4):
                split_lo(Tile(k, i, 4).plus(AHEAD))

        def rope():
            pool.wait_ge(S["in_small"], 96)
            for t in range(NT):
                pool.wait_ge(S[("evac_act", "evac_dve")[t]], 4)
                heads = proj[:, t, 0:2 * D].rearrange("p (h d) -> p h d", d=HD)
                x1, x2 = heads[:, :, 0:HALF], heads[:, :, HALF:2 * HALF]
                c = rope_c[:, t, None, :].to_broadcast([P, 2 * MH, HALF])
                sn = rope_s[:, t, None, :].to_broadcast([P, 2 * MH, HALF])
                for n, (a, b) in enumerate(((x1, c), (x2, sn), (x1, sn), (x2, c))):
                    own.step(pool.tensor_tensor(rope_t[:, n, :, :], a, b, ALU.mult))
                    if n % 2:
                        yield
                own.wait()
                own.step(pool.tensor_tensor(x1, rope_t[:, 0, :, :], rope_t[:, 1, :, :], ALU.subtract))
                own.do(pool.tensor_tensor(x2, rope_t[:, 2, :, :], rope_t[:, 3, :, :], ALU.add))
                yield

        stretches = rope()
        for m in range(4 * (LOOPED - 2), 4 * LOOPED):
            split_lo(Tile(m + AHEAD))
            next(stretches, None)
        pool.sem_inc(S["roped"], 1)

        for m in range(4 * LOOPED, T_OUT):
            split_lo(Tile(m + AHEAD))
        pool.wait_ge(S["gates_f"], 1)
        pool.wait_ge(S["mo_out"], MH)
        for t in range(NT):
            r = proj[:, t, AT["r_a"]:AT["r_a"] + D].rearrange("p (h v) -> p h v", v=GDV)
            own.step(pool.tensor_tensor(r, r, gnorm[:, None, :].to_broadcast([P, GH, GDV]), ALU.mult))
            yb = proj[:, t, 0:D]
            own.step(pool.tensor_tensor(yb, yb, proj[:, t, AT["gate_b"]:AT["gate_b"] + D], ALU.mult))
        own.wait()
        pool.wait_ge(S["gates_f"], 2)
        for t in range(NT):
            r = proj[:, t, AT["r_a"]:AT["r_a"] + D]
            pool.tensor_tensor(r, r, proj[:, t, AT["gate_a"]:AT["gate_a"] + D], ALU.mult)\
                .then_inc(S["gates_p"], 1)
        for m in range(T_OUT, T_Q):
            split_lo(Tile(m + AHEAD))
        pool.wait_ge(S["ln_done"], NT)
        pool.tensor_copy(iota8[:, :, :], iota[:, :, None].to_broadcast([P, P, BLK])).then_inc(S["iota8_ready"], 1)
        with pool.Fori(0, (T_V - T_Q) // NS) as i:
            for k in range(NS):
                split_lo(Tile(T_Q + k, i, NS).plus(AHEAD))

        def scale_j(n, b, i=None):
            if i is None:
                pool.wait_ge(S["hot_ready"], n + 1)
                if n >= HOTS:
                    pool.wait_ge(S["g_done"], n + 1 - HOTS)
                g = gateT[:, n * BLK:n * BLK + POOL_TOKS]
            else:
                pool.wait_ge(S["hot_ready"], i * GB + (b + 1))
                spare_hold(pool, S["g_done"], i * GB + (b + 1 - HOTS))
                g = gateT[:, bass.ds(i * (GB * BLK) + b * BLK, POOL_TOKS)]
            pool.tensor_tensor(hot_j[b % HOTS][:, 0:POOL_TOKS, :],
                               raw_j[b % HOTS][:, :, 0:POOL_TOKS].rearrange("p j n -> p n j"),
                               g[:, :, None].to_broadcast([P, POOL_TOKS, P]), ALU.mult)\
                .then_inc(S["j_scaled"], 1)

        pool.wait_ge(S["selT_done"], 2)
        for n in range(GB):
            scale_j(n, n)
        with pool.Fori(1, SEQ // BLK // GB) as i:
            for b in range(GB):
                scale_j(None, b, i)
        pool.wait_ge(S["g_used"], SEQ // 8)
        pool.dma_start(g2b[:, :], ln2_g.to_broadcast([P, D])).then_inc(S["in_ln2"], 16)
        pool.dma_start(b2b[:, :], ln2_b.to_broadcast([P, D])).then_inc(S["in_ln2"], 16)
        with pool.Fori(0, TILES_V // NS - 1) as i:
            for k in range(NS):
                split_lo(Tile(T_V + k, i, NS).plus(AHEAD))
        split_lo(Tile(T_END - 1))

    @block.scalar
    def _(act):
        own = Chain(act, S["act_own"], S["spare"])

        def split_hi(tile):
            act.wait_ge(raw_full[tile.slot], tile.round(16, 16))
            act.activation(whi[:, tile.slot, :], raw[:, tile.slot, :], ACT.Copy)\
                .then_inc(S["hi_ready"], 1)

        def evac(c, bank, dst, reg):
            if reg:
                spare_hold(act, S["tiles_used"], c)
            else:
                act.wait_ge(S["tiles_used"], c)
            act.activation(dst, ps[:, bank, :], ACT.Copy).then_inc(S["evac_act"], 1)

        for k in range(NS):
            act.wait_ge(in_xT[k], 16)
            act.activation(ahi[:, 2 * k:2 * k + 2, :], xraw[:, 2 * k:2 * k + 2, :], ACT.Copy)\
                .then_inc(S["act_split_hi"], 1)
            if k < AHEAD:
                split_hi(Tile(k))
        for k in range(8):
            split_hi(Tile(k + AHEAD))
            if k % 4 == 3:
                evac(k + 1, 2 * (k // 4), proj[:, 0, k // 4 * CW:(k // 4 + 1) * CW], False)
        act.wait_ge(S["lr_done"], 1)
        act.activation(lrT[:, :], ps[0:GLR, 4, 0:SEQ], ACT.Copy).then_inc(S["lr_copied"], 1)
        with act.Fori(1, LOOPED // 2) as i:
            for k in range(8):
                tile = Tile(k, i, 8)
                split_hi(tile.plus(AHEAD))
                if k % 4 == 3:
                    evac(tile.number(1), 2 * (k // 4), proj[:, 0, bass.ds((i * 2 + k // 4) * CW, CW)], True)
        act.wait_ge(S["z_read"], 1)
        z, l = gla[0][:, :, :, :], gla[1][:, :, :, :]
        own.do(act.activation(l, z, ACT.Abs))
        own.do(act.activation(l, l, ACT.Exp, scale=-1.0))
        act.activation(l, l, ACT.Ln, bias=1.0).then_inc(S["gl_l"], 1)

        scale = HD ** -0.5
        for c in range(LOOPED, NCHUNK):
            h = c - LOOPED
            for q in range(4):
                m = 4 * c + q
                if h < MH and q == 2:
                    act.wait_ge(S["mo_max"], h + 1)
                    for t, (a, b) in enumerate(((0, P), (P, 3 * P))):
                        act.activation(probs[:, h % 2, a:b], masked[:, h % 2, a:b], ACT.Exp,
                                       bias=nmax[:, h % 2, t:t + 1], scale=scale,
                                       accum_out=rowsum[:, h % 2, t:t + 1]).then_inc(S["mo_exp"], 1)
                split_hi(Tile(m + AHEAD))
                if h < MH and q == 0:
                    act.wait_ge(S["mo_tp"], h + 1)
                    act.activation(qk[:, h % 2, :], ps[:, 4, :], ACT.Copy).then_inc(S["mo_qk"], 1)
                if q == 3:
                    evac(m + 1, 2 * (c % 2), proj[:, 0, c * CW:(c + 1) * CW], False)
                    if c == LOOPED + 1:
                        act.wait_ge(S["gl_sum"], 1)
                        own.do(act.activation(gla[1][:, :, :, :], gla[0][:, :, :, :], ACT.Exp,
                                              scale=-1.0 / GATE_NORM))
                        own.step(act.activation(gla[0][:, :, :, :], gla[0][:, :, :, :], ACT.Exp,
                                                scale=1.0 / GATE_NORM))
                    if c == LOOPED + 2:
                        act.activation(gla[3][:, :, :, :], gla[2][:, :, :, :], ACT.Exp,
                                       scale=1.0 / GATE_NORM)
                        act.activation(gla[4][:, :, :, :], gla[4][:, :, :, :], ACT.Exp,
                                       scale=1.0 / GATE_NORM)
                        act.activation(elast[:, :, :, None], gla[2][:, :, :, GC - 1:GC], ACT.Exp,
                                       scale=1.0 / GATE_NORM).then_inc(S["gl_exp"], 1)
                    if c == NCHUNK - 2:
                        act.wait_ge(S["evac_dve"], NCHUNK - 2)
                        act.wait_ge(S["evac_act"], NCHUNK - 2)
                        for name, f in (("r_a", ACT.Silu), ("gate_b", ACT.Sigmoid)):
                            v = proj[:, :, AT[name]:AT[name] + D]
                            own.step(act.activation(v, v, f))
                        own.wait()
                        act.sem_inc(S["gates_f"], 1)
        act.wait_ge(S["evac_dve"], NCHUNK)
        act.wait_ge(S["evac_act"], NCHUNK)
        v = proj[:, :, AT["gate_a"]:AT["gate_a"] + D]
        own.do(act.activation(v, v, ACT.Sigmoid))
        act.sem_inc(S["gates_f"], 1)
        act.wait_ge(S["gl_mm"], 1)
        for t in range(NT):
            act.activation(ksT[:, t, :, :].rearrange("p h d -> p (h d)"), ps[:, 4 + t, :], ACT.Copy)\
                .then_inc(S["gl_ks"], 1)
        own.do(act.activation(square[:, 0:1], ident[:, 0:1], ACT.Sqrt))
        for t in range(NT):
            act.wait_ge(S["gl_o"], t + 1)
            for h in range(GH):
                bank = ((6, 7), (0, 1))[t][h // 2]
                own.do(act.activation(square[:, :], ps[:, bank, (h % 2) * GDV:(h % 2 + 1) * GDV], ACT.Square,
                                      accum_out=ssq[:, t * GH + h:t * GH + h + 1]))
            act.sem_inc(S["gl_ssq"], 1)
            act.wait_ge(S["gl_var"], t + 1)
            act.activation(rrms[:, t * GH:(t + 1) * GH], ssq[:, t * GH:(t + 1) * GH], ACT.Sqrt)\
                .then_inc(S["gl_sqrt"], 1)

        def split_act(sem):
            for b in range(4):
                act.wait_ge(S[sem], b + 1)
                act.activation(ahi[:, 2 * b:2 * b + 2, :].rearrange("p k n -> p (k n)"), ps[:, 2 + b, :],
                               ACT.Copy).then_inc(S["act_split_hi"], 1)

        split_act("y_tp")
        for k in range(TILES_OUT):
            split_hi(Tile(T_OUT + k + AHEAD))

        def ln_sqrt(n):
            for t in range(NT):
                act.wait_ge(S["ln_var"], NT * (n - 1) + t + 1)
                act.activation(rstd[:, t:t + 1], rstd[:, t:t + 1], ACT.Sqrt).then_inc(S["ln_sqrt"], 1)

        ln_sqrt(1)
        split_act("x1_tp")

        with act.Fori(0, TILES_Q // 4) as i:
            for k in range(4):
                tile = Tile(T_Q + k, i, 4)
                split_hi(tile.plus(AHEAD))
                act.wait_ge(S["tiles_used"], tile.number(1))
                act.activation(qs[:, k % 2, :], ps[:, HID[k], 0:SEQ], ACT.Copy).then_inc(S["q_copied"], 1)

        with act.Fori(0, NT * PH) as i:
            for k in range(8):
                tile = Tile(T_U + k, i, 8)
                if k > 0:
                    split_hi(tile.plus(AHEAD))
                spare_hold(act, S["tiles_used"], tile.number(1))
                act.activation(H[:, bass.ds(i * 8 + k, 1), :].rearrange("p a n -> p (a n)"),
                               ps[:, HID[k % 4], 0:SEQ], ACT.Gelu).then_inc(S["hid_used"], 1)
                if k == 0:
                    split_hi(tile.plus(AHEAD))

        act.wait_ge(S["r_neg"], 1)
        act.activation(gdiff[:, :], gdiff[:, :], ACT.Exp).then_inc(S["r_exp"], 1)

        def scale_hots(n, b, i=None):
            if i is None:
                act.wait_ge(S["hot_ready"], n + 1)
                if n >= HOTS:
                    act.wait_ge(S["g_done"], n + 1 - HOTS)
                g = gateT[:, n * BLK + POOL_TOKS:(n + 1) * BLK]
            else:
                act.wait_ge(S["hot_ready"], i * GB + (b + 1))
                spare_hold(act, S["g_done"], i * GB + (b + 1 - HOTS))
                g = gateT[:, bass.ds(i * (GB * BLK) + (b * BLK + POOL_TOKS), BLK - POOL_TOKS)]
            act.activation(gate8[:, b % HOTS, 0:BLK - POOL_TOKS], g, ACT.Copy).then_inc(S["act_own"], 1)
            act.activation(hot_i[b % HOTS][:, :, :], raw_i[b % HOTS][:, :, :].rearrange("p i n -> p n i"), ACT.Copy)
            act.wait_ge(S["act_own"], own.n + n + 1 if i is None else i * GB + (own.n + b + 1))
            for k in range(POOL_TOKS, BLK):
                last = act.activation(hot_j[b % HOTS][:, k, :], raw_j[b % HOTS][:, :, k], ACT.Copy,
                                      scale=gate8[:, b % HOTS, k - POOL_TOKS:k - POOL_TOKS + 1])
            last.then_inc(S["hots_wide"], 1)

        act.wait_ge(S["selT_done"], 2)
        for n in range(GB):
            scale_hots(n, n)
        with act.Fori(1, SEQ // BLK // GB) as i:
            for b in range(GB):
                scale_hots(None, b, i)

        def split_h(tile):
            n = tile.number(-T_V)
            if tile.i is None:
                if tile.first - T_V >= NS:
                    act.wait_ge(S["tiles_used"], tile.number(1 - NS))
            else:
                spare_hold(act, S["tiles_used"], tile.number(1 - NS))
            src = H[:, n, :] if tile.i is None else H[:, bass.ds(n, 1), :].rearrange("p a n -> p (a n)")
            act.activation(hhi[:, tile.slot, :], src, ACT.Copy).then_inc(S["w_hi"], 1)

        act.wait_ge(S["g_used"], SEQ // 8)
        for k in range(AHEAD):
            split_h(Tile(T_V + k))
        for k in range(4):
            split_h(Tile(T_V + k + AHEAD))
            split_hi(Tile(T_V + k + AHEAD))
        with act.Fori(1, TILES_V // 4 - 1) as i:
            for k in range(4):
                tile = Tile(T_V + k, i, 4).plus(AHEAD)
                split_h(tile)
                split_hi(tile)
        for m in range(T_END - 4 + AHEAD, T_END):
            split_h(Tile(m))
            split_hi(Tile(m))
        own.n += SEQ // BLK
        own.do(act.activation(gate_warm[:, :], ident[:, 0:1], ACT.Sqrt))
        ln_sqrt(2)

    @block.vector
    def _(dve):
        own = Chain(dve, S["dve_own"], S["spare"])

        def split_lo(tile):
            dve.wait_ge(S["hi_ready"], tile.number(1))
            dve.tensor_tensor(wlo[:, tile.slot, 0:DVE_COLS], raw[:, tile.slot, 0:DVE_COLS],
                              whi[:, tile.slot, 0:DVE_COLS].bitcast(F32), ALU.subtract)\
                .then_inc(S["lo_ready_dve"], 1)

        for k in range(NS):
            dve.wait_ge(S["act_split_hi"], k + 1)
            dve.tensor_tensor(alo[:, 2 * k:2 * k + 2, :], xraw[:, 2 * k:2 * k + 2, :],
                              ahi[:, 2 * k:2 * k + 2, :].bitcast(F32), ALU.subtract)\
                .then_inc(S["act_split_lo"], 1)
            if k < AHEAD:
                split_lo(Tile(k))
        for k in range(8):
            split_lo(Tile(k + AHEAD))
            if k % 4 == 3:
                dve.wait_ge(S["tiles_used"], k + 1)
                dve.tensor_copy(proj[:, 1, k // 4 * CW:(k // 4 + 1) * CW], ps[:, 2 * (k // 4) + 1, :])\
                    .then_inc(S["evac_dve"], 1)
        dve.wait_ge(S["in_small"], 96)
        dve.wait_ge(S["z_done"], 1)
        for h in range(GH):
            own.step(dve.tensor_scalar(gla[0][:, h, :, :].rearrange("p c t -> p (c t)"),
                                       ps[:, 4 + h // 2, (h % 2) * SEQ:(h % 2 + 1) * SEQ],
                                       bdec[:, h:h + 1], None, ALU.add))
        own.wait()
        dve.sem_inc(S["z_read"], 1)
        with dve.Fori(1, LOOPED // 2) as i:
            for k in range(8):
                tile = Tile(k, i, 8)
                split_lo(tile.plus(AHEAD))
                if k % 4 == 3:
                    spare_hold(dve, S["tiles_used"], tile.number(1))
                    dve.tensor_copy(proj[:, 1, bass.ds((i * 2 + k // 4) * CW, CW)],
                                    ps[:, 2 * (k // 4) + 1, :]).then_inc(S["evac_dve"], 1)

        def decay_sums():
            dve.wait_ge(S["gl_l"], 1)
            own.do(dve.scalar_tensor_tensor(out=gla[1][:, :, :, :].rearrange("p h c t -> p (h c t)"),
                                            in0=gla[0][:, :, :, :].rearrange("p h c t -> p (h c t)"), scalar=0.0,
                                            in1=gla[1][:, :, :, :].rearrange("p h c t -> p (h c t)"),
                                            op0=ALU.min, op1=ALU.subtract))
            yield
            dve.wait_ge(S["consts"], 1)
            for h in range(GH):
                own.step(dve.tensor_tensor_scan(gla[2][:, h, :, :].rearrange("p c t -> p (c t)"), scan_mask[:, :],
                                                gla[1][:, h, :, :].rearrange("p c t -> p (c t)"), 0.0,
                                                ALU.mult, ALU.add))
            own.wait()
            yield

            def rows(a):
                return a.rearrange("p h c t -> p (h c) t")

            b_all = rows(gla[2][:, :, :, :])
            own.step(dve.tensor_tensor(rows(gla[0][:, :, :, :]), b_all,
                                       b_all[:, :, GC // 2 - 1:GC // 2].to_broadcast([P, GH * NCH, GC]),
                                       ALU.subtract))
            own.do(dve.tensor_tensor(rows(gla[4][:, :, :, :]),
                                     b_all[:, :, GC - 1:GC].to_broadcast([P, GH * NCH, GC]), b_all,
                                     ALU.subtract))
            dve.sem_inc(S["gl_sum"], 1)

        scale = HD ** -0.5

        def normalize(h):
            dve.wait_ge(S["mo_exp"], 2 * h + 2)
            own.step(dve.reciprocal(rrow[:, h % 2, :], rowsum[:, h % 2, :]))
            dve.wait_ge(S["mo_o"], h + 1)
            own.wait()
            for t in range(NT):
                last = dve.tensor_scalar(proj[:, t, h * HD:(h + 1) * HD], ps[:, 7, t * P:(t + 1) * P],
                                         rrow[:, h % 2, t:t + 1], None, ALU.mult)
            last.then_inc(S["mo_out"], 1)

        sums = decay_sums()
        for c in range(LOOPED, NCHUNK):
            h = c - LOOPED
            for q in range(4):
                m = 4 * c + q
                if q == 0 and 1 <= h <= MH:
                    normalize(h - 1)
                if q == 2 and h < MH:
                    dve.wait_ge(S["mo_s"], h + 1)
                    own.do(dve.tensor_tensor(masked[:, h % 2, :], ps[:, 5, 0:3 * P], causal[:, :], ALU.add))
                    own.step(dve.tensor_reduce(nmax[:, h % 2, 0:1], masked[:, h % 2, 0:P], AX.X, ALU.max))
                    own.do(dve.tensor_reduce(nmax[:, h % 2, 1:2], masked[:, h % 2, P:3 * P], AX.X, ALU.max))
                    dve.tensor_scalar(nmax[:, h % 2, :], nmax[:, h % 2, :], -scale, None, ALU.mult)\
                        .then_inc(S["mo_max"], 1)
                if q == 3 and h < MH:
                    dve.wait_ge(S["mo_pt"], h + 1)
                    dve.tensor_copy(probsT[:, h % 2, :], ps[:, 6, 0:3 * P]).then_inc(S["mo_ptc"], 1)
                split_lo(Tile(m + AHEAD))
                if c == LOOPED + 1 or c == LOOPED and q == 3:
                    next(sums, None)
                if q == 3:
                    dve.wait_ge(S["tiles_used"], m + 1)
                    dve.tensor_copy(proj[:, 1, c * CW:(c + 1) * CW], ps[:, 2 * (c % 2) + 1, :])\
                        .then_inc(S["evac_dve"], 1)
                if c == NCHUNK - 2 and q == 1:
                    dve.wait_ge(S["gl_exp"], 1)
                    dve.wait_ge(S["gl_tp"], 1)
                    for b in range(2):
                        def part(n):
                            return gla[n][:, 2 * b:2 * b + 2, :, :].rearrange("p h c t -> p (h c t)")
                        for n in (0, 3):
                            dve.scalar_tensor_tensor(out=part(n), in0=ps[:, 4 + b, :], scalar=GDK ** -0.5,
                                                     in1=part(n), op0=ALU.mult, op1=ALU.mult)
                        for n in (1, 4):
                            last = dve.tensor_tensor(part(n), ps[:, 6 + b, :], part(n), ALU.mult)
                    last.then_inc(S["gl_qk"], 1)
        dve.wait_ge(S["gl_mm"], 1)
        for t in range(NT):
            last = dve.copy_predicated(attT[:, t, :, :],
                                       chunk_mask[:, None, :].to_broadcast([P, GH, P]).bitcast(U32),
                                       ps[:, 6 + t, :].rearrange("p (h c) -> p h c", c=P))
        last.then_inc(S["gl_att"], 1)
        dve.wait_ge(S["gl_ds"], 1)
        own.do(dve.tensor_copy(state[:, 0, :, :].rearrange("p (b h) v -> p b (h v)", b=2), ps[:, 0:2, :]))
        dve.sem_inc(S["gl_state"], 1)
        for c in range(1, NCH - 1):
            dve.wait_ge(S["gl_ds"], c + 1)
            for h in range(GH):
                own.step(dve.scalar_tensor_tensor(out=state[:, c, h, :], in0=state[:, c - 1, h, :],
                                                  scalar=elast[:, h, c:c + 1],
                                                  in1=ps[:, 2 * c + h // 2, (h % 2) * GDV:(h % 2 + 1) * GDV],
                                                  op0=ALU.mult, op1=ALU.add))
            own.wait()
            dve.sem_inc(S["gl_state"], 1)
        for t in range(NT):
            four = slice(t * GH, (t + 1) * GH)
            dve.wait_ge(S["gl_ssq"], t + 1)
            dve.tensor_scalar(ssq[:, four], ssq[:, four], 1.0 / GDV, RMS_EPS, ALU.mult, ALU.add)\
                .then_inc(S["gl_var"], 1)
            dve.wait_ge(S["gl_sqrt"], t + 1)
            own.do(dve.reciprocal(rrms[:, four], rrms[:, four]))
            dve.wait_ge(S["gates_p"], t + 1)
            for h in range(GH):
                f = proj[:, t, AT["r_a"] + h * GDV:AT["r_a"] + (h + 1) * GDV]
                bank = ((6, 7), (0, 1))[t][h // 2]
                own.step(dve.scalar_tensor_tensor(out=f, in0=ps[:, bank, (h % 2) * GDV:(h % 2 + 1) * GDV],
                                                  scalar=rrms[:, t * GH + h:t * GH + h + 1], in1=f,
                                                  op0=ALU.mult, op1=ALU.mult))
            own.wait()
            dve.tensor_tensor(proj[:, t, 0:D], proj[:, t, 0:D], proj[:, t, AT["r_a"]:AT["r_a"] + D],
                              ALU.add).then_inc(S["y_ready"], 1)

        def split_act(count):
            for b in range(4):
                dve.wait_ge(S["act_split_hi"], count + b + 1)
                dve.tensor_tensor(alo[:, 2 * b:2 * b + 2, :].rearrange("p k n -> p (k n)"), ps[:, 2 + b, :],
                                  ahi[:, 2 * b:2 * b + 2, :].rearrange("p k n -> p (k n)").bitcast(F32),
                                  ALU.subtract).then_inc(S["act_split_lo"], 1)

        split_act(NS)
        for k in range(TILES_OUT):
            split_lo(Tile(T_OUT + k + AHEAD))

        def layer_norm(banks, n, g, b, tiles, done):
            def total(t):
                for half in range(2):
                    xs = xt[:, t, half * CW:(half + 1) * CW]
                    own.step(dve.scalar_tensor_tensor(out=xs, in0=xs, scalar=ALPHA, in1=ps[:, banks[2 * t + half], :],
                                                      op0=ALU.mult, op1=ALU.add))
                own.wait()
                for half in range(2):
                    own.step(dve.bn_stats(stats[:, t, half, :], xt[:, t, half * CW:(half + 1) * CW]))
                own.wait()
                own.do(dve.bn_aggr(mv[:, t, :], stats[:, t, :, :].rearrange("p a b -> p (a b)")))
                dve.tensor_scalar(rstd[:, t:t + 1], mv[:, t, 1:2], LN_EPS, None, ALU.add)\
                    .then_inc(S["ln_var"], 1)

            dve.wait_ge(S["half_done"], n + 1)
            total(0)
            dve.wait_ge(S["tiles_used"], tiles)
            total(1)
            for t in range(NT):
                dve.wait_ge(S["ln_sqrt"], NT * n + t + 1)
                own.do(dve.reciprocal(rstd[:, t:t + 1], rstd[:, t:t + 1]))
                own.do(dve.scalar_tensor_tensor(out=xt[:, t, :], in0=xt[:, t, :], scalar=mv[:, t, 0:1], in1=g,
                                                op0=ALU.subtract, op1=ALU.mult))
                dve.scalar_tensor_tensor(out=xt[:, t, :], in0=xt[:, t, :], scalar=rstd[:, t:t + 1], in1=b,
                                         op0=ALU.mult, op1=ALU.add).then_inc(S[done], 1)

        dve.wait_ge(S["in_x"], 16)
        dve.wait_ge(S["in_ln1"], 32)
        layer_norm(OUTB, 0, g1b[:, :], b1b[:, :], T_Q, "ln_done")
        split_act(NS + 4)

        with dve.Fori(0, TILES_Q // 4) as i:
            for k in range(4):
                tile = Tile(T_Q + k, i, 4)
                split_lo(tile.plus(AHEAD))
                spare_hold(dve, S["sc_done"], i * 4 + (k + 1))
                dst = H[:, SC:NK, :].rearrange("p (t h) n -> p t (h n)", t=NT)
                dve.tensor_copy(dst[:, :, bass.ds(i * (4 * NK) + k * NK, NK)],
                                ps[:, k % 2, 0:2 * NK].rearrange("p (t k) -> p t k", t=NT))\
                    .then_inc(S["sc_copied"], 1)

        def routing(i):
            dve_max, dve_idx = dve.max, dve.max_index
            own.do(dve.tensor_copy(s_cur[:, :, :].rearrange("p a k -> p (a k)"),
                                   H[:, bass.ds(i + SC, 1), :].rearrange("p a n -> p (a n)")))
            for a in range(2):
                own.do(dve_max(top[:, a, 0:8], s_cur[:, a, :]))
                own.step(dve_idx(topi[:, a, 0:8], top[:, a, 0:8], s_cur[:, a, :]))
                own.do(dve.match_replace(s_cut[:, a, :], top[:, a, 0:8], s_cur[:, a, :], LOWEST))
                yield
                own.do(dve_max(top[:, a, 8:16], s_cut[:, a, :]))
                own.do(dve_idx(topi[:, a, 8:16], top[:, a, 8:16], s_cut[:, a, :]))
            yield
            own.step(dve.tensor_copy(topf[:, :, :], topi[:, :, :]))
            own.do(dve.tensor_tensor(cand[:, :, :], top[:, 0, :, None].to_broadcast([P, TOPK, TOPK]),
                                     top[:, 1, None, :].to_broadcast([P, TOPK, TOPK]), ALU.add))
            c1, c2 = (x[:, :, :].rearrange("p a b -> p (a b)") for x in (cand, cand_cut))
            own.do(dve_max(best[:, 0:8], c1))
            own.step(dve_idx(pos[:, 0:8], best[:, 0:8], c1))
            own.do(dve.match_replace(c2, best[:, 0:8], c1, LOWEST))
            yield
            own.do(dve_max(best[:, 8:16], c2))
            own.step(dve.tensor_copy(sel[:, 2, bass.ds(i * TOPK, TOPK)], best[:, :]))
            own.do(dve_idx(pos[:, 8:16], best[:, 8:16], c2))
            own.step(dve.tensor_scalar(posab[:, 0, :], pos[:, :], 4, None, ALU.logical_shift_right))
            own.do(dve.tensor_scalar(posab[:, 1, :], pos[:, :], TOPK - 1, None, ALU.bitwise_and))
            own.do(dve.tensor_copy(posf[:, :, :], posab[:, :, :]))
            yield
            for a in range(2):
                own.step(dve.tensor_tensor(hot16[:, a, :, :], posf[:, a, :, None].to_broadcast([P, TOPK, TOPK]),
                                           iota[:, None, 0:TOPK].to_broadcast([P, TOPK, TOPK]), ALU.is_equal))
            own.wait()
            for a in range(2):
                own.step(dve.tensor_tensor(hot16[:, a, :, :], hot16[:, a, :, :],
                                           topf[:, a, None, :].to_broadcast([P, TOPK, TOPK]), ALU.mult))
            own.wait()
            yield
            for a in range(2):
                own.step(dve.tensor_reduce(sel[:, a, bass.ds(i * TOPK, TOPK)], hot16[:, a, :, :], AX.X, ALU.add))
            own.wait()
            yield

        spare_hold(dve, S["sc_copied"], TILES_Q)
        with dve.Fori(0, NT * PH) as i:
            own.enter(i, 28)
            steps = routing(i)
            for k in range(8):
                split_lo(Tile(T_U + k, i, 8).plus(AHEAD))
                if k > 0:
                    next(steps, None)
                if k == 7:
                    for _ in steps:
                        pass
            own.leave(NT * PH)

        def by_head(a):
            return a.rearrange("p (u k) -> p u k", k=TOPK)

        vals = by_head(sel[:, 2, :])
        own.do(dve.tensor_tensor(by_head(gdiff[:, :]), vals, vals[:, :, 0:1].to_broadcast([P, NT * PH, TOPK]),
                                 ALU.subtract))
        dve.sem_inc(S["r_neg"], 1)

        def hots(n, b, i=None):
            if i is not None:
                spare_hold(dve, S["hots_wide"], i * GB + (b + 1 - HOTS))
                spare_hold(dve, S["j_scaled"], i * GB + (b + 1 - HOTS))
            elif n >= HOTS:
                dve.wait_ge(S["hots_wide"], n + 1 - HOTS)
                dve.wait_ge(S["j_scaled"], n + 1 - HOTS)
            toks = slice(n * BLK, (n + 1) * BLK) if i is None else bass.ds(i * (GB * BLK) + b * BLK, BLK)
            for hot, a in ((raw_i, 0), (raw_j, 1)):
                last = dve.tensor_tensor(hot[b % HOTS][:, :, :], iota8[:, :, :],
                                         selT[:, a, toks][:, None, :].to_broadcast([P, P, BLK]), ALU.is_equal)
            last.then_inc(S["hot_ready"], 1)

        def into_h(n, b, i=None):
            if i is None:
                dve.wait_ge(S["g_done"], n + 1)
            else:
                spare_hold(dve, S["g_done"], i * GB + (b + 1))
            toks = slice(n * BLK, (n + 1) * BLK) if i is None else bass.ds(i * (GB * BLK) + b * BLK, BLK)
            hv = H[:, :, toks].rearrange("p i n -> p n i")
            g = ps[:, 2 * (b % GB):2 * (b % GB) + 2, :].rearrange("p b (n i) -> p (b n) i", i=NK)
            dve.tensor_tensor(hv, hv, g, ALU.mult).then_inc(S["g_used"], 1)

        dve.wait_ge(S["sel_tp"], 1)
        own.do(dve.tensor_copy(selT[:, :, :].rearrange("p a n -> p (a n)"), ps[:, 6, :]))
        dve.sem_inc(S["selT_done"], 1)
        dve.wait_ge(S["iota8_ready"], 1)
        hots(0, 0)
        dve.wait_ge(S["r_exp"], 1)
        own.do(dve.tensor_reduce(gsum[:, :], by_head(gdiff[:, :]), AX.X, ALU.add))
        own.do(dve.reciprocal(gsum[:, :], gsum[:, :]))
        own.do(dve.tensor_tensor(vals, by_head(gdiff[:, :]), gsum[:, :, None].to_broadcast([P, NT * PH, TOPK]),
                                 ALU.mult))
        dve.sem_inc(S["sel_done"], 1)
        hots(1, 1)
        dve.wait_ge(S["sel_tp"], 2)
        own.do(dve.tensor_copy(gateT[:, :], ps[:, 7, 0:SEQ]))
        dve.sem_inc(S["selT_done"], 1)
        hots(2, 2)
        dve.wait_ge(S["hid_used"], TILES_U)
        into_h(0, 0)
        with dve.Fori(0, SEQ // BLK // GB - 1) as i:
            for b in range(GB):
                hots(b + LAG, b + LAG, i)
                into_h(b + 1, b + 1, i)
        hots(SEQ // BLK - 1, GB - 1)
        for n in range(SEQ // BLK - LAG, SEQ // BLK):
            into_h(n, n)

        def split_h(tile):
            n = tile.number(-T_V)
            if tile.i is None:
                dve.wait_ge(S["w_hi"], n + 1)
                src = H[:, n, :]
            else:
                dve.wait_ge(S["w_hi"], tile.number(1 - T_V))
                src = H[:, bass.ds(n, 1), :].rearrange("p a n -> p (a n)")
            dve.tensor_tensor(hlo[:, tile.slot, :], src, hhi[:, tile.slot, :].bitcast(F32), ALU.subtract)\
                .then_inc(S["w_lo"], 1)

        for k in range(AHEAD):
            split_h(Tile(T_V + k))
        for k in range(4):
            split_h(Tile(T_V + k + AHEAD))
            split_lo(Tile(T_V + k + AHEAD))
        with dve.Fori(1, TILES_V // 4 - 1) as i:
            for k in range(4):
                tile = Tile(T_V + k, i, 4).plus(AHEAD)
                split_h(tile)
                split_lo(tile)
        for m in range(T_END - 4 + AHEAD, T_END):
            split_h(Tile(m))
            split_lo(Tile(m))
        dve.wait_ge(S["in_ln2"], 32)
        layer_norm((0, 1, 2, 3), 1, g2b[:, :], b2b[:, :], T_END, "out_ready")

    @block.tensor
    def _(pe):
        def tile_ready(tile):
            pe.wait_ge(S["lo_ready_dve"], tile.number(1))
            pe.wait_ge(S["lo_ready_pool"], tile.number(1))

        def three(out, ah, al, bh, bl, start, stop):
            pe.matmul(out, ah, bh, start=start, stop=False)
            pe.matmul(out, ah, bl, start=False, stop=False)
            return pe.matmul(out, al, bh, start=False, stop=stop)

        def project(tile, c2, q):
            tile_ready(tile)
            for t in range(NT):
                for kk in range(2):
                    k = 2 * q + kk
                    cols = slice(kk * CW, (kk + 1) * CW)
                    last = three(ps[:, 2 * c2 + t, :], ahi[:, k, t * P:(t + 1) * P], alo[:, k, t * P:(t + 1) * P],
                                 whi[:, tile.slot, cols], wlo[:, tile.slot, cols], k == 0, k == KC - 1)
            last.then_inc(S["tiles_used"], 1)

        for c in range(2):
            for q in range(4):
                if c == 0:
                    pe.wait_ge(S["act_split_lo"], q + 1)
                project(Tile(4 * c + q), c, q)
        pe.wait_ge(S["in_lr"], 16)
        for c in range(KC):
            last = pe.matmul(ps[0:GLR, 4, 0:SEQ], wlr[:, c, :], xraw[:, c, :], start=c == 0, stop=c == KC - 1)
        last.then_inc(S["lr_done"], 1)
        pe.wait_ge(S["in_small"], 96)
        pe.wait_ge(S["lr_copied"], 1)
        for h in range(GH):
            last = pe.matmul(ps[:, 4 + h // 2, (h % 2) * SEQ:(h % 2 + 1) * SEQ],
                             wdec[:, h * GDK:(h + 1) * GDK], lrT[:, :], start=True, stop=True)
        last.then_inc(S["z_done"], 1)
        with pe.Fori(1, LOOPED // 2) as i:
            for c in range(2):
                pe.wait_ge(S["evac_act"], i * 2 + (c - 1))
                pe.wait_ge(S["evac_dve"], i * 2 + (c - 1))
                for q in range(4):
                    project(Tile(4 * c + q, i, 8), c, q)

        def turn(dst, src):
            return pe.transpose(dst, src, ident[:, :])

        def head_transposes(h):
            pe.wait_ge(S["roped"], 1)
            if h > 0:
                pe.wait_ge(S["mo_qk"], h)
            for n, part in enumerate((0, D)):
                for t in range(NT):
                    last = turn(ps[:, 4, (2 * n + t) * P:(2 * n + t + 1) * P],
                                proj[:, t, part + h * HD:part + (h + 1) * HD])
            last.then_inc(S["mo_tp"], 1)

        def head_scores(h):
            pe.wait_ge(S["mo_qk"], h + 1)
            if h > 0:
                pe.wait_ge(S["mo_max"], h)
            a = qk[:, h % 2, :]
            pe.matmul(ps[:, 5, 0:P], a[:, 0:P], a[:, 2 * P:3 * P], start=True, stop=True)
            pe.matmul(ps[:, 5, P:3 * P], a[:, P:2 * P], a[:, 2 * P:4 * P], start=True, stop=True)\
                .then_inc(S["mo_s"], 1)

        def head_probs(h):
            pe.wait_ge(S["mo_exp"], 2 * h + 2)
            if h > 0:
                pe.wait_ge(S["mo_ptc"], h)
            for n in range(3):
                last = turn(ps[:, 6, n * P:(n + 1) * P], probs[:, h % 2, n * P:(n + 1) * P])
            last.then_inc(S["mo_pt"], 1)

        def head_output(h):
            pe.wait_ge(S["mo_ptc"], h + 1)
            if h > 0:
                pe.wait_ge(S["mo_out"], h)
            v = AT["v_b"] + h * HD
            pt = probsT[:, h % 2, :]
            pe.matmul(ps[:, 7, 0:P], pt[:, 0:P], proj[:, 0, v:v + HD], start=True, stop=True)
            pe.matmul(ps[:, 7, P:2 * P], pt[:, P:2 * P], proj[:, 0, v:v + HD], start=True, stop=False)
            pe.matmul(ps[:, 7, P:2 * P], pt[:, 2 * P:3 * P], proj[:, 1, v:v + HD], start=False, stop=True)\
                .then_inc(S["mo_o"], 1)

        def gla_transposes():
            pe.wait_ge(S["mo_out"], MH)
            for n, name in enumerate(("q_a", "k_a")):
                for h in range(GH):
                    for t in range(NT):
                        col = ((h % 2) * NT + t) * P
                        last = turn(ps[:, 4 + 2 * n + h // 2, col:col + P],
                                    proj[:, t, AT[name] + h * GDK:AT[name] + (h + 1) * GDK])
            last.then_inc(S["gl_tp"], 1)

        def flat(n, h):
            return gla[n][:, h, :, :].rearrange("p c t -> p (c t)")

        def gla_within():
            pe.wait_ge(S["gl_qk"], 1)
            for t in range(NT):
                for h in range(GH):
                    turn(ps[:, 4 + t, h * P:(h + 1) * P], flat(4, h)[:, t * P:(t + 1) * P])
            for t in range(NT):
                for h in range(GH):
                    last = pe.matmul(ps[:, 6 + t, h * P:(h + 1) * P], flat(1, h)[:, t * P:(t + 1) * P],
                                     flat(0, h)[:, t * P:(t + 1) * P], start=True, stop=True)
            last.then_inc(S["gl_mm"], 1)

        for c in range(LOOPED, NCHUNK):
            h = c - LOOPED
            pe.wait_ge(S["evac_act"], c - 1)
            pe.wait_ge(S["evac_dve"], c - 1)
            beside = (head_transposes, head_scores, head_probs, head_output)
            for q in range(4):
                project(Tile(4 * c + q), c % 2, q)
                if h < MH:
                    beside[q](h)
                if c == NCHUNK - 2 and q == 0:
                    gla_transposes()
                if c == NCHUNK - 1 and q == 0:
                    gla_within()

        pe.wait_ge(S["evac_act"], NCHUNK)
        pe.wait_ge(S["evac_dve"], NCHUNK)
        pe.wait_ge(S["gl_ks"], 2)
        for c in range(NCH - 1):
            lo, t = (c % 2) * GC, c // 2
            for h in range(GH):
                v = AT["v_a"] + h * GDV
                last = pe.matmul(ps[:, 2 * c + h // 2, (h % 2) * GDV:(h % 2 + 1) * GDV],
                                 ksT[lo:lo + GC, t, h, :], proj[lo:lo + GC, t, v:v + GDV], start=True, stop=True)
            last.then_inc(S["gl_ds"], 1)
        pe.wait_ge(S["gl_att"], 1)
        for t in range(NT):
            pe.wait_ge(S["gl_state"], 2 * t + 1)
            for h in range(GH):
                v = AT["v_a"] + h * GDV
                bank = ((6, 7), (0, 1))[t][h // 2]
                cols = slice((h % 2) * GDV, (h % 2 + 1) * GDV)
                last = pe.matmul(ps[:, bank, cols], attT[:, t, h, :], proj[:, t, v:v + GDV], start=True,
                                 stop=False, skip_group_check=True)
                for c in (2 * t, 2 * t + 1):
                    if c > 0:
                        rows = slice((c % 2) * GC, (c % 2 + 1) * GC)
                        last = pe.matmul(ps[rows, bank, cols], flat(3, h)[:, c * GC:(c + 1) * GC],
                                         state[:, c - 1, h, :], start=False, stop=True, skip_group_check=True)
            last.then_inc(S["gl_o"], 1)

        def turn_act(src, sem, ready):
            for t in range(NT):
                pe.wait_ge(ready, t + 1)
                for b in range(4):
                    for kk in range(2):
                        last = turn(ps[:, 2 + b, (kk * NT + t) * P:(kk * NT + t + 1) * P], src(t, 2 * b + kk))
                    if t == NT - 1:
                        last.then_inc(sem, 1)

        turn_act(lambda t, k: proj[:, t, k * P:(k + 1) * P], S["y_tp"], S["y_ready"])
        pe.wait_ge(S["act_split_lo"], NS + 4)
        for k in range(TILES_OUT):
            tile = Tile(T_OUT + k)
            tile_ready(tile)
            for t in range(NT):
                for half in range(2):
                    cols = slice(half * CW, (half + 1) * CW)
                    last = three(ps[:, OUTB[2 * t + half], :], ahi[:, k, t * P:(t + 1) * P], alo[:, k, t * P:(t + 1) * P],
                                 whi[:, tile.slot, cols], wlo[:, tile.slot, cols], k == 0, k == KC - 1)
                if k == KC - 1 and t == 0:
                    last.then_inc(S["half_done"], 1)
            last.then_inc(S["tiles_used"], 1)

        turn_act(lambda t, k: xt[:, t, k * P:(k + 1) * P], S["x1_tp"], S["ln_done"])
        pe.wait_ge(S["act_split_lo"], NS + 8)

        def by_tokens(tile, bank):
            tile_ready(tile)
            for k in range(KC):
                cols = slice(k * P, (k + 1) * P)
                o = ps[:, bank, 0:SEQ]
                wh, wl = whi[:, tile.slot, cols], wlo[:, tile.slot, cols]
                last = three(o, wh, wl, ahi[:, k, :], alo[:, k, :], k == 0, k == KC - 1)
            last.then_inc(S["tiles_used"], 1)

        def scores(k, i=None):
            if i is None:
                pe.wait_ge(S["q_copied"], k + 1)
                if k >= 2:
                    pe.wait_ge(S["sc_copied"], k - 1)
            else:
                pe.wait_ge(S["q_copied"], i * 4 + (k + 1))
                pe.wait_ge(S["sc_copied"], i * 4 + (k - 1))
            for t in range(NT):
                last = pe.matmul(ps[:, k % 2, t * P:(t + 1) * P], qs[:, k % 2, t * P:(t + 1) * P], keys[:, k % 2, :],
                                 start=True, stop=True)
            last.then_inc(S["sc_done"], 1)

        by_tokens(Tile(T_Q), HID[0])
        for k in range(4):
            by_tokens(Tile(T_Q + k + 1), HID[(k + 1) % 4])
            scores(k)
        with pe.Fori(1, TILES_Q // 4) as i:
            for k in range(4):
                by_tokens(Tile(T_Q + k + 1, i, 4), HID[(k + 1) % 4])
                scores(k, i)

        for k in range(1, 4):
            by_tokens(Tile(T_U + k), HID[k])
        with pe.Fori(1, TILES_U // 4) as i:
            for k in range(4):
                pe.wait_ge(S["hid_used"], i * 4 + (k - 3))
                by_tokens(Tile(T_U + k, i, 4), HID[k])

        def turn_choices(parts, bank):
            for n, a in enumerate(parts):
                for t in range(NT):
                    last = turn(ps[:, bank, (n * NT + t) * P:(n * NT + t + 1) * P], sel[:, a, t * P:(t + 1) * P])
            last.then_inc(S["sel_tp"], 1)

        pe.wait_ge(S["r_neg"], 1)
        turn_choices((0, 1), 6)
        pe.wait_ge(S["sel_done"], 1)
        turn_choices((2,), 7)

        def gate_tables(n, b, i=None):
            if i is None:
                pe.wait_ge(S["hots_wide"], n + 1)
                pe.wait_ge(S["j_scaled"], n + 1)
            else:
                pe.wait_ge(S["hots_wide"], i * GB + (b + 1))
                pe.wait_ge(S["j_scaled"], i * GB + (b + 1))
                pe.wait_ge(S["g_used"], i * GB + (b + 1 - GB))
            for k in range(BLK):
                last = pe.matmul(ps[:, 2 * b + k // 4, (k % 4) * P:(k % 4 + 1) * P], hot_j[b % HOTS][:, k, :],
                                 hot_i[b % HOTS][:, k, :], start=True, stop=True)
            last.then_inc(S["g_done"], 1)

        pe.wait_ge(S["selT_done"], 2)
        pe.wait_ge(S["hid_used"], TILES_U)
        for n in range(GB):
            gate_tables(n, n)
        with pe.Fori(1, SEQ // BLK // GB) as i:
            for b in range(GB):
                gate_tables(None, b, i)

        def values(tile, start, stop):
            pe.wait_ge(S["w_lo"], tile.number(1 - T_V))
            tile_ready(tile)
            for t in range(NT):
                tok = slice(t * P, (t + 1) * P)
                for half in range(2):
                    cols = slice(half * CW, (half + 1) * CW)
                    o = ps[:, 2 * t + half, :]
                    hh, hl = hhi[:, tile.slot, tok], hlo[:, tile.slot, tok]
                    wh, wl = whi[:, tile.slot, cols], wlo[:, tile.slot, cols]
                    pe.matmul(o, hh, wh, start=start, stop=False)
                    pe.matmul(o, hh, wl, start=False, stop=False)
                    last = pe.matmul(o, hl, wh, start=False, stop=stop)
                if stop and t == 0:
                    last.then_inc(S["half_done"], 1)
            last.then_inc(S["tiles_used"], 1)

        for k in range(4):
            values(Tile(T_V + k), k == 0, False)
        with pe.Fori(1, TILES_V // 4 - 1) as i:
            for k in range(4):
                values(Tile(T_V + k, i, 4), False, False)
        for m in range(T_END - 4, T_END):
            values(Tile(m), False, m == T_END - 1)

    block.__exit__(None, None, None)


def _columns(w_in):
    parts, o = {}, 0
    for name, width in WIDTH_IN:
        parts[name] = w_in[:, o:o + width]
        o += width
    return parts


def kernel(x, w_in, gla_w_decay, gla_b_decay, gla_norm_g, w_out, ln1_g, ln1_b,
           peer_w_q, peer_sub_keys, peer_u, peer_v, ln2_g, ln2_b):
    import concourse.bacc as _bacc
    from concourse.bass_utils import run_bass_kernel_spmd as _run

    c = np.ascontiguousarray
    a = {k: np.asarray(v) for k, v in dict(
        x=x, w_in=w_in, gla_w_decay=gla_w_decay, gla_b_decay=gla_b_decay, gla_norm_g=gla_norm_g, w_out=w_out,
        ln1_g=ln1_g, ln1_b=ln1_b, peer_w_q=peer_w_q, peer_sub_keys=peer_sub_keys, peer_u=peer_u,
        peer_v=peer_v, ln2_g=ln2_g, ln2_b=ln2_b).items()}
    parts = _columns(a["w_in"][0])
    w = np.concatenate([parts[n] for n, _ in ORDER], axis=1)
    inv_freq = np.power(np.float32(THETA), -np.arange(HALF, dtype=np.float32) * np.float32(2.0) / np.float32(2 * HALF))
    ang = np.arange(SEQ, dtype=np.float32)[:, None] * inv_freq[None, :]
    rot = [c(f(ang).astype(np.float32).reshape(NT, P, HALF).transpose(1, 0, 2)) for f in (np.cos, np.sin)]
    x2 = a["x"].reshape(SEQ, D)
    arrays = {
        "x": c(x2),
        "xT": c(x2.T.reshape(KC, P, SEQ).transpose(1, 0, 2)),
        "w_lr": c(parts["lr"].reshape(KC, P, GLR).transpose(1, 0, 2)),
        "w_tiles_in": c(w.reshape(4, 2, P, NCHUNK, CW).transpose(3, 0, 2, 1, 4).reshape(TILES_IN, P, W)),
        "w_tiles_out": c(a["w_out"][0].reshape(TILES_OUT, P, W)),
        "w_tiles_q": c(a["peer_w_q"][0].reshape(KC, P, TILES_Q, P).transpose(2, 1, 0, 3).reshape(TILES_Q, P, W)),
        "w_tiles_u": c(a["peer_u"][0].reshape(NK, NK, KC, P).transpose(0, 3, 2, 1).reshape(TILES_U, P, W)),
        "w_tiles_v": c(a["peer_v"][0].reshape(TILES_V, P, W)),
        "w_decay": c(a["gla_w_decay"][0]),
        "b_decay": c(a["gla_b_decay"][0].reshape(GH, GDK).T),
        "norm_g": c(a["gla_norm_g"]),
        "keysT": c(a["peer_sub_keys"][0].transpose(2, 0, 1)),
        "ln1_g": c(a["ln1_g"]), "ln1_b": c(a["ln1_b"]), "ln2_g": c(a["ln2_g"]), "ln2_b": c(a["ln2_b"]),
        "cos": rot[0], "sin": rot[1],
    }
    nc = _bacc.Bacc("TRN2", target_bir_lowering=False, num_devices=1)
    args = [nc.dram_tensor(n, v.shape, mybir.dt.from_np(v.dtype), kind="ExternalInput").ap()
            for n, v in arrays.items()]
    args.append(nc.dram_tensor("out", (SEQ, D), F32, kind="ExternalOutput").ap())
    layer(nc, *args)
    r = _run(nc, [arrays], core_ids=[0])
    return r.results[0]["out"].reshape(1, SEQ, D)
```

```python
import numpy as np
import concourse.bass as bass
from concourse import mybir
from concourse.alu_op_type import AluOpType as ALU

F32 = mybir.dt.float32
F32R = mybir.dt.float32r
BF16 = mybir.dt.bfloat16
U32 = mybir.dt.uint32
ACT = mybir.ActivationFunctionType
AX = mybir.AxisListType

P = 128
SEQ, D = 256, 1024
NT = SEQ // P
KC = D // P
W = 1024
NS = 4
AHEAD = NS - 1

GH, GDK, GDV, GLR, GC = 4, D // 8, D // 4, 16, 64
NCH = SEQ // GC
GATE_NORM = 16.0
MH, HD = 8, D // 8
HALF = HD // 8
THETA = 500000.0
PH, NK, TOPK = 8, 128, 16
ALPHA = 2.0 ** 0.25
LN_EPS, RMS_EPS, NEG = 1e-5, 1e-6, -1e30
LOWEST = -3.0e38

CW = 512
ORDER = (("q_b", 1024), ("k_b", 1024), ("v_b", 1024), ("q_a", 512), ("k_a", 512),
         ("v_a", 1024), ("r_a", 1024), ("gate_b", 1024), ("gate_a", 1024))
WIDTH_IN = (("q_a", 512), ("k_a", 512), ("v_a", 1024), ("r_a", 1024), ("lr", 16), ("q_b", 1024),
            ("k_b", 1024), ("v_b", 1024), ("gate_a", 1024), ("gate_b", 1024))
AT = {}
_o = 0
for _n, _w in ORDER:
    AT[_n] = _o
    _o += _w
PW = _o
NCHUNK = PW // CW

TILES_IN = NCHUNK * 4
TILES_OUT = D // P
TILES_Q = PH * 2
TILES_U = NK
TILES_V = NK
T_OUT = TILES_IN
T_Q = T_OUT + TILES_OUT
T_U = T_Q + TILES_Q
T_V = T_U + TILES_U
T_END = T_V + TILES_V
DVE_COLS = 3 * W // 4
LOOPED = 6
HEADS = 4 * LOOPED
HEAD_STEPS = dict(transposes=0, qk_copy=1, scores=2, maxima=3, exp=4, probs=5, probs_copy=6,
                  output=7, normalize=8)
GLA_TP, GLA_QK, GLA_WITHIN, GLA_COPIES = 47, (48, 49), 51, 52
SILU, TIMES_NORM = 49, (51, 52)
GLA_DS, GLA_STATE, GLA_OUT, GLA_SSQ, GLA_VAR = (53, 54, 55), (54, 55, 56), (56, 57), (57, 58), (58, 59)
GLA_SQRT, GLA_RMS = (59, 60), (60, 61)
GATE_B, TIMES_GATE_B, GATE_A, Y_HALF = 56, (57, 58), 60, 61
TAIL = 3
BLK = 8
HOTS = 2
GB = 4
POOL_TOKS = 6
Y_LATE = 2
LAG = 3


class Tile:

    def __init__(self, first, i=None, per=0):
        self.first, self.i, self.per = first, i, per
        self.slot = first % NS

    def plus(self, n):
        return Tile(self.first + n, self.i, self.per)

    def number(self, add=0):
        return self.first + add if self.i is None else self.i * self.per + (self.first + add)

    def round(self, times=1, add=0):
        r = self.first // NS * times + add
        return r if self.i is None else self.i * (self.per // NS * times) + r


class Chain:

    def __init__(self, eng, sem, spare):
        self.eng, self.sem, self.spare = eng, sem, spare
        self.n, self.i, self.per = 0, None, 0

    def enter(self, i, per):
        self.i, self.per, self.start = i, per, self.n

    def leave(self, times):
        assert self.n - self.start == self.per, (self.n - self.start, self.per)
        self.n = self.start + times * self.per
        self.i = None

    def step(self, ins):
        ins.then_inc(self.sem, 1)
        self.n += 1

    def wait(self):
        if self.i is None:
            self.eng.wait_ge(self.sem, self.n)
        else:
            hold(self.eng, self.sem, self.i * self.per + self.n, self.spare)

    def do(self, ins):
        self.step(ins)
        self.wait()


def head_at(step, m):
    h, odd = divmod(m - HEADS - HEAD_STEPS[step], 2)
    return h if not odd and 0 <= h < MH else None


def hold(eng, sem, value, spare):
    eng.wait_ge(sem, value)
    eng.sem_inc(spare, 1)


def layer(nc, x, xT, w_lr, w_tiles_in, w_tiles_out, w_tiles_q, w_tiles_u, w_tiles_v, w_decay,
          b_decay, norm_g, keysT, ln1_g, ln1_b, ln2_g, ln2_b, cos, sin, out):
    start = (nc.sbuf_base + 63) // 64 * 64
    at = [start]

    def place(name, shape, dt=F32, alias=None):
        size = int(np.prod(shape[1:])) * (2 if dt is BF16 else 4)
        offset = at[0] if alias is None else alias
        t = nc.alloc_sbuf_tensor_at(name, shape, dt, offset=offset)
        if alias is None:
            at[0] += (size + 31) // 32 * 32
        return t

    ring_at = at[0]
    raw = place("raw", [P, NS, W])
    wlo = place("wlo", [P, NS, W], F32R, alias=ring_at)
    whi = place("whi", [P, NS, W], F32R)
    act_at = at[0]
    ahi = place("ahi", [P, KC, SEQ], F32R)
    alo = place("alo", [P, KC, SEQ], F32R)
    hot_size = BLK * P * 4
    hot_i = [place(f"hot_i{b}", [P, BLK, P], alias=act_at + b * hot_size) for b in range(2)]
    hot_j = [place(f"hot_j{b}", [P, BLK, P], alias=act_at + (2 + b) * hot_size) for b in range(2)]
    xt = place("xt", [P, NT, D])
    ident = place("ident", [P, P])
    keys = place("keys", [P, 2, NK])
    iota = place("iota", [P, P])
    stats = place("stats", [P, NT, 2, 6])
    mv = place("mv", [P, NT, 2])
    rstd = place("rstd", [P, NT])
    shift = place("shift", [P, 1])
    gate_warm = place("gate_warm", [P, 1])
    work_at = at[0]

    proj = place("proj", [P, NT, PW])
    xraw_at = at[0]
    xraw = place("xraw", [P, KC, SEQ])
    rope_t = place("rope_t", [P, 4, 2 * MH, HALF])
    state = place("state", [P, NCH - 1, GH, GDV], alias=xraw_at)
    g1b = place("g1b", [P, D])
    b1b = place("b1b", [P, D])
    qk = place("qk", [P, 2, 4 * P])
    masked = place("masked", [P, 2, 3 * P])
    probs = place("probs", [P, 2, 3 * P])
    probsT = place("probsT", [P, 2, 3 * P])
    causal = place("causal", [P, 3 * P])
    gla = [place(f"gla{n}", [P, GH, NCH, GC]) for n in range(5)]
    ksT = place("ksT", [P, NT, GH, P])
    attT = place("attT", [P, NT, GH, P])
    chunk_mask = place("chunk_mask", [P, P])
    scan_mask = place("scan_mask", [P, SEQ])
    rope_c = place("rope_c", [P, NT, HALF])
    rope_s = place("rope_s", [P, NT, HALF])
    gnorm = place("gnorm", [P, GDV])
    wlr = place("wlr", [P, KC, GLR])
    lrT = place("lrT", [GLR, SEQ])
    wdec = place("wdec", [GLR, GH * GDK])
    bdec = place("bdec", [P, GH])
    elast = place("elast", [P, GH, NCH])
    nmax = place("nmax", [P, 2, 2])
    rowsum = place("rowsum", [P, 4, 2])
    rrow = place("rrow", [P, 2, 2])
    ssq = place("ssq", [P, NT * GH])
    rrms = place("rrms", [P, NT * GH])
    square = place("square", [P, GDV])
    assert at[0] <= nc.sbuf_usable_end, at[0]

    at[0] = work_at
    H = place("H", [P, NK, SEQ])
    SC = NK - 2 * PH
    tail_at = at[0]
    sel = place("sel", [P, 3, NT * P])
    selT = place("selT", [P, 2, SEQ], BF16)
    gateT = place("gateT", [P, SEQ])
    iota8 = place("iota8", [P, P, BLK], BF16)
    gate8 = place("gate8", [P, HOTS, BLK])
    gdiff = place("gdiff", [P, NT * P])
    gsum = place("gsum", [P, NT * PH])
    hot_at = at[0]
    qs = place("qs", [P, 2, SEQ])
    s_cur = place("s_cur", [P, 2, NK])
    s_cut = place("s_cut", [P, 2, NK])
    top = place("top", [P, 2, TOPK])
    topi = place("topi", [P, 2, TOPK], U32)
    topf = place("topf", [P, 2, TOPK])
    cand = place("cand", [P, TOPK, TOPK])
    cand_cut = place("cand_cut", [P, TOPK, TOPK])
    best = place("best", [P, TOPK])
    pos = place("pos", [P, TOPK], U32)
    posab = place("posab", [P, 2, TOPK], U32)
    posf = place("posf", [P, 2, TOPK])
    hot16 = place("hot16", [P, 2, TOPK, TOPK])
    raw_ij = [place(f"raw_ij{b}", [P, 2, P, BLK], BF16, alias=hot_at + b * hot_size) for b in range(HOTS)]
    at[0] = max(at[0], hot_at + 2 * hot_size)
    assert at[0] <= nc.sbuf_usable_end, at[0]
    at[0] = tail_at
    hhi = place("hhi", [P, NS, SEQ], F32R)
    hlo = place("hlo", [P, NS, SEQ], F32R)
    g2b = place("g2b", [P, D])
    b2b = place("b2b", [P, D])
    assert at[0] <= nc.sbuf_usable_end, at[0]

    ps = nc.alloc_psum_tensor("ps", [P, 8, CW], F32)
    HID = (2, 3, 4, 5)
    Y_BANKS = (4, 5, 2, 3)
    DS_BANKS = ((4, 5), (6, 7), (4, 5))
    OUTB = (6, 7, 0, 1)

    names = ("raw_full0 raw_full1 raw_full2 raw_full3 in_xT0 in_xT1 in_xT2 in_xT3 in_lr in_x in_small "
             "in_ln1 in_ln2 hi_ready lo_ready_dve lo_ready_pool tiles_used evac_act evac_dve consts "
             "act_split_hi act_split_lo lr_done lr_copied z_done z_read roped mo_tp mo_qk mo_s mo_max "
             "mo_exp mo_pt mo_ptc mo_o mo_out gl_l gl_sum gl_exp gl_tp gl_qk gl_mm gl_ks gl_att gl_ds "
             "gl_state gl_o gl_ssq gl_var gl_sqrt gates_f gates_p gate_a_ready y_ready y_tp ln_var "
             "ln_shift ln_scaled ln_times_g ln_sqrt ln_done x1_tp ln_done0 out_ready0 q_copied sc_done "
             "sc_copied hid_used r_neg r_exp half_done sel_done sel_tp selT_done iota8_ready hot_ready "
             "j_scaled hots_wide g_done g_used first_hi first_lo w_hi w_lo out_ready stored dve_own "
             "pool_own act_own spare ").split()
    S = {n: nc.alloc_semaphore(n) for n in names}

    raw_full = [S[f"raw_full{n}"] for n in range(NS)]
    in_xT = [S[f"in_xT{n}"] for n in range(NS)]

    block = nc.Block()
    block.__enter__()

    def spare_hold(e, sem, value):
        hold(e, sem, value, S["spare"])

    @block.sync
    def _(sp):
        def load(tile, src, wait=True):
            if wait:
                sp.wait_ge(S["tiles_used"], tile.number(1 - NS))
            sp.dma_start(raw[:, tile.slot, :], src).then_inc(raw_full[tile.slot], 16)

        for k in range(NS):
            sp.dma_start(xraw[:, 2 * k:2 * k + 2, :], xT[:, 2 * k:2 * k + 2, :]).then_inc(in_xT[k], 16)
            load(Tile(k), w_tiles_in[k, :, :], wait=False)
        sp.dma_start(wlr[:, :, :], w_lr).then_inc(S["in_lr"], 16)
        for dst, src in ((wdec[:, :], w_decay), (bdec[:, :], b_decay), (rope_c[:, :, :], cos),
                         (rope_s[:, :, :], sin), (keys[:, :, :], keysT),
                         (gnorm[:, :], norm_g.to_broadcast([P, GDV]))):
            sp.dma_start(dst, src).then_inc(S["in_small"], 16)
        for first, n, src, skip in ((0, TILES_IN, w_tiles_in, 1), (T_OUT, TILES_OUT, w_tiles_out, 0),
                                    (T_Q, TILES_Q, w_tiles_q, 0), (T_U, TILES_U, w_tiles_u, 0),
                                    (T_V, TILES_V, w_tiles_v, 0)):
            with sp.Fori(skip, n // NS) as i:
                for k in range(NS):
                    load(Tile(first + k, i, NS), src[bass.ds(i * NS + k, 1), :, :].rearrange("a p n -> p (a n)"))
        for t, ready in enumerate(("out_ready0", "out_ready")):
            for half in range(2):
                cols = slice(half * CW, (half + 1) * CW)
                sp.wait_ge(S[ready], half + 1)
                sp.dma_start(out[t * P:(t + 1) * P, cols], xt[:, t, cols]).then_inc(S["stored"], 16)
        sp.wait_ge(S["stored"], 32 * NT)

    @block.gpsimd
    def _(pool):
        own = Chain(pool, S["pool_own"], S["spare"])

        def split_lo(tile):
            pool.wait_ge(S["hi_ready"], tile.number(1))
            pool.tensor_tensor(wlo[:, tile.slot, DVE_COLS:], raw[:, tile.slot, DVE_COLS:],
                               whi[:, tile.slot, DVE_COLS:].bitcast(F32), ALU.subtract)\
                .then_inc(S["lo_ready_pool"], 1)

        for m in range(AHEAD):
            split_lo(Tile(m))
        own.step(pool.memset(scan_mask[:, :], 1.0))
        own.step(pool.memset(ident[:, :], 0.0))
        own.step(pool.memset(causal[:, :], 0.0))
        own.step(pool.memset(chunk_mask[:, :], 1.0))
        own.step(pool.memset(attT[:, :, :, :], 0.0))
        own.do(pool.iota(iota[:, :], [[1, P]], base=0, channel_multiplier=0,
                         allow_small_or_imprecise_dtypes=True))
        own.step(pool.memset(scan_mask[:, :].rearrange("p (c t) -> p c t", t=GC)[:, :, 0:1], 0.0))
        own.step(pool.affine_select(out=ident[:, :], in_=ident[:, :], compare_op=ALU.not_equal, fill=1.0,
                                    base=0, pattern=[[-1, P]], channel_multiplier=1))
        for c in (0, 2):
            part = causal[:, c * P:(c + 1) * P]
            own.step(pool.affine_select(out=part, in_=part, compare_op=ALU.is_ge, fill=NEG, base=0,
                                        pattern=[[-1, P]], channel_multiplier=1))
        own.do(pool.affine_select(out=chunk_mask[:, :], in_=chunk_mask[:, :], compare_op=ALU.is_ge,
                                  fill=0.0, base=0, pattern=[[1, P]], channel_multiplier=-1))
        own.do(pool.memset(chunk_mask[0:GC, GC:P], 0.0))
        pool.sem_inc(S["consts"], 1)
        for m in range(4):
            split_lo(Tile(m + AHEAD))
        pool.dma_start(xt[:, :, :], x.rearrange("(t p) d -> p t d", p=P)).then_inc(S["in_x"], 16)
        pool.dma_start(g1b[:, :], ln1_g.to_broadcast([P, D])).then_inc(S["in_ln1"], 16)
        pool.dma_start(b1b[:, :], ln1_b.to_broadcast([P, D])).then_inc(S["in_ln1"], 16)
        with pool.Fori(1, LOOPED - 2) as i:
            for k in range(4):
                split_lo(Tile(k, i, 4).plus(AHEAD))

        def rope():
            pool.wait_ge(S["in_small"], 96)
            for t in range(NT):
                pool.wait_ge(S[("evac_act", "evac_dve")[t]], 4)
                heads = proj[:, t, 0:2 * D].rearrange("p (h d) -> p h d", d=HD)
                x1, x2 = heads[:, :, 0:HALF], heads[:, :, HALF:2 * HALF]
                c = rope_c[:, t, None, :].to_broadcast([P, 2 * MH, HALF])
                sn = rope_s[:, t, None, :].to_broadcast([P, 2 * MH, HALF])
                for n, (a, b) in enumerate(((x1, c), (x2, sn), (x1, sn), (x2, c))):
                    own.step(pool.tensor_tensor(rope_t[:, n, :, :], a, b, ALU.mult))
                    if n % 2:
                        yield
                own.wait()
                own.step(pool.tensor_tensor(x1, rope_t[:, 0, :, :], rope_t[:, 1, :, :], ALU.subtract))
                own.do(pool.tensor_tensor(x2, rope_t[:, 2, :, :], rope_t[:, 3, :, :], ALU.add))
                yield

        stretches = rope()
        for m in range(4 * (LOOPED - 2), 4 * LOOPED):
            split_lo(Tile(m + AHEAD))
            next(stretches, None)
        pool.sem_inc(S["roped"], 1)

        def ln_bias(b, done):
            for half in range(2):
                cols = slice(half * CW, (half + 1) * CW)
                pool.tensor_tensor(xt[:, 0, cols], xt[:, 0, cols], b[:, cols], ALU.add).then_inc(S[done], 1)

        for m in range(4 * LOOPED, T_Q - AHEAD):
            split_lo(Tile(m + AHEAD))
            for t in range(NT):
                if m == TIMES_NORM[t]:
                    pool.wait_ge(S["gates_f"], 1)
                    r = proj[:, t, AT["r_a"]:AT["r_a"] + D].rearrange("p (h v) -> p h v", v=GDV)
                    pool.tensor_tensor(r, r, gnorm[:, None, :].to_broadcast([P, GH, GDV]), ALU.mult)\
                        .then_inc(S["gates_p"], 1)
                if m == TIMES_GATE_B[t]:
                    pool.wait_ge(S["gates_f"], 2)
                    pool.wait_ge(S["mo_out"], MH)
                    yb = proj[:, t, 0:D]
                    pool.tensor_tensor(yb, yb, proj[:, t, AT["gate_b"]:AT["gate_b"] + D], ALU.mult)\
                        .then_inc(S["gates_p"], 1)
        for k in range(AHEAD):
            tile = Tile(T_Q + k)
            pool.wait_ge(S["hi_ready"], tile.number(1))
            pool.tensor_tensor(wlo[:, tile.slot, :], raw[:, tile.slot, :], whi[:, tile.slot, :].bitcast(F32),
                               ALU.subtract).then_inc(S["lo_ready_pool"], 1)
            if k == 0:
                pool.wait_ge(S["in_ln1"], 32)
                pool.wait_ge(S["ln_times_g"], 1)
                ln_bias(b1b, "ln_done0")
        for m in range(T_Q, T_Q + 4):
            split_lo(Tile(m + AHEAD))
        pool.wait_ge(S["ln_done"], 2)
        pool.tensor_copy(iota8[:, :, :], iota[:, :, None].to_broadcast([P, P, BLK])).then_inc(S["iota8_ready"], 1)
        with pool.Fori(1, (T_V - T_Q) // NS - 1) as i:
            for k in range(NS):
                split_lo(Tile(T_Q + k, i, NS).plus(AHEAD))
        for m in range(T_V - NS, T_V - 1):
            split_lo(Tile(m + AHEAD))

        def scale_j(n, b, i=None):
            if i is None:
                pool.wait_ge(S["hot_ready"], n + 1)
                if n >= HOTS:
                    pool.wait_ge(S["g_done"], n + 1 - HOTS)
                g = gateT[:, n * BLK:n * BLK + POOL_TOKS]
            else:
                pool.wait_ge(S["hot_ready"], i * GB + (b + 1))
                spare_hold(pool, S["g_done"], i * GB + (b + 1 - HOTS))
                g = gateT[:, bass.ds(i * (GB * BLK) + b * BLK, POOL_TOKS)]
            pool.tensor_tensor(hot_j[b % HOTS][:, 0:POOL_TOKS, :],
                               raw_ij[b % HOTS][:, 1, :, 0:POOL_TOKS].rearrange("p j n -> p n j"),
                               g[:, :, None].to_broadcast([P, POOL_TOKS, P]), ALU.mult)\
                .then_inc(S["j_scaled"], 1)

        pool.wait_ge(S["selT_done"], 1)
        pool.wait_ge(S["tiles_used"], T_V)
        for n in range(GB):
            scale_j(n, n)
            if n == 1:
                split_lo(Tile(T_V + AHEAD - 1))
        with pool.Fori(1, SEQ // BLK // GB) as i:
            for b in range(GB):
                scale_j(None, b, i)
        pool.wait_ge(S["g_used"], SEQ // BLK)
        pool.dma_start(g2b[:, :], ln2_g.to_broadcast([P, D])).then_inc(S["in_ln2"], 16)
        pool.dma_start(b2b[:, :], ln2_b.to_broadcast([P, D])).then_inc(S["in_ln2"], 16)
        with pool.Fori(0, TILES_V // NS - 1) as i:
            for k in range(NS):
                split_lo(Tile(T_V + k, i, NS).plus(AHEAD))
        split_lo(Tile(T_END - 1))
        pool.wait_ge(S["in_ln2"], 32)
        pool.wait_ge(S["ln_scaled"], 2)
        own.do(pool.tensor_tensor(xt[:, 0, :], xt[:, 0, :], g2b[:, :], ALU.mult))
        ln_bias(b2b, "out_ready0")

    @block.scalar
    def _(act):
        own = Chain(act, S["act_own"], S["spare"])

        def split_hi(tile):
            act.wait_ge(raw_full[tile.slot], tile.round(16, 16))
            act.activation(whi[:, tile.slot, :], raw[:, tile.slot, :], ACT.Copy)\
                .then_inc(S["hi_ready"], 1)

        def evac(c, bank, dst, reg):
            if reg:
                spare_hold(act, S["tiles_used"], c)
            else:
                act.wait_ge(S["tiles_used"], c)
            act.activation(dst, ps[:, bank, :], ACT.Copy).then_inc(S["evac_act"], 1)

        for k in range(NS):
            act.wait_ge(in_xT[k], 16)
            act.activation(ahi[:, 2 * k:2 * k + 2, :], xraw[:, 2 * k:2 * k + 2, :], ACT.Copy)\
                .then_inc(S["act_split_hi"], 1)
            if k < AHEAD:
                split_hi(Tile(k))
        for k in range(8):
            split_hi(Tile(k + AHEAD))
            if k % 4 == 3:
                evac(k + 1, 2 * (k // 4), proj[:, 0, k // 4 * CW:(k // 4 + 1) * CW], False)
            if k == 4:
                act.wait_ge(S["lr_done"], 1)
                act.activation(lrT[:, :], ps[0:GLR, 4, 0:SEQ], ACT.Copy).then_inc(S["lr_copied"], 1)
        with act.Fori(1, LOOPED // 2) as i:
            for k in range(8):
                tile = Tile(k, i, 8)
                split_hi(tile.plus(AHEAD))
                if k % 4 == 3:
                    evac(tile.number(1), 2 * (k // 4), proj[:, 0, bass.ds((i * 2 + k // 4) * CW, CW)], True)
        act.wait_ge(S["z_read"], 1)
        z, l = gla[0][:, :, :, :], gla[1][:, :, :, :]
        own.do(act.activation(l, z, ACT.Abs))
        own.do(act.activation(l, l, ACT.Exp, scale=-1.0))
        act.activation(l, l, ACT.Ln, bias=1.0).then_inc(S["gl_l"], 1)

        scale = HD ** -0.5
        def gla_banks(t, h):
            return ps[:, ((6, 7), (4, 5))[t][h // 2], (h % 2) * GDV:(h % 2 + 1) * GDV]

        def y_high(b):
            act.wait_ge(S["y_tp"], b + 1)
            act.activation(ahi[:, 2 * b:2 * b + 2, :].rearrange("p k n -> p (k n)"), ps[:, Y_BANKS[b], :],
                           ACT.Copy).then_inc(S["act_split_hi"], 1)

        def gate_a_rest():
            act.wait_ge(S["tiles_used"], T_OUT)
            for t in range(NT):
                act.activation(proj[:, t, AT["gate_a"] + CW:AT["gate_a"] + D], ps[:, 2 + t, :], ACT.Sigmoid)\
                    .then_inc(S["gate_a_ready"], 1)

        for m in range(4 * LOOPED, T_OUT):
            c, q = divmod(m, 4)
            h = head_at("exp", m)
            if h is not None:
                act.wait_ge(S["mo_max"], h + 1)
                for t, (a, b) in enumerate(((0, P), (P, 3 * P))):
                    act.activation(probs[:, h % 2, a:b], masked[:, h % 2, a:b], ACT.Exp,
                                   bias=nmax[:, h % 2, t:t + 1], scale=scale,
                                   accum_out=rowsum[:, h % 4, t:t + 1]).then_inc(S["mo_exp"], 1)
            h = head_at("qk_copy", m)
            if h is not None:
                act.wait_ge(S["mo_tp"], h + 1)
                act.activation(qk[:, h % 2, :], ps[:, 4, :], ACT.Copy).then_inc(S["mo_qk"], 1)
            if m == SILU:
                act.wait_ge(S["evac_dve"], 12)
                act.wait_ge(S["evac_act"], 12)
                v = proj[:, :, AT["r_a"]:AT["r_a"] + D]
                own.do(act.activation(v, v, ACT.Silu))
                act.sem_inc(S["gates_f"], 1)
            if m == GLA_COPIES:
                act.wait_ge(S["gl_mm"], 1)
                for t in range(NT):
                    act.activation(ksT[:, t, :, :].rearrange("p h d -> p (h d)"), ps[:, 4 + t, :], ACT.Copy)\
                        .then_inc(S["gl_ks"], 1)
            if m == GATE_B:
                act.wait_ge(S["evac_dve"], 14)
                act.wait_ge(S["evac_act"], 14)
                v = proj[:, :, AT["gate_b"]:AT["gate_b"] + D]
                own.do(act.activation(v, v, ACT.Sigmoid))
                act.sem_inc(S["gates_f"], 1)
            for t in range(NT):
                if m == GLA_SSQ[t]:
                    act.wait_ge(S["gl_o"], t + 1)
                    for h in range(GH):
                        own.do(act.activation(square[:, :], gla_banks(t, h), ACT.Square,
                                              accum_out=ssq[:, t * GH + h:t * GH + h + 1]))
                    act.sem_inc(S["gl_ssq"], 1)
                if m == GLA_SQRT[t]:
                    act.wait_ge(S["gl_var"], t + 1)
                    act.activation(rrms[:, t * GH:(t + 1) * GH], ssq[:, t * GH:(t + 1) * GH], ACT.Sqrt)\
                        .then_inc(S["gl_sqrt"], 1)
            if m == GATE_A:
                act.wait_ge(S["tiles_used"], T_OUT - 4)
                act.activation(proj[:, :, AT["gate_a"]:AT["gate_a"] + CW], ps[:, 0:2, :], ACT.Sigmoid)\
                    .then_inc(S["gate_a_ready"], 1)
            if m == T_OUT - 1:
                gate_a_rest()
                y_high(0)
                y_high(1)
            split_hi(Tile(m + AHEAD))
            if q == 3 and c < NCHUNK - 2:
                evac(m + 1, 2 * (c % 2), proj[:, 0, c * CW:(c + 1) * CW], False)
            if q == 3 and c == LOOPED + 1:
                act.wait_ge(S["gl_sum"], 1)
                own.do(act.activation(gla[1][:, :, :, :], gla[0][:, :, :, :], ACT.Exp,
                                      scale=-1.0 / GATE_NORM))
                own.step(act.activation(gla[0][:, :, :, :], gla[0][:, :, :, :], ACT.Exp,
                                        scale=1.0 / GATE_NORM))
            if q == 3 and c == LOOPED + 2:
                act.activation(gla[3][:, :, :, :], gla[2][:, :, :, :], ACT.Exp, scale=1.0 / GATE_NORM)
                act.activation(gla[4][:, :, :, :], gla[4][:, :, :, :], ACT.Exp, scale=1.0 / GATE_NORM)
                act.activation(elast[:, :, :, None], gla[2][:, :, :, GC - 1:GC], ACT.Exp,
                               scale=1.0 / GATE_NORM).then_inc(S["gl_exp"], 1)
        def ln_sqrt(n, t):
            act.wait_ge(S["ln_var"], NT * n + t + 1)
            act.activation(rstd[:, t:t + 1], rstd[:, t:t + 1], ACT.Sqrt).then_inc(S["ln_sqrt"], 1)

        def layer_norm(n, t):
            ln_sqrt(n, t)
            act.wait_ge(S["ln_shift"], n + 1)
            act.activation(xt[:, t, :], xt[:, t, :], ACT.Identity, bias=shift[:, :], scale=rstd[:, t:t + 1])\
                .then_inc(S["ln_scaled"], 1)

        for k in range(TILES_OUT):
            split_hi(Tile(T_OUT + k + AHEAD))
            if k == Y_LATE - 1:
                y_high(2)
                y_high(3)
                own.do(act.activation(gate_warm[:, :], ident[:, 0:1], ACT.Sqrt))
            if k == TILES_OUT - AHEAD:
                layer_norm(0, 0)
            if k == TILES_OUT - 1:
                ln_sqrt(0, 1)

        for t in range(NT):
            for j in range(2):
                act.wait_ge(S["x1_tp"], 2 * t + j + 1)
                act.activation(ahi[:, 4 * j:4 * j + 4, t * P:(t + 1) * P],
                               ps[:, 2 + 2 * t + j, :].rearrange("p (k n) -> p k n", n=P), ACT.Copy)\
                    .then_inc(S["act_split_hi"], 1)

        with act.Fori(0, TILES_Q // 4) as i:
            for k in range(4):
                tile = Tile(T_Q + k, i, 4)
                split_hi(tile.plus(AHEAD))
                act.wait_ge(S["tiles_used"], tile.number(1))
                act.activation(qs[:, k % 2, :], ps[:, HID[k], 0:SEQ], ACT.Copy).then_inc(S["q_copied"], 1)

        with act.Fori(0, NT * PH - 1) as i:
            for k in range(8):
                tile = Tile(T_U + k, i, 8)
                if k > 0:
                    split_hi(tile.plus(AHEAD))
                spare_hold(act, S["tiles_used"], tile.number(1))
                act.activation(H[:, bass.ds(i * 8 + k, 1), :].rearrange("p a n -> p (a n)"),
                               ps[:, HID[k % 4], 0:SEQ], ACT.Gelu).then_inc(S["hid_used"], 1)
                if k == 0:
                    split_hi(tile.plus(AHEAD))
        for m in range(T_V - 8, T_V):
            if m < T_V - 1:
                split_hi(Tile(m + AHEAD))
            act.wait_ge(S["tiles_used"], m + 1)
            act.activation(H[:, m - T_U, :], ps[:, HID[m % 4], 0:SEQ], ACT.Gelu).then_inc(S["hid_used"], 1)
            if m == T_V - 4:
                act.wait_ge(S["r_neg"], 1)
                act.activation(gdiff[:, :], gdiff[:, :], ACT.Exp).then_inc(S["r_exp"], 1)

        def scale_hots(n, b, i=None):
            if i is None:
                act.wait_ge(S["hot_ready"], n + 1)
                if n >= HOTS:
                    act.wait_ge(S["g_done"], n + 1 - HOTS)
                g = gateT[:, n * BLK + POOL_TOKS:(n + 1) * BLK]
            else:
                act.wait_ge(S["hot_ready"], i * GB + (b + 1))
                spare_hold(act, S["g_done"], i * GB + (b + 1 - HOTS))
                g = gateT[:, bass.ds(i * (GB * BLK) + (b * BLK + POOL_TOKS), BLK - POOL_TOKS)]
            act.activation(gate8[:, b % HOTS, 0:BLK - POOL_TOKS], g, ACT.Copy).then_inc(S["act_own"], 1)
            act.activation(hot_i[b % HOTS][:, :, :], raw_ij[b % HOTS][:, 0, :, :].rearrange("p i n -> p n i"), ACT.Copy)
            act.wait_ge(S["act_own"], own.n + n + 1 if i is None else i * GB + (own.n + b + 1))
            for k in range(POOL_TOKS, BLK):
                last = act.activation(hot_j[b % HOTS][:, k, :], raw_ij[b % HOTS][:, 1, :, k], ACT.Copy,
                                      scale=gate8[:, b % HOTS, k - POOL_TOKS:k - POOL_TOKS + 1])
            last.then_inc(S["hots_wide"], 1)

        act.wait_ge(S["selT_done"], 1)
        act.wait_ge(S["tiles_used"], T_V)
        for n in range(GB):
            scale_hots(n, n)
            if n == 1:
                split_hi(Tile(T_V + AHEAD - 1))
        with act.Fori(1, SEQ // BLK // GB) as i:
            for b in range(GB):
                scale_hots(None, b, i)

        def split_h(tile):
            n = tile.number(-T_V)
            if tile.i is None:
                if tile.first - T_V >= NS:
                    act.wait_ge(S["tiles_used"], tile.number(1 - NS))
            else:
                spare_hold(act, S["tiles_used"], tile.number(1 - NS))
            src = H[:, n, :] if tile.i is None else H[:, bass.ds(n, 1), :].rearrange("p a n -> p (a n)")
            act.activation(hhi[:, tile.slot, :], src, ACT.Copy).then_inc(S["w_hi"], 1)

        for t, blocks in enumerate((SEQ // BLK // NT, SEQ // BLK)):
            act.wait_ge(S["g_used"], blocks)
            for k in range(AHEAD):
                act.activation(hhi[:, (T_V + k) % NS, t * P:(t + 1) * P], H[:, k, t * P:(t + 1) * P], ACT.Copy)\
                    .then_inc(S[("first_hi", "w_hi")[t]], 1)
        for k in range(4):
            split_h(Tile(T_V + k + AHEAD))
            split_hi(Tile(T_V + k + AHEAD))
        with act.Fori(1, TILES_V // 4 - 1) as i:
            for k in range(4):
                tile = Tile(T_V + k, i, 4).plus(AHEAD)
                split_h(tile)
                split_hi(tile)
        for m in range(T_END - 4 + AHEAD, T_END):
            split_h(Tile(m))
            split_hi(Tile(m))
        own.n += SEQ // BLK
        own.do(act.activation(gate_warm[:, :], ident[:, 0:1], ACT.Sqrt))
        layer_norm(1, 0)
        ln_sqrt(1, 1)

    @block.vector
    def _(dve):
        own = Chain(dve, S["dve_own"], S["spare"])

        def split_lo(tile):
            dve.wait_ge(S["hi_ready"], tile.number(1))
            dve.tensor_tensor(wlo[:, tile.slot, 0:DVE_COLS], raw[:, tile.slot, 0:DVE_COLS],
                              whi[:, tile.slot, 0:DVE_COLS].bitcast(F32), ALU.subtract)\
                .then_inc(S["lo_ready_dve"], 1)

        for k in range(NS):
            dve.wait_ge(S["act_split_hi"], k + 1)
            dve.tensor_tensor(alo[:, 2 * k:2 * k + 2, :], xraw[:, 2 * k:2 * k + 2, :],
                              ahi[:, 2 * k:2 * k + 2, :].bitcast(F32), ALU.subtract)\
                .then_inc(S["act_split_lo"], 1)
            if k < AHEAD:
                split_lo(Tile(k))
        for k in range(8):
            split_lo(Tile(k + AHEAD))
            if k % 4 == 3:
                dve.wait_ge(S["tiles_used"], k + 1)
                dve.tensor_copy(proj[:, 1, k // 4 * CW:(k // 4 + 1) * CW], ps[:, 2 * (k // 4) + 1, :])\
                    .then_inc(S["evac_dve"], 1)
        dve.wait_ge(S["in_small"], 96)
        dve.wait_ge(S["z_done"], 1)
        for h in range(GH):
            own.step(dve.tensor_scalar(gla[0][:, h, :, :].rearrange("p c t -> p (c t)"),
                                       ps[:, 4 + h // 2, (h % 2) * SEQ:(h % 2 + 1) * SEQ],
                                       bdec[:, h:h + 1], None, ALU.add))
        own.wait()
        dve.sem_inc(S["z_read"], 1)
        with dve.Fori(1, LOOPED // 2) as i:
            for k in range(8):
                tile = Tile(k, i, 8)
                split_lo(tile.plus(AHEAD))
                if k % 4 == 3:
                    spare_hold(dve, S["tiles_used"], tile.number(1))
                    dve.tensor_copy(proj[:, 1, bass.ds((i * 2 + k // 4) * CW, CW)],
                                    ps[:, 2 * (k // 4) + 1, :]).then_inc(S["evac_dve"], 1)

        def decay_sums():
            dve.wait_ge(S["gl_l"], 1)
            own.do(dve.scalar_tensor_tensor(out=gla[1][:, :, :, :].rearrange("p h c t -> p (h c t)"),
                                            in0=gla[0][:, :, :, :].rearrange("p h c t -> p (h c t)"), scalar=0.0,
                                            in1=gla[1][:, :, :, :].rearrange("p h c t -> p (h c t)"),
                                            op0=ALU.min, op1=ALU.subtract))
            yield
            dve.wait_ge(S["consts"], 1)
            for h in range(GH):
                own.step(dve.tensor_tensor_scan(gla[2][:, h, :, :].rearrange("p c t -> p (c t)"), scan_mask[:, :],
                                                gla[1][:, h, :, :].rearrange("p c t -> p (c t)"), 0.0,
                                                ALU.mult, ALU.add))
            own.wait()
            yield

            def rows(a):
                return a.rearrange("p h c t -> p (h c) t")

            b_all = rows(gla[2][:, :, :, :])
            own.step(dve.tensor_tensor(rows(gla[0][:, :, :, :]), b_all,
                                       b_all[:, :, GC // 2 - 1:GC // 2].to_broadcast([P, GH * NCH, GC]),
                                       ALU.subtract))
            own.do(dve.tensor_tensor(rows(gla[4][:, :, :, :]),
                                     b_all[:, :, GC - 1:GC].to_broadcast([P, GH * NCH, GC]), b_all,
                                     ALU.subtract))
            dve.sem_inc(S["gl_sum"], 1)

        scale = HD ** -0.5

        def normalize(h):
            dve.wait_ge(S["mo_exp"], 2 * h + 2)
            own.step(dve.reciprocal(rrow[:, h % 2, :], rowsum[:, h % 4, :]))
            dve.wait_ge(S["mo_o"], h + 1)
            own.wait()
            for t in range(NT):
                last = dve.tensor_scalar(proj[:, t, h * HD:(h + 1) * HD], ps[:, 7, t * P:(t + 1) * P],
                                         rrow[:, h % 2, t:t + 1], None, ALU.mult)
            last.then_inc(S["mo_out"], 1)

        sums = decay_sums()
        def gla_banks(t, h):
            return ps[:, ((6, 7), (4, 5))[t][h // 2], (h % 2) * GDV:(h % 2 + 1) * GDV]

        def y_low(b):
            dve.wait_ge(S["act_split_hi"], NS + b + 1)
            dve.tensor_tensor(alo[:, 2 * b:2 * b + 2, :].rearrange("p k n -> p (k n)"), ps[:, Y_BANKS[b], :],
                              ahi[:, 2 * b:2 * b + 2, :].rearrange("p k n -> p (k n)").bitcast(F32),
                              ALU.subtract).then_inc(S["act_split_lo"], 1)

        def y(t, half):
            z = proj[:, t, AT["r_a"] + half * CW:AT["r_a"] + (half + 1) * CW]
            yb = proj[:, t, half * CW:(half + 1) * CW]
            own.do(dve.tensor_tensor(z, z, proj[:, t, AT["gate_a"] + half * CW:AT["gate_a"] + (half + 1) * CW],
                                     ALU.mult))
            dve.tensor_tensor(yb, yb, z, ALU.add).then_inc(S["y_ready"], 1)

        for m in range(4 * LOOPED, T_OUT):
            c, q = divmod(m, 4)
            h = head_at("normalize", m)
            if h is not None:
                normalize(h)
            h = head_at("maxima", m)
            if h is not None:
                dve.wait_ge(S["mo_s"], h + 1)
                own.do(dve.tensor_tensor(masked[:, h % 2, :], ps[:, 5, 0:3 * P], causal[:, :], ALU.add))
                own.step(dve.tensor_reduce(nmax[:, h % 2, 0:1], masked[:, h % 2, 0:P], AX.X, ALU.max))
                own.do(dve.tensor_reduce(nmax[:, h % 2, 1:2], masked[:, h % 2, P:3 * P], AX.X, ALU.max))
                dve.tensor_scalar(nmax[:, h % 2, :], nmax[:, h % 2, :], -scale, None, ALU.mult)\
                    .then_inc(S["mo_max"], 1)
            h = head_at("probs_copy", m)
            if h is not None:
                dve.wait_ge(S["mo_pt"], h + 1)
                dve.tensor_copy(probsT[:, h % 2, :], ps[:, 6, 0:3 * P]).then_inc(S["mo_ptc"], 1)
            for b in range(2):
                if m == GLA_QK[b]:
                    dve.wait_ge(S["gl_exp"], 1)
                    dve.wait_ge(S["gl_tp"], 1)

                    def part(n):
                        return gla[n][:, 2 * b:2 * b + 2, :, :].rearrange("p h c t -> p (h c t)")
                    for n in (0, 3):
                        dve.scalar_tensor_tensor(out=part(n), in0=ps[:, 4 + b, :], scalar=GDK ** -0.5,
                                                 in1=part(n), op0=ALU.mult, op1=ALU.mult)
                    for n in (1, 4):
                        last = dve.tensor_tensor(part(n), ps[:, 6 + b, :], part(n), ALU.mult)
                    last.then_inc(S["gl_qk"], 1)
            if m == GLA_COPIES:
                dve.wait_ge(S["gl_mm"], 1)
                for t in range(NT):
                    last = dve.copy_predicated(attT[:, t, :, :],
                                               chunk_mask[:, None, :].to_broadcast([P, GH, P]).bitcast(U32),
                                               ps[:, 6 + t, :].rearrange("p (h c) -> p h c", c=P))
                last.then_inc(S["gl_att"], 1)
            if m == GLA_STATE[0]:
                dve.wait_ge(S["gl_ds"], 1)
                own.do(dve.tensor_copy(state[:, 0, :, :].rearrange("p (b h) v -> p b (h v)", b=2), ps[:, 4:6, :]))
                dve.sem_inc(S["gl_state"], 1)
            for n in range(1, NCH - 1):
                if m == GLA_STATE[n]:
                    dve.wait_ge(S["gl_ds"], n + 1)
                    for h in range(GH):
                        bank = DS_BANKS[n][h // 2]
                        own.step(dve.scalar_tensor_tensor(out=state[:, n, h, :], in0=state[:, n - 1, h, :],
                                                          scalar=elast[:, h, n:n + 1],
                                                          in1=ps[:, bank, (h % 2) * GDV:(h % 2 + 1) * GDV],
                                                          op0=ALU.mult, op1=ALU.add))
                    own.wait()
                    dve.sem_inc(S["gl_state"], 1)
            for t in range(NT):
                four = slice(t * GH, (t + 1) * GH)
                if m == GLA_VAR[t]:
                    dve.wait_ge(S["gl_ssq"], t + 1)
                    dve.tensor_scalar(ssq[:, four], ssq[:, four], 1.0 / GDV, RMS_EPS, ALU.mult, ALU.add)\
                        .then_inc(S["gl_var"], 1)
                if m == GLA_RMS[t]:
                    dve.wait_ge(S["gl_sqrt"], t + 1)
                    own.do(dve.reciprocal(rrms[:, four], rrms[:, four]))
                    dve.wait_ge(S["gates_p"], t + 1)
                    for h in range(GH):
                        f = proj[:, t, AT["r_a"] + h * GDV:AT["r_a"] + (h + 1) * GDV]
                        own.step(dve.scalar_tensor_tensor(out=f, in0=gla_banks(t, h),
                                                          scalar=rrms[:, t * GH + h:t * GH + h + 1], in1=f,
                                                          op0=ALU.mult, op1=ALU.mult))
                    own.wait()
            if m == Y_HALF:
                dve.wait_ge(S["gates_p"], 2 * NT)
                dve.wait_ge(S["gate_a_ready"], 1)
                for t in range(NT):
                    y(t, 0)
            if m == T_OUT - 1:
                y_low(0)
            split_lo(Tile(m + AHEAD))
            if c == LOOPED + 1 or c == LOOPED and q == 3:
                next(sums, None)
            if q == 3 and c < NCHUNK - 2:
                dve.wait_ge(S["tiles_used"], m + 1)
                dve.tensor_copy(proj[:, 1, c * CW:(c + 1) * CW], ps[:, 2 * (c % 2) + 1, :])\
                    .then_inc(S["evac_dve"], 1)
        for t in range(NT):
            dve.wait_ge(S["gate_a_ready"], t + 2)
            y(t, 1)
        y_low(1)
        for k in range(TILES_OUT - AHEAD):
            split_lo(Tile(T_OUT + k + AHEAD))
            if k == Y_LATE - 1:
                y_low(2)
                y_low(3)
        def layer_norm(banks, n, g, b, tiles, done):
            def total(t):
                for half in range(2):
                    xs = xt[:, t, half * CW:(half + 1) * CW]
                    own.step(dve.scalar_tensor_tensor(out=xs, in0=xs, scalar=ALPHA, in1=ps[:, banks[2 * t + half], :],
                                                      op0=ALU.mult, op1=ALU.add))
                own.wait()
                for half in range(2):
                    own.step(dve.bn_stats(stats[:, t, half, :], xt[:, t, half * CW:(half + 1) * CW]))
                own.wait()
                own.do(dve.bn_aggr(mv[:, t, :], stats[:, t, :, :].rearrange("p a b -> p (a b)")))
                dve.tensor_scalar(rstd[:, t:t + 1], mv[:, t, 1:2], LN_EPS, None, ALU.add)\
                    .then_inc(S["ln_var"], 1)

            def apply(t):
                dve.wait_ge(S["ln_sqrt"], NT * n + t + 1)
                own.do(dve.reciprocal(rstd[:, t:t + 1], rstd[:, t:t + 1]))
                halves = [slice(half * CW, (half + 1) * CW) for half in range(2)]
                for cols in halves:
                    own.step(dve.scalar_tensor_tensor(out=xt[:, t, cols], in0=xt[:, t, cols], scalar=mv[:, t, 0:1],
                                                      in1=g[:, cols], op0=ALU.subtract, op1=ALU.mult))
                own.wait()
                for cols in halves:
                    dve.scalar_tensor_tensor(out=xt[:, t, cols], in0=xt[:, t, cols], scalar=rstd[:, t:t + 1],
                                             in1=b[:, cols], op0=ALU.mult, op1=ALU.add).then_inc(S[done], 1)

            dve.wait_ge(S["half_done"], n + 1)
            total(0)
            dve.wait_ge(S["ln_sqrt"], NT * n + 1)
            own.do(dve.reciprocal(rstd[:, 0:1], rstd[:, 0:1]))
            dve.scalar_tensor_tensor(out=shift[:, :], in0=mv[:, 0, 0:1], scalar=-1.0, in1=rstd[:, 0:1],
                                     op0=ALU.mult, op1=ALU.mult).then_inc(S["ln_shift"], 1)
            if n == 0:
                dve.wait_ge(S["ln_scaled"], 1)
                dve.tensor_tensor(xt[:, 0, :], xt[:, 0, :], g, ALU.mult).then_inc(S["ln_times_g"], 1)
            dve.wait_ge(S["tiles_used"], tiles)
            if n == 0:
                dve.sem_inc(S["lo_ready_dve"], AHEAD)
            total(1)
            if n == 0:
                x1_low(0)
            apply(1)

        def x1_low(t):
            for j in range(2):
                dve.wait_ge(S["act_split_hi"], NS + 4 + 2 * t + j + 1)
                part = (slice(None), slice(4 * j, 4 * j + 4), slice(t * P, (t + 1) * P))
                dve.tensor_tensor(alo[part], ps[:, 2 + 2 * t + j, :].rearrange("p (k n) -> p k n", n=P),
                                  ahi[part].bitcast(F32), ALU.subtract).then_inc(S["act_split_lo"], 1)

        dve.wait_ge(S["in_x"], 16)
        dve.wait_ge(S["in_ln1"], 32)
        layer_norm(OUTB, 0, g1b[:, :], b1b[:, :], T_Q, "ln_done")
        x1_low(1)

        with dve.Fori(0, TILES_Q // 4) as i:
            for k in range(4):
                tile = Tile(T_Q + k, i, 4)
                split_lo(tile.plus(AHEAD))
                spare_hold(dve, S["sc_done"], i * 4 + (k + 1))
                dst = H[:, SC:NK, :].rearrange("p (t h) n -> p t (h n)", t=NT)
                dve.tensor_copy(dst[:, :, bass.ds(i * (4 * NK) + k * NK, NK)],
                                ps[:, k % 2, 0:2 * NK].rearrange("p (t k) -> p t k", t=NT))\
                    .then_inc(S["sc_copied"], 1)

        def routing(i):
            dve_max, dve_idx = dve.max, dve.max_index
            own.do(dve.tensor_copy(s_cur[:, :, :].rearrange("p a k -> p (a k)"),
                                   H[:, bass.ds(i + SC, 1), :].rearrange("p a n -> p (a n)")))
            for a in range(2):
                own.do(dve_max(top[:, a, 0:8], s_cur[:, a, :]))
                own.step(dve_idx(topi[:, a, 0:8], top[:, a, 0:8], s_cur[:, a, :]))
                own.do(dve.match_replace(s_cut[:, a, :], top[:, a, 0:8], s_cur[:, a, :], LOWEST))
                yield
                own.do(dve_max(top[:, a, 8:16], s_cut[:, a, :]))
                own.do(dve_idx(topi[:, a, 8:16], top[:, a, 8:16], s_cut[:, a, :]))
            yield
            own.step(dve.tensor_copy(topf[:, :, :], topi[:, :, :]))
            own.do(dve.tensor_tensor(cand[:, :, :], top[:, 0, :, None].to_broadcast([P, TOPK, TOPK]),
                                     top[:, 1, None, :].to_broadcast([P, TOPK, TOPK]), ALU.add))
            c1, c2 = (x[:, :, :].rearrange("p a b -> p (a b)") for x in (cand, cand_cut))
            own.do(dve_max(best[:, 0:8], c1))
            own.step(dve_idx(pos[:, 0:8], best[:, 0:8], c1))
            own.do(dve.match_replace(c2, best[:, 0:8], c1, LOWEST))
            yield
            own.do(dve_max(best[:, 8:16], c2))
            own.step(dve.tensor_copy(sel[:, 2, bass.ds(i * TOPK, TOPK)], best[:, :]))
            own.do(dve_idx(pos[:, 8:16], best[:, 8:16], c2))
            own.step(dve.tensor_scalar(posab[:, 0, :], pos[:, :], 4, None, ALU.logical_shift_right))
            own.do(dve.tensor_scalar(posab[:, 1, :], pos[:, :], TOPK - 1, None, ALU.bitwise_and))
            own.do(dve.tensor_copy(posf[:, :, :], posab[:, :, :]))
            yield
            for a in range(2):
                own.step(dve.tensor_tensor(hot16[:, a, :, :], posf[:, a, :, None].to_broadcast([P, TOPK, TOPK]),
                                           iota[:, None, 0:TOPK].to_broadcast([P, TOPK, TOPK]), ALU.is_equal))
            own.wait()
            for a in range(2):
                own.step(dve.tensor_tensor(hot16[:, a, :, :], hot16[:, a, :, :],
                                           topf[:, a, None, :].to_broadcast([P, TOPK, TOPK]), ALU.mult))
            own.wait()
            yield
            for a in range(2):
                own.step(dve.tensor_reduce(sel[:, a, bass.ds(i * TOPK, TOPK)], hot16[:, a, :, :], AX.X, ALU.add))
            own.wait()
            yield

        spare_hold(dve, S["sc_copied"], TILES_Q)
        with dve.Fori(0, NT * PH - 1) as i:
            own.enter(i, 28)
            steps = routing(i)
            for k in range(8):
                split_lo(Tile(T_U + k, i, 8).plus(AHEAD))
                if k > 0:
                    next(steps, None)
                if k == 7:
                    for _ in steps:
                        pass
            own.leave(NT * PH - 1)

        def by_head(a):
            return a.rearrange("p (u k) -> p u k", k=TOPK)

        vals = by_head(sel[:, 2, :])

        def hots(n, b, i=None):
            if i is not None:
                spare_hold(dve, S["hots_wide"], i * GB + (b + 1 - HOTS))
                spare_hold(dve, S["j_scaled"], i * GB + (b + 1 - HOTS))
            elif n >= HOTS:
                dve.wait_ge(S["hots_wide"], n + 1 - HOTS)
                dve.wait_ge(S["j_scaled"], n + 1 - HOTS)
            toks = slice(n * BLK, (n + 1) * BLK) if i is None else bass.ds(i * (GB * BLK) + b * BLK, BLK)
            dve.tensor_tensor(raw_ij[b % HOTS][:, :, :, :], iota8[:, None, :, :].to_broadcast([P, 2, P, BLK]),
                              selT[:, :, toks][:, :, None, :].to_broadcast([P, 2, P, BLK]), ALU.is_equal)\
                .then_inc(S["hot_ready"], 1)

        def into_h(n, b, i=None):
            if i is None:
                dve.wait_ge(S["g_done"], n + 1)
            else:
                spare_hold(dve, S["g_done"], i * GB + (b + 1))
            toks = slice(n * BLK, (n + 1) * BLK) if i is None else bass.ds(i * (GB * BLK) + b * BLK, BLK)
            hv = H[:, :, toks].rearrange("p i n -> p n i")
            g = ps[:, 2 * (b % GB):2 * (b % GB) + 2, :].rearrange("p b (n i) -> p (b n) i", i=NK)
            dve.tensor_tensor(hv, hv, g, ALU.mult).then_inc(S["g_used"], 1)

        steps = routing(NT * PH - 1)
        for k in range(5):
            split_lo(Tile(T_V - 8 + k).plus(AHEAD))
            if k < 4:
                next(steps, None)
                next(steps, None)
            if k == 3:
                for _ in steps:
                    pass
                own.do(dve.tensor_tensor(by_head(gdiff[:, :]), vals,
                                         vals[:, :, 0:1].to_broadcast([P, NT * PH, TOPK]), ALU.subtract))
                dve.sem_inc(S["r_neg"], 1)
            if k == 4:
                dve.wait_ge(S["r_exp"], 1)
                own.do(dve.tensor_reduce(gsum[:, :], by_head(gdiff[:, :]), AX.X, ALU.add))
                own.do(dve.reciprocal(gsum[:, :], gsum[:, :]))
                own.do(dve.tensor_tensor(vals, by_head(gdiff[:, :]),
                                         gsum[:, :, None].to_broadcast([P, NT * PH, TOPK]), ALU.mult))
                dve.sem_inc(S["sel_done"], 1)
        dve.wait_ge(S["sel_tp"], 1)
        own.step(dve.tensor_copy(selT[:, :, :].rearrange("p a n -> p (a n)"), ps[:, 6, :]))
        own.do(dve.tensor_copy(gateT[:, :], ps[:, 7, 0:SEQ]))
        dve.sem_inc(S["selT_done"], 1)
        dve.wait_ge(S["iota8_ready"], 1)
        hots(0, 0)
        hots(1, 1)
        split_lo(Tile(T_V))
        hots(2, 2)
        split_lo(Tile(T_V + 1))
        split_lo(Tile(T_V + 2))
        def first_lo(t):
            for k in range(AHEAD):
                dve.wait_ge(S[("first_hi", "w_hi")[t]], k + 1)
                slot, tok = (T_V + k) % NS, slice(t * P, (t + 1) * P)
                dve.tensor_tensor(hlo[:, slot, tok], H[:, k, tok], hhi[:, slot, tok].bitcast(F32), ALU.subtract)\
                    .then_inc(S[("first_lo", "w_lo")[t]], 1)

        dve.wait_ge(S["hid_used"], TILES_U)
        into_h(0, 0)
        with dve.Fori(0, SEQ // BLK // GB - 1) as i:
            for b in range(GB):
                hots(b + LAG, b + LAG, i)
                into_h(b + 1, b + 1, i)
        hots(SEQ // BLK - 1, GB - 1)
        into_h(SEQ // BLK - 3, 1)
        into_h(SEQ // BLK - 2, 2)
        dve.wait_ge(S["j_scaled"], SEQ // BLK)
        dve.wait_ge(S["hots_wide"], SEQ // BLK)
        first_lo(0)
        into_h(SEQ // BLK - 1, 3)
        first_lo(1)

        def split_h(tile):
            n = tile.number(-T_V)
            if tile.i is None:
                dve.wait_ge(S["w_hi"], n + 1)
                src = H[:, n, :]
            else:
                dve.wait_ge(S["w_hi"], tile.number(1 - T_V))
                src = H[:, bass.ds(n, 1), :].rearrange("p a n -> p (a n)")
            dve.tensor_tensor(hlo[:, tile.slot, :], src, hhi[:, tile.slot, :].bitcast(F32), ALU.subtract)\
                .then_inc(S["w_lo"], 1)

        for k in range(4):
            split_h(Tile(T_V + k + AHEAD))
            split_lo(Tile(T_V + k + AHEAD))
        with dve.Fori(1, TILES_V // 4 - 1) as i:
            for k in range(4):
                tile = Tile(T_V + k, i, 4).plus(AHEAD)
                split_h(tile)
                split_lo(tile)
        for m in range(T_END - 4 + AHEAD, T_END):
            split_h(Tile(m))
            split_lo(Tile(m))
        dve.wait_ge(S["in_ln2"], 32)
        layer_norm((0, 1, 2, 3), 1, g2b[:, :], b2b[:, :], T_END, "out_ready")

    @block.tensor
    def _(pe):
        def tile_ready(tile):
            pe.wait_ge(S["lo_ready_dve"], tile.number(1))
            pe.wait_ge(S["lo_ready_pool"], tile.number(1))

        def three(out, ah, al, bh, bl, start, stop):
            pe.matmul(out, ah, bh, start=start, stop=False)
            pe.matmul(out, ah, bl, start=False, stop=False)
            return pe.matmul(out, al, bh, start=False, stop=stop)

        def project(tile, c2, q):
            tile_ready(tile)
            for t in range(NT):
                for kk in range(2):
                    k = 2 * q + kk
                    cols = slice(kk * CW, (kk + 1) * CW)
                    last = three(ps[:, 2 * c2 + t, :], ahi[:, k, t * P:(t + 1) * P], alo[:, k, t * P:(t + 1) * P],
                                 whi[:, tile.slot, cols], wlo[:, tile.slot, cols], k == 0, k == KC - 1)
            last.then_inc(S["tiles_used"], 1)

        for q in range(4):
            pe.wait_ge(S["act_split_lo"], q + 1)
            project(Tile(q), 0, q)
        pe.wait_ge(S["in_lr"], 16)
        for c in range(KC):
            last = pe.matmul(ps[0:GLR, 4, 0:SEQ], wlr[:, c, :], xraw[:, c, :], start=c == 0, stop=c == KC - 1)
        last.then_inc(S["lr_done"], 1)
        for q in range(4):
            project(Tile(4 + q), 1, q)
        pe.wait_ge(S["in_small"], 96)
        pe.wait_ge(S["lr_copied"], 1)
        for h in range(GH):
            last = pe.matmul(ps[:, 4 + h // 2, (h % 2) * SEQ:(h % 2 + 1) * SEQ],
                             wdec[:, h * GDK:(h + 1) * GDK], lrT[:, :], start=True, stop=True)
        last.then_inc(S["z_done"], 1)
        with pe.Fori(1, LOOPED // 2) as i:
            for c in range(2):
                pe.wait_ge(S["evac_act"], i * 2 + (c - 1))
                pe.wait_ge(S["evac_dve"], i * 2 + (c - 1))
                for q in range(4):
                    project(Tile(4 * c + q, i, 8), c, q)

        def turn(dst, src):
            return pe.transpose(dst, src, ident[:, :])

        def head_transposes(h):
            pe.wait_ge(S["roped"], 1)
            if h > 0:
                pe.wait_ge(S["mo_qk"], h)
            for n, part in enumerate((0, D)):
                for t in range(NT):
                    last = turn(ps[:, 4, (2 * n + t) * P:(2 * n + t + 1) * P],
                                proj[:, t, part + h * HD:part + (h + 1) * HD])
            last.then_inc(S["mo_tp"], 1)

        def head_scores(h):
            pe.wait_ge(S["mo_qk"], h + 1)
            if h > 0:
                pe.wait_ge(S["mo_max"], h)
            a = qk[:, h % 2, :]
            pe.matmul(ps[:, 5, 0:P], a[:, 0:P], a[:, 2 * P:3 * P], start=True, stop=True)
            pe.matmul(ps[:, 5, P:3 * P], a[:, P:2 * P], a[:, 2 * P:4 * P], start=True, stop=True)\
                .then_inc(S["mo_s"], 1)

        def head_probs(h):
            pe.wait_ge(S["mo_exp"], 2 * h + 2)
            if h > 0:
                pe.wait_ge(S["mo_ptc"], h)
            for n in range(3):
                last = turn(ps[:, 6, n * P:(n + 1) * P], probs[:, h % 2, n * P:(n + 1) * P])
            last.then_inc(S["mo_pt"], 1)

        def head_output(h):
            pe.wait_ge(S["mo_ptc"], h + 1)
            if h > 0:
                pe.wait_ge(S["mo_out"], h)
            v = AT["v_b"] + h * HD
            pt = probsT[:, h % 2, :]
            pe.matmul(ps[:, 7, 0:P], pt[:, 0:P], proj[:, 0, v:v + HD], start=True, stop=True)
            pe.matmul(ps[:, 7, P:2 * P], pt[:, P:2 * P], proj[:, 0, v:v + HD], start=True, stop=False)
            pe.matmul(ps[:, 7, P:2 * P], pt[:, 2 * P:3 * P], proj[:, 1, v:v + HD], start=False, stop=True)\
                .then_inc(S["mo_o"], 1)

        def gla_transposes():
            pe.wait_ge(S["mo_out"], MH)
            for n, name in enumerate(("q_a", "k_a")):
                for h in range(GH):
                    for t in range(NT):
                        col = ((h % 2) * NT + t) * P
                        last = turn(ps[:, 4 + 2 * n + h // 2, col:col + P],
                                    proj[:, t, AT[name] + h * GDK:AT[name] + (h + 1) * GDK])
            last.then_inc(S["gl_tp"], 1)

        def flat(n, h):
            return gla[n][:, h, :, :].rearrange("p c t -> p (c t)")

        def gla_within():
            pe.wait_ge(S["gl_qk"], 2)
            for t in range(NT):
                for h in range(GH):
                    turn(ps[:, 4 + t, h * P:(h + 1) * P], flat(4, h)[:, t * P:(t + 1) * P])
            for t in range(NT):
                for h in range(GH):
                    last = pe.matmul(ps[:, 6 + t, h * P:(h + 1) * P], flat(1, h)[:, t * P:(t + 1) * P],
                                     flat(0, h)[:, t * P:(t + 1) * P], start=True, stop=True)
            last.then_inc(S["gl_mm"], 1)

        def gla_increment(c):
            if c == 0:
                pe.wait_ge(S["gl_ks"], 2)
            elif c == 1:
                pe.wait_ge(S["gl_att"], 1)
            else:
                pe.wait_ge(S["gl_state"], 1)
            lo, t = (c % 2) * GC, c // 2
            for h in range(GH):
                v = AT["v_a"] + h * GDV
                last = pe.matmul(ps[:, DS_BANKS[c][h // 2], (h % 2) * GDV:(h % 2 + 1) * GDV],
                                 ksT[lo:lo + GC, t, h, :], proj[lo:lo + GC, t, v:v + GDV], start=True, stop=True)
            last.then_inc(S["gl_ds"], 1)

        def gla_output(t):
            pe.wait_ge(S["gl_state"], t + 2)
            for h in range(GH):
                v = AT["v_a"] + h * GDV
                bank = ((6, 7), (4, 5))[t][h // 2]
                cols = slice((h % 2) * GDV, (h % 2 + 1) * GDV)
                last = pe.matmul(ps[:, bank, cols], attT[:, t, h, :], proj[:, t, v:v + GDV], start=True,
                                 stop=False, skip_group_check=True)
                for c in (2 * t, 2 * t + 1):
                    if c > 0:
                        rows = slice((c % 2) * GC, (c % 2 + 1) * GC)
                        last = pe.matmul(ps[rows, bank, cols], flat(3, h)[:, c * GC:(c + 1) * GC],
                                         state[:, c - 1, h, :], start=False, stop=True, skip_group_check=True)
            last.then_inc(S["gl_o"], 1)

        for m in range(4 * LOOPED, T_OUT):
            c, q = divmod(m, 4)
            if q == 0:
                pe.wait_ge(S["evac_act"], c - 1)
                pe.wait_ge(S["evac_dve"], c - 1)
            project(Tile(m), c % 2, q)
            for step, f in (("transposes", head_transposes), ("scores", head_scores), ("probs", head_probs),
                            ("output", head_output)):
                h = head_at(step, m)
                if h is not None:
                    f(h)
            if m == GLA_TP:
                gla_transposes()
            if m == GLA_WITHIN:
                gla_within()
            for n in range(NCH - 1):
                if m == GLA_DS[n]:
                    gla_increment(n)
            for t in range(NT):
                if m == GLA_OUT[t]:
                    gla_output(t)

        def turn_y(half):
            pe.wait_ge(S["y_ready"], NT * (half + 1))
            for b in (2 * half, 2 * half + 1):
                for kk in range(2):
                    for t in range(NT):
                        k = 2 * b + kk
                        last = turn(ps[:, Y_BANKS[b], (kk * NT + t) * P:(kk * NT + t + 1) * P],
                                    proj[:, t, k * P:(k + 1) * P])
                last.then_inc(S["y_tp"], 1)

        turn_y(0)
        def out_half(tile, k, t):
            for half in range(2):
                cols = slice(half * CW, (half + 1) * CW)
                last = three(ps[:, OUTB[2 * t + half], :], ahi[:, k, t * P:(t + 1) * P], alo[:, k, t * P:(t + 1) * P],
                             whi[:, tile.slot, cols], wlo[:, tile.slot, cols], k == 0, k == KC - 1)
            return last

        for k in range(TILES_OUT - TAIL):
            if k == Y_LATE:
                turn_y(1)
            pe.wait_ge(S["act_split_lo"], NS + k // 2 + 1)
            tile = Tile(T_OUT + k)
            tile_ready(tile)
            out_half(tile, k, 0)
            out_half(tile, k, 1).then_inc(S["tiles_used"], 1)
        pe.wait_ge(S["act_split_lo"], NS + 4)
        for t in range(NT):
            for k in range(TILES_OUT - TAIL, TILES_OUT):
                tile = Tile(T_OUT + k)
                tile_ready(tile)
                last = out_half(tile, k, t)
                if t == 1:
                    last.then_inc(S["tiles_used"], 1)
            if t == 0:
                last.then_inc(S["half_done"], 1)

        for t in range(NT):
            for j in range(2):
                pe.wait_ge(S[("ln_done0", "ln_done")[t]], j + 1)
                for k in range(4):
                    last = turn(ps[:, 2 + 2 * t + j, k * P:(k + 1) * P], xt[:, t, (4 * j + k) * P:(4 * j + k + 1) * P])
                last.then_inc(S["x1_tp"], 1)
        pe.wait_ge(S["act_split_lo"], NS + 8)

        def by_tokens(tile, bank):
            tile_ready(tile)
            for k in range(KC):
                cols = slice(k * P, (k + 1) * P)
                o = ps[:, bank, 0:SEQ]
                wh, wl = whi[:, tile.slot, cols], wlo[:, tile.slot, cols]
                last = three(o, wh, wl, ahi[:, k, :], alo[:, k, :], k == 0, k == KC - 1)
            last.then_inc(S["tiles_used"], 1)

        def scores(k, i=None):
            if i is None:
                pe.wait_ge(S["q_copied"], k + 1)
                if k >= 2:
                    pe.wait_ge(S["sc_copied"], k - 1)
            else:
                pe.wait_ge(S["q_copied"], i * 4 + (k + 1))
                pe.wait_ge(S["sc_copied"], i * 4 + (k - 1))
            for t in range(NT):
                last = pe.matmul(ps[:, k % 2, t * P:(t + 1) * P], qs[:, k % 2, t * P:(t + 1) * P], keys[:, k % 2, :],
                                 start=True, stop=True)
            last.then_inc(S["sc_done"], 1)

        by_tokens(Tile(T_Q), HID[0])
        for k in range(4):
            by_tokens(Tile(T_Q + k + 1), HID[(k + 1) % 4])
            scores(k)
        with pe.Fori(1, TILES_Q // 4) as i:
            for k in range(4):
                by_tokens(Tile(T_Q + k + 1, i, 4), HID[(k + 1) % 4])
                scores(k, i)

        for k in range(1, 4):
            by_tokens(Tile(T_U + k), HID[k])
        with pe.Fori(1, TILES_U // 4 - 1) as i:
            for k in range(4):
                pe.wait_ge(S["hid_used"], i * 4 + (k - 3))
                by_tokens(Tile(T_U + k, i, 4), HID[k])

        for m in range(T_V - 4, T_V):
            if m == T_V - 1:
                pe.wait_ge(S["sel_done"], 1)
                for a in range(3):
                    for t in range(NT):
                        col = ((a % 2) * NT + t) * P
                        last = turn(ps[:, 6 + a // 2, col:col + P], sel[:, a, t * P:(t + 1) * P])
                last.then_inc(S["sel_tp"], 1)
            pe.wait_ge(S["hid_used"], m - T_U - 3)
            by_tokens(Tile(m), HID[m % 4])

        def gate_tables(n, b, i=None):
            if i is None:
                pe.wait_ge(S["hots_wide"], n + 1)
                pe.wait_ge(S["j_scaled"], n + 1)
            else:
                pe.wait_ge(S["hots_wide"], i * GB + (b + 1))
                pe.wait_ge(S["j_scaled"], i * GB + (b + 1))
                pe.wait_ge(S["g_used"], i * GB + (b + 1 - GB))
            for k in range(BLK):
                last = pe.matmul(ps[:, 2 * b + k // 4, (k % 4) * P:(k % 4 + 1) * P], hot_j[b % HOTS][:, k, :],
                                 hot_i[b % HOTS][:, k, :], start=True, stop=True)
            last.then_inc(S["g_done"], 1)

        pe.wait_ge(S["selT_done"], 1)
        pe.wait_ge(S["hid_used"], TILES_U)
        for n in range(GB):
            gate_tables(n, n)
        with pe.Fori(1, SEQ // BLK // GB) as i:
            for b in range(GB):
                gate_tables(None, b, i)

        def values(tile, t, start, stop):
            tok = slice(t * P, (t + 1) * P)
            for half in range(2):
                cols = slice(half * CW, (half + 1) * CW)
                o = ps[:, 2 * t + half, :]
                hh, hl = hhi[:, tile.slot, tok], hlo[:, tile.slot, tok]
                wh, wl = whi[:, tile.slot, cols], wlo[:, tile.slot, cols]
                pe.matmul(o, hh, wh, start=start, stop=False)
                pe.matmul(o, hh, wl, start=False, stop=False)
                last = pe.matmul(o, hl, wh, start=False, stop=stop)
            return last

        def values_ready(tile):
            pe.wait_ge(S["w_lo"], tile.number(1 - T_V))
            tile_ready(tile)

        pe.wait_ge(S["g_used"], SEQ // BLK - 3)
        for k in range(AHEAD):
            pe.wait_ge(S["first_lo"], k + 1)
            tile_ready(Tile(T_V + k))
            values(Tile(T_V + k), 0, k == 0, False)
        pe.wait_ge(S["g_used"], SEQ // BLK - 2)
        for k in range(AHEAD):
            values_ready(Tile(T_V + k))
            values(Tile(T_V + k), 1, k == 0, False).then_inc(S["tiles_used"], 1)
        values_ready(Tile(T_V + AHEAD))
        values(Tile(T_V + AHEAD), 0, False, False)
        values(Tile(T_V + AHEAD), 1, False, False).then_inc(S["tiles_used"], 1)
        with pe.Fori(1, TILES_V // 4 - 1) as i:
            for k in range(4):
                tile = Tile(T_V + k, i, 4)
                values_ready(tile)
                values(tile, 0, False, False)
                values(tile, 1, False, False).then_inc(S["tiles_used"], 1)
        for m in range(T_END - 4, T_END - TAIL):
            values_ready(Tile(m))
            values(Tile(m), 0, False, False)
            values(Tile(m), 1, False, False).then_inc(S["tiles_used"], 1)
        for t in range(NT):
            for m in range(T_END - TAIL, T_END):
                values_ready(Tile(m))
                last = values(Tile(m), t, False, m == T_END - 1)
                if t == 1:
                    last.then_inc(S["tiles_used"], 1)
            if t == 0:
                last.then_inc(S["half_done"], 1)

    block.__exit__(None, None, None)


def _columns(w_in):
    parts, o = {}, 0
    for name, width in WIDTH_IN:
        parts[name] = w_in[:, o:o + width]
        o += width
    return parts


def kernel(x, w_in, gla_w_decay, gla_b_decay, gla_norm_g, w_out, ln1_g, ln1_b,
           peer_w_q, peer_sub_keys, peer_u, peer_v, ln2_g, ln2_b):
    import concourse.bacc as _bacc
    from concourse.bass_utils import run_bass_kernel_spmd as _run

    c = np.ascontiguousarray
    a = {k: np.asarray(v) for k, v in dict(
        x=x, w_in=w_in, gla_w_decay=gla_w_decay, gla_b_decay=gla_b_decay, gla_norm_g=gla_norm_g, w_out=w_out,
        ln1_g=ln1_g, ln1_b=ln1_b, peer_w_q=peer_w_q, peer_sub_keys=peer_sub_keys, peer_u=peer_u,
        peer_v=peer_v, ln2_g=ln2_g, ln2_b=ln2_b).items()}
    parts = _columns(a["w_in"][0])
    w = np.concatenate([parts[n] for n, _ in ORDER], axis=1)
    inv_freq = np.power(np.float32(THETA), -np.arange(HALF, dtype=np.float32) * np.float32(2.0) / np.float32(2 * HALF))
    ang = np.arange(SEQ, dtype=np.float32)[:, None] * inv_freq[None, :]
    rot = [c(f(ang).astype(np.float32).reshape(NT, P, HALF).transpose(1, 0, 2)) for f in (np.cos, np.sin)]
    x2 = a["x"].reshape(SEQ, D)
    arrays = {
        "x": c(x2),
        "xT": c(x2.T.reshape(KC, P, SEQ).transpose(1, 0, 2)),
        "w_lr": c(parts["lr"].reshape(KC, P, GLR).transpose(1, 0, 2)),
        "w_tiles_in": c(w.reshape(4, 2, P, NCHUNK, CW).transpose(3, 0, 2, 1, 4).reshape(TILES_IN, P, W)),
        "w_tiles_out": c(a["w_out"][0].reshape(TILES_OUT, P, W)),
        "w_tiles_q": c(a["peer_w_q"][0].reshape(KC, P, TILES_Q, P).transpose(2, 1, 0, 3).reshape(TILES_Q, P, W)),
        "w_tiles_u": c(a["peer_u"][0].reshape(NK, NK, KC, P).transpose(0, 3, 2, 1).reshape(TILES_U, P, W)),
        "w_tiles_v": c(a["peer_v"][0].reshape(TILES_V, P, W)),
        "w_decay": c(a["gla_w_decay"][0]),
        "b_decay": c(a["gla_b_decay"][0].reshape(GH, GDK).T),
        "norm_g": c(a["gla_norm_g"]),
        "keysT": c(a["peer_sub_keys"][0].transpose(2, 0, 1)),
        "ln1_g": c(a["ln1_g"]), "ln1_b": c(a["ln1_b"]), "ln2_g": c(a["ln2_g"]), "ln2_b": c(a["ln2_b"]),
        "cos": rot[0], "sin": rot[1],
    }
    nc = _bacc.Bacc("TRN2", target_bir_lowering=False, num_devices=1)
    args = [nc.dram_tensor(n, v.shape, mybir.dt.from_np(v.dtype), kind="ExternalInput").ap()
            for n, v in arrays.items()]
    args.append(nc.dram_tensor("out", (SEQ, D), F32, kind="ExternalOutput").ap())
    layer(nc, *args)
    r = _run(nc, [arrays], core_ids=[0])
    return r.results[0]["out"].reshape(1, SEQ, D)
```
